# Optimizing a Trainium2 kernel written in Bass

```python
import math
import jax, jax.numpy as jnp
from jax import lax
import numpy as np
import jax
import jax.numpy as jnp

D_MODEL = 1024
BATCH = 1
SEQ = 512
DEPTH = 2

CHUNK = 64
HEAD_DIM = 64
N_HEADS_ATTN = 8
N_IDX_HEADS = 4
IDX_DIM = 64
TOPK_MAX = 256
Q_BLOCK = 64
N_HEADS_RET = 4
N_HEADS_MLSTM = 4
CONV_WIDTH = 4
ROPE_THETA = 10000.0
N_EXPERTS = 16
N_GROUPS = 4
EXPERTS_PER_GROUP = N_EXPERTS // N_GROUPS
TOP_K_EXPERTS = 2
D_FF_EXPERT = 256
LN_EPS = 1e-5

MIX_ATTN = N_HEADS_ATTN * HEAD_DIM
MIX_RET = N_HEADS_RET * HEAD_DIM
MIX_MLSTM = N_HEADS_MLSTM * HEAD_DIM
D_MIX = MIX_ATTN + MIX_RET + MIX_MLSTM

DEEPNORM_ALPHA = (2.0 * DEPTH) ** 0.25
DEEPNORM_BETA = (8.0 * DEPTH) ** -0.25

SPLIT_SIZES = (
    MIX_ATTN, MIX_ATTN, MIX_ATTN,
    N_IDX_HEADS * IDX_DIM, IDX_DIM, N_IDX_HEADS,
    MIX_RET, MIX_RET, MIX_RET, MIX_RET,
    MIX_MLSTM, MIX_MLSTM, MIX_MLSTM, MIX_MLSTM,
    N_HEADS_MLSTM, N_HEADS_MLSTM,
)
IN_PROJ_WIDTH = sum(SPLIT_SIZES)
SPLIT_OFFSETS = tuple(int(v) for v in np.cumsum((0,) + SPLIT_SIZES)[:-1])
SPLIT_POINTS = SPLIT_OFFSETS[1:]


def layer_norm(x, g, b):
    xf = x.astype(jnp.float32)
    mu = jnp.mean(xf, axis=-1, keepdims=True)
    var = jnp.mean(jnp.square(xf - mu), axis=-1, keepdims=True)
    return ((xf - mu) * lax.rsqrt(var + LN_EPS) * g + b).astype(x.dtype)

def head_norm(x):
    xf = x.astype(jnp.float32)
    mu = jnp.mean(xf, axis=-1, keepdims=True)
    var = jnp.mean(jnp.square(xf - mu), axis=-1, keepdims=True)
    return ((xf - mu) * lax.rsqrt(var + LN_EPS)).astype(x.dtype)

def rope_tables(positions):
    half = HEAD_DIM // 2
    inv_freq = ROPE_THETA ** (-jnp.arange(half, dtype=jnp.float32) / half)
    ang = positions.astype(jnp.float32)[..., None] * inv_freq
    return jnp.cos(ang)[:, :, None, :], jnp.sin(ang)[:, :, None, :]

def apply_rope(x, cos, sin):
    half = x.shape[-1] // 2
    x1 = x[..., :half].astype(jnp.float32)
    x2 = x[..., half:].astype(jnp.float32)
    return jnp.concatenate([x1 * cos - x2 * sin, x2 * cos + x1 * sin], axis=-1).astype(x.dtype)

def causal_conv(x, w, b):
    seq = x.shape[1]
    xp = jnp.pad(x, ((0, 0), (CONV_WIDTH - 1, 0), (0, 0)))
    out = b
    for j in range(CONV_WIDTH):
        out = out + xp[:, j:j + seq] * w[j]
    return out

def dsa_attention(q, k, v, iq, ik, iw):
    bsz, seq, n_heads, hd = q.shape
    topk = min(TOPK_MAX, seq // 4)
    n_blocks = seq // Q_BLOCK
    key_pos = jnp.arange(seq)
    iw = iw.astype(jnp.float32) * (N_IDX_HEADS ** -0.5) * (IDX_DIM ** -0.5)
    gather = jax.vmap(lambda arr, ids: arr[ids])

    def one_block(blk):
        start = blk * Q_BLOCK
        qb = lax.dynamic_slice_in_dim(q, start, Q_BLOCK, axis=1)
        iqb = lax.dynamic_slice_in_dim(iq, start, Q_BLOCK, axis=1)
        iwb = lax.dynamic_slice_in_dim(iw, start, Q_BLOCK, axis=1)
        q_pos = start + jnp.arange(Q_BLOCK)
        limit = (q_pos // CHUNK + 1) * CHUNK
        visible = key_pos[None, :] < limit[:, None]
        rel = jax.nn.relu(jnp.einsum('bqhd,bsd->bqhs', iqb, ik).astype(jnp.float32))
        score = jnp.einsum('bqhs,bqh->bqs', rel, iwb)
        score = jnp.where(visible[None], score, -jnp.inf)
        _, idx = lax.top_k(score, topk)
        valid = idx < limit[None, :, None]
        k_sel = gather(k, idx)
        v_sel = gather(v, idx)
        s = jnp.einsum('bqhd,bqkhd->bqhk', qb, k_sel).astype(jnp.float32) * (hd ** -0.5)
        s = jnp.where(valid[:, :, None, :], s, -jnp.inf)
        p = jax.nn.softmax(s, axis=-1).astype(v.dtype)
        return jnp.einsum('bqhk,bqkhd->bqhd', p, v_sel)

    out = lax.map(one_block, jnp.arange(n_blocks))
    return out.transpose(1, 0, 2, 3, 4).reshape(bsz, seq, n_heads, hd)

def retention_chunkwise(q, k, v):
    bsz, seq, nh, hd = q.shape
    dv = v.shape[-1]
    n_chunks = seq // CHUNK
    f32 = jnp.float32
    log_gamma = jnp.log1p(-(2.0 ** (-5.0 - jnp.arange(nh, dtype=f32))))

    def to_chunks(a):
        return a.astype(f32).reshape(bsz, n_chunks, CHUNK, nh, -1)

    qc = to_chunks(q)
    kc = to_chunks(k) * (hd ** -0.5)
    vc = to_chunks(v)
    pos = jnp.arange(CHUNK, dtype=f32)
    diff = pos[:, None] - pos[None, :]
    decay_in = jnp.where(diff >= 0, jnp.exp(diff[None] * log_gamma[:, None, None]), 0.0)
    scores = jnp.einsum('bnihd,bnjhd->bnhij', qc, kc) * decay_in
    inner = jnp.einsum('bnhij,bnjhe->bnihe', scores, vc)
    k_decay = jnp.exp((CHUNK - 1.0 - pos)[None, :] * log_gamma[:, None])
    chunk_kv = jnp.einsum('bnjhd,hj,bnjhe->nbhde', kc, k_decay, vc)
    chunk_decay = jnp.exp(CHUNK * log_gamma)[None, :, None, None]

    def step(state, kv):
        return state * chunk_decay + kv, state

    _, prev = lax.scan(step, jnp.zeros((bsz, nh, hd, dv), f32), chunk_kv)
    q_decay = jnp.exp((pos + 1.0)[None, :] * log_gamma[:, None])
    cross = jnp.einsum('bnihd,hi,nbhde->bnihe', qc, q_decay, prev)
    return (inner + cross).reshape(bsz, seq, nh, dv)

def mlstm_chunkwise(q, k, v, i_pre, f_pre):
    bsz, seq, nh, hd = q.shape
    n_chunks = seq // CHUNK
    f32 = jnp.float32

    def to_chunks(a):
        return a.astype(f32).reshape(bsz, n_chunks, CHUNK, nh, -1).transpose(1, 0, 3, 2, 4)

    qc = to_chunks(q)
    kc = to_chunks(k) * (hd ** -0.5)
    vc = to_chunks(v)
    ic = to_chunks(i_pre[..., None])[..., 0]
    lfc = to_chunks(jax.nn.log_sigmoid(f_pre.astype(f32))[..., None])[..., 0]
    causal = jnp.tril(jnp.ones((CHUNK, CHUNK), dtype=bool))

    def step(carry, xs):
        c_mem, n_mem, m_mem = carry
        q_, k_, v_, i_, lf_ = xs
        b = jnp.cumsum(lf_, axis=-1)
        log_w = jnp.where(causal, b[..., :, None] - b[..., None, :] + i_[..., None, :], -jnp.inf)
        log_inter = b + m_mem[..., None]
        m_q = jnp.maximum(log_inter, jnp.max(log_w, axis=-1))
        w = jnp.exp(log_w - m_q[..., None])
        inter = jnp.exp(log_inter - m_q)
        s = jnp.einsum('bhjd,bhld->bhjl', q_, k_) * w
        num = jnp.einsum('bhjl,bhle->bhje', s, v_) + inter[..., None] * jnp.einsum('bhjd,bhde->bhje', q_, c_mem)
        den = jnp.sum(s, axis=-1) + inter * jnp.einsum('bhjd,bhd->bhj', q_, n_mem)
        h = num / jnp.maximum(jnp.abs(den), jnp.exp(-m_q))[..., None]
        b_last = b[..., -1]
        log_k = b_last[..., None] - b + i_
        m_new = jnp.maximum(b_last + m_mem, jnp.max(log_k, axis=-1))
        kw = jnp.exp(log_k - m_new[..., None])
        decay = jnp.exp(b_last + m_mem - m_new)
        c_new = decay[..., None, None] * c_mem + jnp.einsum('bhl,bhld,bhle->bhde', kw, k_, v_)
        n_new = decay[..., None] * n_mem + jnp.einsum('bhl,bhld->bhd', kw, k_)
        return (c_new, n_new, m_new), h

    init = (jnp.zeros((bsz, nh, hd, hd), f32), jnp.zeros((bsz, nh, hd), f32), jnp.zeros((bsz, nh), f32))
    _, hs = lax.scan(step, init, (qc, kc, vc, ic, lfc))
    return hs.transpose(1, 0, 3, 2, 4).reshape(bsz, seq, nh, hd)

def token_mixers(h, w_in, w_out, i_bias, f_bias, conv_w, conv_b, cos, sin):
    bsz, seq, _ = h.shape
    (aq, ak, av, iq, ik, iw, rq, rk, rv, rg,
     mq, mk, mv, mo, mi, mf) = jnp.split(h @ w_in, SPLIT_POINTS, axis=-1)

    def heads(a, n):
        return a.reshape(bsz, seq, n, -1)

    o_a = dsa_attention(apply_rope(heads(aq, N_HEADS_ATTN), cos, sin),
                        apply_rope(heads(ak, N_HEADS_ATTN), cos, sin),
                        heads(av, N_HEADS_ATTN),
                        apply_rope(heads(iq, N_IDX_HEADS), cos, sin),
                        apply_rope(heads(ik, 1), cos, sin)[:, :, 0],
                        iw).reshape(bsz, seq, MIX_ATTN)
    y_r = retention_chunkwise(apply_rope(heads(rq, N_HEADS_RET), cos, sin),
                              apply_rope(heads(rk, N_HEADS_RET), cos, sin),
                              heads(rv, N_HEADS_RET))
    o_b = (head_norm(y_r).reshape(bsz, seq, MIX_RET) * jax.nn.silu(rg)).astype(h.dtype)
    qk = jax.nn.silu(causal_conv(jnp.concatenate([mq, mk], axis=-1), conv_w, conv_b))
    mq_c, mk_c = jnp.split(qk, 2, axis=-1)
    h_tilde = mlstm_chunkwise(heads(mq_c, N_HEADS_MLSTM), heads(mk_c, N_HEADS_MLSTM),
                              heads(mv, N_HEADS_MLSTM), mi + i_bias, mf + f_bias)
    h_t = jax.nn.sigmoid(heads(mo, N_HEADS_MLSTM).astype(jnp.float32)) * h_tilde
    o_c = head_norm(h_t).reshape(bsz, seq, MIX_MLSTM).astype(h.dtype)
    return jnp.concatenate([o_a, o_b, o_c], axis=-1) @ w_out

def moe_ffn(h, w_router, b_router, w_gate, w_up, w_down):
    n_tok = h.shape[0]
    scores = jax.nn.sigmoid((h @ w_router).astype(jnp.float32))
    biased = scores + b_router.astype(jnp.float32)
    grouped = biased.reshape(n_tok, N_GROUPS, EXPERTS_PER_GROUP)
    group_score = jnp.sum(lax.top_k(grouped, TOP_K_EXPERTS)[0], axis=-1)
    best_group = jnp.argmax(group_score, axis=-1)
    in_group = jnp.take_along_axis(grouped, best_group[:, None, None], axis=1)[:, 0]
    _, local = lax.top_k(in_group, TOP_K_EXPERTS)
    expert_idx = best_group[:, None] * EXPERTS_PER_GROUP + local
    wts = jnp.take_along_axis(scores, expert_idx, axis=1)
    wts = wts / jnp.sum(wts, axis=-1, keepdims=True)
    gate = jnp.einsum('tk,tke->te', wts, jax.nn.one_hot(expert_idx, N_EXPERTS, dtype=jnp.float32))
    hid = jax.nn.silu(jnp.einsum('td,edf->tef', h, w_gate)) * jnp.einsum('td,edf->tef', h, w_up)
    hid = hid * gate[:, :, None].astype(hid.dtype)
    return jnp.einsum('tef,efd->td', hid, w_down)

def first_inputs(seed: int = 0) -> dict:
    key = jax.random.key(seed)
    ks = jax.random.split(key, 20)
    f32 = jnp.float32

    def nrm(k, shape, scale):
        return jax.random.normal(k, shape, f32) * scale

    x = nrm(ks[0], (BATCH, SEQ, D_MODEL), 1.0)
    c = nrm(ks[1], (BATCH, D_MODEL), 1.0)
    offset = jax.random.randint(ks[2], (BATCH, 1), 0, 1024, dtype=jnp.int32)
    positions = offset + jnp.arange(SEQ, dtype=jnp.int32)[None, :]
    w_ada = nrm(ks[3], (DEPTH, D_MODEL, 6 * D_MODEL), 0.1 * D_MODEL ** -0.5)
    b_ada = nrm(ks[4], (DEPTH, 6 * D_MODEL), 0.02)
    col_scale = np.ones(IN_PROJ_WIDTH, np.float32)
    for part in (2, 8, 12):
        col_scale[SPLIT_OFFSETS[part]:SPLIT_OFFSETS[part] + SPLIT_SIZES[part]] = DEEPNORM_BETA
    w_in = nrm(ks[5], (DEPTH, D_MODEL, IN_PROJ_WIDTH), D_MODEL ** -0.5) * jnp.asarray(col_scale)
    i_bias = nrm(ks[6], (DEPTH, N_HEADS_MLSTM), 0.1)
    f_bias = jnp.linspace(3.0, 6.0, N_HEADS_MLSTM, dtype=f32)[None, :] + nrm(ks[7], (DEPTH, N_HEADS_MLSTM), 0.01)
    conv_w = nrm(ks[8], (DEPTH, CONV_WIDTH, 2 * MIX_MLSTM), CONV_WIDTH ** -0.5)
    conv_b = nrm(ks[9], (DEPTH, 2 * MIX_MLSTM), 0.01)
    w_out = nrm(ks[10], (DEPTH, D_MIX, D_MODEL), DEEPNORM_BETA * D_MIX ** -0.5)
    ln_mix_g = 1.0 + nrm(ks[11], (DEPTH, D_MODEL), 0.01)
    ln_mix_b = nrm(ks[12], (DEPTH, D_MODEL), 0.01)
    w_router = nrm(ks[13], (D_MODEL, N_EXPERTS), D_MODEL ** -0.5)
    b_router = nrm(ks[14], (N_EXPERTS,), 0.01)
    w_gate = nrm(ks[15], (DEPTH, N_EXPERTS, D_MODEL, D_FF_EXPERT), D_MODEL ** -0.5)
    w_up = nrm(ks[16], (DEPTH, N_EXPERTS, D_MODEL, D_FF_EXPERT), DEEPNORM_BETA * D_MODEL ** -0.5)
    w_down = nrm(ks[17], (DEPTH, N_EXPERTS, D_FF_EXPERT, D_MODEL), DEEPNORM_BETA * D_FF_EXPERT ** -0.5)
    ln_ffn_g = 1.0 + nrm(ks[18], (DEPTH, D_MODEL), 0.01)
    ln_ffn_b = nrm(ks[19], (DEPTH, D_MODEL), 0.01)
    return {'x': x, 'c': c, 'positions': positions, 'w_ada': w_ada, 'b_ada': b_ada,
            'w_in': w_in, 'i_bias': i_bias, 'f_bias': f_bias, 'conv_w': conv_w, 'conv_b': conv_b,
            'w_out': w_out, 'ln_mix_g': ln_mix_g, 'ln_mix_b': ln_mix_b,
            'w_router': w_router, 'b_router': b_router, 'w_gate': w_gate, 'w_up': w_up,
            'w_down': w_down, 'ln_ffn_g': ln_ffn_g, 'ln_ffn_b': ln_ffn_b}

def first_block(x, c, positions, w_ada, b_ada, w_in, i_bias, f_bias, conv_w, conv_b,
              w_out, ln_mix_g, ln_mix_b, w_router, b_router, w_gate, w_up, w_down,
              ln_ffn_g, ln_ffn_b):
    bsz, seq, d = x.shape
    cos, sin = rope_tables(positions)
    c_act = jax.nn.silu(c)
    for l in range(DEPTH):
        mod = (c_act @ w_ada[l] + b_ada[l])[:, None, :]
        sh_m, sc_m, g_m, sh_f, sc_f, g_f = jnp.split(mod, 6, axis=-1)
        h = x * (1.0 + sc_m) + sh_m
        mix = token_mixers(h, w_in[l], w_out[l], i_bias[l], f_bias[l], conv_w[l], conv_b[l], cos, sin)
        x = layer_norm(DEEPNORM_ALPHA * x + (1.0 + g_m) * mix, ln_mix_g[l], ln_mix_b[l])
        h = x * (1.0 + sc_f) + sh_f
        y = moe_ffn(h.reshape(bsz * seq, d), w_router, b_router, w_gate[l], w_up[l], w_down[l])
        x = layer_norm(DEEPNORM_ALPHA * x + (1.0 + g_f) * y.reshape(bsz, seq, d), ln_ffn_g[l], ln_ffn_b[l])
    return x


CTX_LEN = 256
GRID_W = 64
MIX_WIDTH = D_MODEL
A_WIDTH = MIX_WIDTH // 2
A_GROUPS = 4
A_GROUP_CH = A_WIDTH // A_GROUPS
A_CHUNK = 128
NA_HEADS = 8
NA_HEAD_DIM = (MIX_WIDTH - A_WIDTH) // NA_HEADS
NA_WIDTH = NA_HEADS * NA_HEAD_DIM
NA_WIN_ROWS = 8
NA_WIN_COLS = 16
O_NA_Q = 2 * A_WIDTH
O_NA_K = O_NA_Q + NA_WIDTH
O_NA_V = O_NA_K + NA_WIDTH
AB_IN_WIDTH = O_NA_V + NA_WIDTH
FN_WIDTH = MIX_WIDTH // 2
FN_GROUPS = 4
FN_GROUP_CH = FN_WIDTH // FN_GROUPS
GLA_HEADS = 4
GLA_VAL_WIDTH = MIX_WIDTH - FN_WIDTH
GLA_KEY_WIDTH = GLA_VAL_WIDTH // 2
GLA_DK = GLA_KEY_WIDTH // GLA_HEADS
GLA_DV = GLA_VAL_WIDTH // GLA_HEADS
GLA_LOW_RANK = 16
GLA_GATE_TEMP = 16.0
GLA_CHUNK = 64
O_Q = FN_WIDTH
O_K = O_Q + GLA_KEY_WIDTH
O_V = O_K + GLA_KEY_WIDTH
O_G = O_V + GLA_VAL_WIDTH
O_A = O_G + GLA_VAL_WIDTH
CD_IN_WIDTH = O_A + 2 * GLA_LOW_RANK
FFN_HIDDEN = -(-8 * D_MODEL // (3 * 256)) * 256
ROPE_BASE = 10000.0
RMS_EPS = 1e-6
NEG_INF = -1e30
N_EVEN = (DEPTH + 1) // 2
N_ODD = DEPTH // 2


def rmsnorm(x, w):
    xf = x.astype(jnp.float32)
    y = xf * lax.rsqrt(jnp.mean(xf * xf, axis=-1, keepdims=True) + RMS_EPS)
    return (y * w.astype(jnp.float32)).astype(x.dtype)

def modulate(h, shift, scale):
    return h * (1.0 + scale) + shift

def swiglu(h, w_gate, w_up, w_down):
    return (jax.nn.silu(h @ w_gate) * (h @ w_up)) @ w_down

def _rope_1d(xh, pos):
    half = xh.shape[-1] // 2
    inv_freq = ROPE_BASE ** (-jnp.arange(half, dtype=jnp.float32) / half)
    ang = pos.astype(jnp.float32)[:, None] * inv_freq[None, :]
    cos = jnp.cos(ang)[None, :, None, :].astype(xh.dtype)
    sin = jnp.sin(ang)[None, :, None, :].astype(xh.dtype)
    x1, x2 = xh[..., :half], xh[..., half:]
    return jnp.concatenate([x1 * cos - x2 * sin, x2 * cos + x1 * sin], axis=-1)

def axial_rope(x):
    t = jnp.arange(x.shape[1])
    d2 = x.shape[-1] // 2
    return jnp.concatenate([_rope_1d(x[..., :d2], t // GRID_W), _rope_1d(x[..., d2:], t % GRID_W)], axis=-1)

def chunk_token_mlp(uv, norm_w, sgu_w, sgu_b):
    B, T, _ = uv.shape
    uv = jax.nn.gelu(uv)
    u, v = uv[..., :A_WIDTH], uv[..., A_WIDTH:]
    v = rmsnorm(v, norm_w)
    vg = v.reshape(B, T // A_CHUNK, A_CHUNK, A_GROUPS, A_GROUP_CH)
    gate = jnp.einsum('gpq,bnqgc->bnpgc', sgu_w, vg) + sgu_b.T[None, None, :, :, None]
    return u * gate.reshape(B, T, A_WIDTH)

def _na_heads(t):
    return t.reshape(t.shape[0], t.shape[1], NA_HEADS, NA_HEAD_DIM)

def neighbourhood_attention(q, k, v, k_ctx, v_ctx, rel_bias):
    B, T, H, dh = q.shape
    rows = T // GRID_W
    wr = min(NA_WIN_ROWS, rows)
    scale = dh ** -0.5
    qg = q.reshape(B, rows, GRID_W, H, dh)
    kg = k.reshape(B, rows, GRID_W, H, dh)
    vg = v.reshape(B, rows, GRID_W, H, dh)
    col = jnp.arange(GRID_W)
    col_start = jnp.clip(col - NA_WIN_COLS // 2, 0, GRID_W - NA_WIN_COLS)
    col_mask = (col[None, :] >= col_start[:, None]) & (col[None, :] < col_start[:, None] + NA_WIN_COLS)
    col_idx = jnp.clip(col[None, :] - col[:, None] + NA_WIN_COLS - 1, 0, 2 * NA_WIN_COLS - 2)

    def row_block(r):
        row_start = jnp.clip(r - wr // 2, 0, rows - wr)
        qr = lax.dynamic_index_in_dim(qg, r, axis=1, keepdims=False)
        kb = lax.dynamic_slice_in_dim(kg, row_start, wr, axis=1)
        vb = lax.dynamic_slice_in_dim(vg, row_start, wr, axis=1)
        row_idx = row_start + jnp.arange(wr) - r + NA_WIN_ROWS - 1
        bias = jnp.transpose(rel_bias[:, row_idx][:, :, col_idx], (0, 2, 1, 3))
        s_nb = jnp.einsum('bqhd,bwkhd->bhqwk', qr, kb).astype(jnp.float32) * scale + bias[None].astype(jnp.float32)
        s_nb = jnp.where(col_mask[:, None, :], s_nb, NEG_INF).reshape(B, H, GRID_W, wr * GRID_W)
        s_cx = jnp.einsum('bqhd,bchd->bhqc', qr, k_ctx).astype(jnp.float32) * scale
        p = jax.nn.softmax(jnp.concatenate([s_nb, s_cx], axis=-1), axis=-1).astype(v.dtype)
        p_nb = p[..., :wr * GRID_W].reshape(B, H, GRID_W, wr, GRID_W)
        p_cx = p[..., wr * GRID_W:]
        return jnp.einsum('bhqwk,bwkhd->bqhd', p_nb, vb) + jnp.einsum('bhqc,bchd->bqhd', p_cx, v_ctx)

    out = lax.map(row_block, jnp.arange(rows))
    return jnp.moveaxis(out, 0, 1).reshape(B, T, H * dh)

def context_attention(q, k, v):
    B, T, H, dh = q.shape
    s = jnp.einsum('bqhd,bkhd->bhqk', q, k).astype(jnp.float32) * dh ** -0.5
    p = jax.nn.softmax(s, axis=-1).astype(v.dtype)
    return jnp.einsum('bhqk,bkhd->bqhd', p, v).reshape(B, T, H * dh)

def ab_mixer(h, hc, w_in, w_out, sgu_norm_w, sgu_w, sgu_b, rel_bias, with_ctx_out):
    p = h @ w_in
    a_out = chunk_token_mlp(p[..., :O_NA_Q], sgu_norm_w, sgu_w, sgu_b)
    q_l = _na_heads(p[..., O_NA_Q:O_NA_K])
    k_l = _na_heads(p[..., O_NA_K:O_NA_V])
    v_l = _na_heads(p[..., O_NA_V:])
    if with_ctx_out:
        pc = hc @ w_in
        kv_c = pc[..., O_NA_K:]
    else:
        pc = None
        kv_c = hc @ w_in[:, O_NA_K:]
    k_c = _na_heads(kv_c[..., :NA_WIDTH])
    v_c = _na_heads(kv_c[..., NA_WIDTH:])
    b_out = neighbourhood_attention(q_l, k_l, v_l, k_c, v_c, rel_bias)
    y = jnp.concatenate([a_out, b_out], axis=-1) @ w_out
    if not with_ctx_out:
        return y, None
    a_c = chunk_token_mlp(pc[..., :O_NA_Q], sgu_norm_w, sgu_w, sgu_b)
    b_c = context_attention(_na_heads(pc[..., O_NA_Q:O_NA_K]), k_c, v_c)
    y_c = jnp.concatenate([a_c, b_c], axis=-1) @ w_out
    return y, y_c

def fourier_mix(f):
    B, T, _ = f.shape
    fg = f.reshape(B, T, FN_GROUPS, FN_GROUP_CH).astype(jnp.float32)
    out = jnp.fft.fft2(fg, axes=(1, 3), norm='ortho').real
    return out.reshape(B, T, FN_WIDTH).astype(f.dtype)

def _to_heads(t, n_heads):
    B, T, _ = t.shape
    return jnp.transpose(t.reshape(B, T, n_heads, -1), (0, 2, 1, 3))

def log_decay(a_lr, w, b):
    return jax.nn.log_sigmoid((a_lr @ w + b).astype(jnp.float32)) / GLA_GATE_TEMP

def _gla_chunk_terms(k, v, log_a):
    B, H, T, dk = k.shape
    n = T // GLA_CHUNK
    kc = k.reshape(B, H, n, GLA_CHUNK, dk)
    vc = v.reshape(B, H, n, GLA_CHUNK, -1)
    b = jnp.cumsum(log_a.reshape(B, H, n, GLA_CHUNK, dk), axis=3)
    b_last = b[:, :, :, -1:, :]
    kv = jnp.einsum('bhnld,bhnle->bhnde', kc * jnp.exp(b_last - b), vc)
    return kc, vc, b, kv, jnp.exp(b_last[:, :, :, 0, :])

def _gla_scan(kv, decay, s0):
    def step(s, inp):
        d, kv_n = inp
        return d[..., None] * s + kv_n, s
    s_fin, s_prev = lax.scan(step, s0, (jnp.moveaxis(decay, 2, 0), jnp.moveaxis(kv, 2, 0)))
    return jnp.moveaxis(s_prev, 0, 2), s_fin

def gla_final_state(k, v, log_a, s0):
    _, _, _, kv, decay = _gla_chunk_terms(k, v, log_a)
    _, s_fin = _gla_scan(kv, decay, s0)
    return s_fin

def gla_chunked(q, k, v, log_a, s0):
    B, H, T, dk = q.shape
    kc, vc, b, kv, decay = _gla_chunk_terms(k, v, log_a)
    s_prev, s_fin = _gla_scan(kv, decay, s0)
    qe = q.reshape(B, H, -1, GLA_CHUNK, dk) * jnp.exp(b)
    lower = jnp.tril(jnp.ones((GLA_CHUNK, GLA_CHUNK), jnp.float32))
    att = jnp.einsum('bhnld,bhnmd->bhnlm', qe, kc * jnp.exp(-b)) * lower
    o = jnp.einsum('bhnlm,bhnme->bhnle', att, vc) + jnp.einsum('bhnld,bhnde->bhnle', qe, s_prev)
    return o.reshape(B, H, T, -1), s_fin

def gla_output(o, g, head_norm_w):
    B, H, T, dv = o.shape
    o = rmsnorm(jnp.transpose(o, (0, 2, 1, 3)), head_norm_w)
    return (o * jax.nn.silu(g.reshape(B, T, H, dv).astype(jnp.float32))).reshape(B, T, H * dv).astype(g.dtype)

def _split_cd(p):
    return p[..., :O_Q], p[..., O_Q:O_K], p[..., O_K:O_V], p[..., O_V:O_G], p[..., O_G:O_A], p[..., O_A:]

def cd_mixer(h, hc, w_in, w_out, dec_w_f, dec_b_f, dec_w_b, dec_b_b, head_norm_w, with_ctx_out):
    B, T, _ = h.shape
    f32 = jnp.float32
    flip = lambda t: jnp.flip(t, axis=2)
    f_l, q_l, k_l, v_l, g_l, a_l = _split_cd(h @ w_in)
    q_l = axial_rope(q_l.reshape(B, T, GLA_HEADS, GLA_DK)) * GLA_DK ** -0.5
    k_l = axial_rope(k_l.reshape(B, T, GLA_HEADS, GLA_DK))
    ql = jnp.transpose(q_l, (0, 2, 1, 3)).astype(f32)
    kl = jnp.transpose(k_l, (0, 2, 1, 3)).astype(f32)
    vl = _to_heads(v_l, GLA_HEADS).astype(f32)
    la_lf = _to_heads(log_decay(a_l[..., :GLA_LOW_RANK], dec_w_f, dec_b_f), GLA_HEADS)
    la_lb = _to_heads(log_decay(a_l[..., GLA_LOW_RANK:], dec_w_b, dec_b_b), GLA_HEADS)
    if with_ctx_out:
        f_c, q_c, k_c, v_c, g_c, a_c = _split_cd(hc @ w_in)
    else:
        pc = hc @ jnp.concatenate([w_in[:, O_K:O_G], w_in[:, O_A:]], axis=1)
        k_c = pc[..., :GLA_KEY_WIDTH]
        v_c = pc[..., GLA_KEY_WIDTH:GLA_KEY_WIDTH + GLA_VAL_WIDTH]
        a_c = pc[..., GLA_KEY_WIDTH + GLA_VAL_WIDTH:]
    kc = _to_heads(k_c, GLA_HEADS).astype(f32)
    vc = _to_heads(v_c, GLA_HEADS).astype(f32)
    la_cf = _to_heads(log_decay(a_c[..., :GLA_LOW_RANK], dec_w_f, dec_b_f), GLA_HEADS)
    la_cb = _to_heads(log_decay(a_c[..., GLA_LOW_RANK:], dec_w_b, dec_b_b), GLA_HEADS)
    s0 = jnp.zeros((hc.shape[0], GLA_HEADS, GLA_DK, GLA_DV), f32)
    if with_ctx_out:
        qc = (_to_heads(q_c, GLA_HEADS) * GLA_DK ** -0.5).astype(f32)
        o_cf, s_f = gla_chunked(qc, kc, vc, la_cf, s0)
        o_cb, s_b = gla_chunked(flip(qc), flip(kc), flip(vc), flip(la_cb), s0)
        o_c = o_cf + flip(o_cb)
    else:
        s_f = gla_final_state(kc, vc, la_cf, s0)
        s_b = gla_final_state(flip(kc), flip(vc), flip(la_cb), s0)
    o_lf, _ = gla_chunked(ql, kl, vl, la_lf, s_f)
    o_lb, _ = gla_chunked(flip(ql), flip(kl), flip(vl), flip(la_lb), s_b)
    o_l = o_lf + flip(o_lb)
    y = jnp.concatenate([fourier_mix(f_l), gla_output(o_l, g_l, head_norm_w)], axis=-1) @ w_out
    if not with_ctx_out:
        return y, None
    y_c = jnp.concatenate([fourier_mix(f_c), gla_output(o_c, g_c, head_norm_w)], axis=-1) @ w_out
    return y, y_c

def second_inputs(seed: int = 0) -> dict:
    key = jax.random.key(seed)
    ks = jax.random.split(key, 26)
    D = D_MODEL

    def nrm(k, shape, s):
        return jax.random.normal(k, shape, jnp.float32) * s

    return {
        'x': nrm(ks[0], (BATCH, SEQ, D), 1.0),
        'c': nrm(ks[1], (BATCH, D), 1.0),
        'ctx': nrm(ks[2], (BATCH, CTX_LEN, D), 1.0),
        'c_ctx': nrm(ks[3], (D,), 1.0),
        'ada_w': nrm(ks[4], (DEPTH, D, 6 * D), 0.5 * D ** -0.5),
        'ada_b': nrm(ks[5], (DEPTH, 6 * D), 0.02),
        'norm_mix_w': 1.0 + nrm(ks[6], (DEPTH, D), 0.05),
        'norm_ffn_w': 1.0 + nrm(ks[7], (DEPTH, D), 0.05),
        'ffn_w_gate': nrm(ks[8], (DEPTH, D, FFN_HIDDEN), D ** -0.5),
        'ffn_w_up': nrm(ks[9], (DEPTH, D, FFN_HIDDEN), D ** -0.5),
        'ffn_w_down': nrm(ks[10], (DEPTH, FFN_HIDDEN, D), FFN_HIDDEN ** -0.5),
        'ab_w_in': nrm(ks[11], (N_EVEN, D, AB_IN_WIDTH), D ** -0.5),
        'ab_w_out': nrm(ks[12], (N_EVEN, MIX_WIDTH, D), MIX_WIDTH ** -0.5),
        'ab_sgu_norm_w': 1.0 + nrm(ks[13], (N_EVEN, A_WIDTH), 0.05),
        'ab_sgu_w': nrm(ks[14], (N_EVEN, A_GROUPS, A_CHUNK, A_CHUNK), A_CHUNK ** -0.5),
        'ab_sgu_b': 1.0 + nrm(ks[15], (N_EVEN, A_GROUPS, A_CHUNK), 0.05),
        'ab_rel_bias': nrm(ks[16], (N_EVEN, NA_HEADS, 2 * NA_WIN_ROWS - 1, 2 * NA_WIN_COLS - 1), 0.5),
        'cd_w_in': nrm(ks[17], (N_ODD, D, CD_IN_WIDTH), D ** -0.5),
        'cd_w_out': nrm(ks[18], (N_ODD, MIX_WIDTH, D), MIX_WIDTH ** -0.5),
        'cd_decay_w_fwd': nrm(ks[19], (N_ODD, GLA_LOW_RANK, GLA_KEY_WIDTH), GLA_LOW_RANK ** -0.5),
        'cd_decay_b_fwd': nrm(ks[20], (N_ODD, GLA_KEY_WIDTH), 0.1),
        'cd_decay_w_bwd': nrm(ks[21], (N_ODD, GLA_LOW_RANK, GLA_KEY_WIDTH), GLA_LOW_RANK ** -0.5),
        'cd_decay_b_bwd': nrm(ks[22], (N_ODD, GLA_KEY_WIDTH), 0.1),
        'cd_head_norm_w': 1.0 + nrm(ks[23], (N_ODD, GLA_DV), 0.05),
        'final_norm_w': 1.0 + nrm(ks[24], (D,), 0.05),
    }

def second_block(x, c, ctx, c_ctx, ada_w, ada_b, norm_mix_w, norm_ffn_w, ffn_w_gate, ffn_w_up, ffn_w_down,
              ab_w_in, ab_w_out, ab_sgu_norm_w, ab_sgu_w, ab_sgu_b, ab_rel_bias,
              cd_w_in, cd_w_out, cd_decay_w_fwd, cd_decay_b_fwd, cd_decay_w_bwd, cd_decay_b_bwd, cd_head_norm_w,
              final_norm_w):
    silu_c = jax.nn.silu(c)
    silu_cc = jax.nn.silu(c_ctx)
    for i in range(DEPTH):
        last = i == DEPTH - 1
        j = i // 2
        mod = (silu_c @ ada_w[i] + ada_b[i])[:, None, :]
        mod_c = (silu_cc @ ada_w[i] + ada_b[i])[None, None, :]
        sh_m, sc_m, g_m, sh_f, sc_f, g_f = jnp.split(mod, 6, axis=-1)
        shc_m, scc_m, gc_m, shc_f, scc_f, gc_f = jnp.split(mod_c, 6, axis=-1)
        h = modulate(rmsnorm(x, norm_mix_w[i]), sh_m, sc_m)
        hc = modulate(rmsnorm(ctx, norm_mix_w[i]), shc_m, scc_m)
        if i % 2 == 0:
            y, y_c = ab_mixer(h, hc, ab_w_in[j], ab_w_out[j], ab_sgu_norm_w[j], ab_sgu_w[j], ab_sgu_b[j],
                              ab_rel_bias[j], not last)
        else:
            y, y_c = cd_mixer(h, hc, cd_w_in[j], cd_w_out[j], cd_decay_w_fwd[j], cd_decay_b_fwd[j],
                              cd_decay_w_bwd[j], cd_decay_b_bwd[j], cd_head_norm_w[j], not last)
        x = x + g_m * y
        x = x + g_f * swiglu(modulate(rmsnorm(x, norm_ffn_w[i]), sh_f, sc_f), ffn_w_gate[i], ffn_w_up[i], ffn_w_down[i])
        if not last:
            ctx = ctx + gc_m * y_c
            ctx = ctx + gc_f * swiglu(modulate(rmsnorm(ctx, norm_ffn_w[i]), shc_f, scc_f),
                                      ffn_w_gate[i], ffn_w_up[i], ffn_w_down[i])
    return rmsnorm(x, final_norm_w)


def setup_inputs(seed=0):
    out = dict(first_inputs(seed))
    for name, value in second_inputs(seed + 1).items():
        if name != "x":
            out[name + "_2"] = value
    return out


def reference(
    x, c, positions, w_ada, b_ada, w_in, i_bias, f_bias, conv_w, conv_b, w_out, ln_mix_g,
    ln_mix_b, w_router, b_router, w_gate, w_up, w_down, ln_ffn_g, ln_ffn_b, c_2, ctx_2, c_ctx_2,
    ada_w_2, ada_b_2, norm_mix_w_2, norm_ffn_w_2, ffn_w_gate_2, ffn_w_up_2, ffn_w_down_2,
    ab_w_in_2, ab_w_out_2, ab_sgu_norm_w_2, ab_sgu_w_2, ab_sgu_b_2, ab_rel_bias_2, cd_w_in_2,
    cd_w_out_2, cd_decay_w_fwd_2, cd_decay_b_fwd_2, cd_decay_w_bwd_2, cd_decay_b_bwd_2,
    cd_head_norm_w_2, final_norm_w_2,
):
    x = first_block(
        x, c, positions, w_ada, b_ada, w_in, i_bias, f_bias, conv_w, conv_b, w_out, ln_mix_g,
        ln_mix_b, w_router, b_router, w_gate, w_up, w_down, ln_ffn_g, ln_ffn_b,
    )
    return second_block(
        x, c_2, ctx_2, c_ctx_2, ada_w_2, ada_b_2, norm_mix_w_2, norm_ffn_w_2, ffn_w_gate_2,
        ffn_w_up_2, ffn_w_down_2, ab_w_in_2, ab_w_out_2, ab_sgu_norm_w_2, ab_sgu_w_2,
        ab_sgu_b_2, ab_rel_bias_2, cd_w_in_2, cd_w_out_2, cd_decay_w_fwd_2, cd_decay_b_fwd_2,
        cd_decay_w_bwd_2, cd_decay_b_bwd_2, cd_head_norm_w_2, final_norm_w_2,
    )


_drawn_inputs = setup_inputs


def setup_inputs(seed=0):
    import zlib

    import numpy as np

    out = dict(_drawn_inputs(seed))
    spreads = {}
    factors = {'i_bias': 64.0,
     'conv_b': 5.723,
     'ln_mix_g': 3.057,
     'ln_ffn_g': 3.157,
     'ln_ffn_b': 3.092,
     'norm_mix_w_2': 2.736,
     'norm_ffn_w_2': 2.711,
     'ab_sgu_norm_w_2': 7.111,
     'ab_sgu_b_2': 7.255,
     'ab_rel_bias_2': 7.294,
     'cd_decay_w_fwd_2': 3.802,
     'cd_decay_b_fwd_2': 8.0,
     'cd_decay_w_bwd_2': 3.22,
     'cd_decay_b_bwd_2': 8.0,
     'cd_head_norm_w_2': 8.0}
    for name, (base, spread) in spreads.items():
        noise = np.random.default_rng([zlib.crc32(name.encode()), seed]).standard_normal(out[name].shape)
        drawn = base * np.exp(spread * noise) if base else spread * noise
        out[name] = jnp.asarray(drawn.astype(out[name].dtype))
    for name, factor in factors.items():
        out[name] = (out[name] * factor).astype(out[name].dtype)
    return out
```

```python
import math
from contextlib import ExitStack

import numpy as np
import concourse.bass as bass
from concourse import mybir

F32 = mybir.dt.float32
I32 = mybir.dt.int32
ALU = mybir.AluOpType
ACT = mybir.ActivationFunctionType
AX = mybir.AxisListType

P = 128
D = 1024
KD = D // P
T = 512
TT = T // P
TC = 256
TA = T + TC
DEPTH = 2
HD = 64
HALF = HD // 2
NH_A, NH_I, NH_R, NH_M = 8, 4, 4, 4
TOPK = 128
CONV = 4
NE, NG, EPG, FE = 16, 4, 4, 256
EPS = 1e-5
RMS_EPS = 1e-6
ALPHA = (2.0 * DEPTH) ** 0.25
NEG = -1.0e30
MAGIC = 12582912.0
TWO_PI = (6.28125, 0.0019350051879882812, 3.019915981956753e-07)
PI_IN = 3.1415925

C_AQ, C_AK, C_IQ, C_IK, C_RQ, C_RK, C_RG, C_MQ, C_MK, C_MO, C_G = 0, 4, 8, 10, 11, 13, 15, 17, 19, 21, 23
N_ROPE = 15
N_CH = 24
N_V = 1024
V_A, V_R, V_M = 0, 512, 768

K_ID, K_ROT, K_HEAD, K_ONE, K_MEAN, K_UP = (P * i for i in range(6))
K_DEC = 6 * P
K_SELH = K_DEC + NH_R * T
K_SELP = K_SELH + NH_M * P
K_RANK = K_SELP + NH_M // 2 * P
K_FREQ = K_RANK + NE + NG
K_N = K_FREQ + 1

J_ROT, J_MASK, J_COS, J_SIN, J_RST = 0, P, 3 * P, 3 * P + T, 3 * P + 2 * T
J_DFT = J_RST + TA
J_N = J_DFT + 2 * P
FFN = 2816


class Buffers:
    pass


class Item:

    def __init__(self, q, segs, vs, o):
        self.q, self.segs, self.vs, self.o = q, segs, vs, o


class Steps:

    def __init__(self, eng, sem):
        self.eng, self.sem, self.n = eng, sem, 0

    def __call__(self, ins):
        ins.then_inc(self.sem, 1)
        self.n += 1
        self.eng.wait_ge(self.sem, self.n)


def take(M, names):
    M.blocks += 1
    return {n: M.nc.alloc_semaphore(f"b{M.blocks}_{n}") for n in names.split()}


def give(nc, s):
    nc.clear_and_free_semaphores(list(s.values()))
    nc.all_engine_barrier()


def setup(nc, M, A):
    s = take(M, "loaded stream step table pre c_in c_sig")
    with ExitStack() as ctx:
        pi = ctx.enter_context(M.nc.sbuf_tensor(f"{M.blocks}_pos_int", [P, T], I32))
        ang = ctx.enter_context(M.nc.sbuf_tensor(f"{M.blocks}_angle", [P, T], F32))
        turns = ctx.enter_context(M.nc.sbuf_tensor(f"{M.blocks}_turns", [P, T], F32))
        r = ctx.enter_context(M.nc.sbuf_tensor(f"{M.blocks}_reduced", [P, 2, T], F32))
        sg = ctx.enter_context(M.nc.sbuf_tensor(f"{M.blocks}_cond_sig", [P, 3, KD], F32))
        block = ctx.enter_context(nc.Block())

        @block.sync
        def _(sp):
            sp.dma_start(M.K[:], A["consts"]).then_inc(s["loaded"], 16)
            sp.dma_start(pi[:], A["positions"].partition_broadcast(P)).then_inc(s["loaded"], 16)
            sp.dma_start(M.cond[:], A["cond"]).then_inc(s["c_in"], 16)
            sp.dma_start(M.xT[:, :, 0:T], A["x"]).then_inc(s["stream"], 16)
            sp.dma_start(M.xT[:, :, T:TA], A["ctx"]).then_inc(s["stream"], 16)
            sp.wait_ge(s["stream"], 32)

        @block.vector
        def _(dve):
            step = Steps(dve, s["step"])
            dve.wait_ge(s["loaded"], 32)
            step(nc.vector.tensor_copy(r[:, 0, :], pi[:]))
            step(nc.vector.tensor_scalar(ang[:], r[:, 0, :], M.K[:, K_FREQ:K_FREQ + 1], None, ALU.mult))
            for j, quarter in enumerate((0.25, 0.0)):
                step(nc.vector.tensor_scalar(turns[:], ang[:], float(1 / (2 * math.pi)), quarter, ALU.mult, ALU.add))
                step(nc.vector.tensor_scalar(turns[:], turns[:], MAGIC, None, ALU.add))
                step(nc.vector.tensor_scalar(turns[:], turns[:], -MAGIC, None, ALU.add))
                src = ang[:]
                for c in TWO_PI:
                    step(nc.vector.scalar_tensor_tensor(out=r[:, j, :], in0=turns[:], scalar=-c, in1=src,
                                                        op0=ALU.mult, op1=ALU.add))
                    src = r[:, j, :]
                if quarter:
                    step(nc.vector.tensor_scalar(r[:, j, :], r[:, j, :], math.pi / 2, None, ALU.add))
                step(nc.vector.tensor_scalar(r[:, j, :], r[:, j, :], -PI_IN, PI_IN, ALU.max, ALU.min))
            nc.vector.tensor_scalar(r[:, 0, :], r[:, 0, :], 1.0, None, ALU.mult).then_inc(s["table"], 1)
            dve.wait_ge(s["c_sig"], 1)
            nc.vector.tensor_tensor(M.cond[:], M.cond[:], sg[:], ALU.mult).then_inc(s["pre"], 1)
            dve.wait_ge(s["pre"], 1)

        @block.scalar
        def _(act):
            act.wait_ge(s["c_in"], 16)
            nc.scalar.activation(sg[:], M.cond[:], ACT.Sigmoid).then_inc(s["c_sig"], 1)
            act.wait_ge(s["table"], 1)
            nc.scalar.activation(M.cos[:], r[:, 0, :], ACT.Sin)
            nc.scalar.activation(M.sin[:], r[:, 1, :], ACT.Sin)
    give(nc, s)


def ada(nc, M, w, b, col, ncol, plus_one):
    s = take(M, "w0 w1 used b_in mod_done step")
    ready = (s["w0"], s["w1"])
    NB = 4
    with ExitStack() as ctx:
        W = ctx.enter_context(M.nc.sbuf_tensor(f"{M.blocks}_ada_w", [P, 2, KD, NB * P], F32))
        B = ctx.enter_context(M.nc.sbuf_tensor(f"{M.blocks}_ada_b", [P, 48], F32))
        block = ctx.enter_context(nc.Block())
        N = 48 // NB

        @block.sync
        def _(sp):
            sp.dma_start(B[:], b).then_inc(s["b_in"], 16)
            for u in range(2):
                sp.dma_start(W[:, u], w(u)).then_inc(ready[u], 16)
            with sp.Fori(1, N // 2) as i:
                for u in range(2):
                    sp.wait_ge(s["used"], 2 * i + u - 1)
                    sp.dma_start(W[:, u], w(2 * i + u)).then_inc(ready[u], 16)

        @block.tensor
        def _(pe):
            with pe.Fori(0, N // 2) as i:
                for u in range(2):
                    pe.wait_ge(ready[u], 16 * i + 16)
                    for n in range(NB):
                        for k in range(KD):
                            mm = nc.tensor.matmul(
                                M.PS[:, 0, bass.ds((2 * i + u) * NB * ncol + n * ncol, ncol)],
                                W[:, u, k, n * P:(n + 1) * P], M.condT[:, k, col:col + ncol],
                                start=(k == 0), stop=(k == KD - 1))
                    mm.then_inc(s["used"], 1)

        @block.vector
        def _(dve):
            dve.wait_ge(s["b_in"], 16)
            dve.wait_ge(s["used"], N)
            out = M.mod[:, 0:48 * ncol].rearrange("p (n c) -> p n c", c=ncol)
            src = M.PS[:, 0, 0:48 * ncol].rearrange("p (n c) -> p n c", c=ncol)
            step = Steps(dve, s["step"])
            for c in range(ncol):
                step(nc.vector.tensor_tensor(out[:, :, c], src[:, :, c], B[:], ALU.add))
            for part in plus_one:
                a, z = part * KD * ncol, (part + 1) * KD * ncol
                nc.vector.tensor_scalar(M.mod[:, a:z], M.mod[:, a:z], 1.0, None, ALU.add).then_inc(s["mod_done"], 1)
    give(nc, s)


def modcol(M, part, k, ncol=1, c=0):
    j = (part * KD + k) * ncol + c
    return M.mod[:, j:j + 1]


def proj1(nc, M, A, l, B):
    s = take(M, "h_done w0 w1 used psum_free raw_done rot_done t1 t2 turned wv wi tok_done tok_free iw_in")
    ready = (s["w0"], s["w1"])
    with ExitStack() as ctx:
        W = ctx.enter_context(M.nc.sbuf_tensor(f"{M.blocks}_proj_w", [P, 2, KD, P], F32))
        WV = ctx.enter_context(M.nc.sbuf_tensor(f"{M.blocks}_proj_wv", [P, 2, KD, 512], F32))
        WI = ctx.enter_context(M.nc.sbuf_tensor(f"{M.blocks}_proj_wi", [P, KD, NH_I], F32))
        t1 = ctx.enter_context(M.nc.sbuf_tensor(f"{M.blocks}_rope_cos", [P, 2, T], F32))
        t2 = ctx.enter_context(M.nc.sbuf_tensor(f"{M.blocks}_rope_sin", [P, 2, T], F32))
        block = ctx.enter_context(nc.Block())
        PAIRS = N_ROPE // 2

        @block.sync
        def _(sp):
            for u in range(2):
                sp.dma_start(W[:, u], A["w_in_t"][l, u]).then_inc(ready[u], 16)
            for g in range(2):
                sp.dma_start(WV[:, g], A["w_in_v"][l, g]).then_inc(s["wv"], 16)
            sp.dma_start(WI[:], A["w_in_i"][l]).then_inc(s["wi"], 16)
            with sp.Fori(1, N_CH // 2) as i:
                for u in range(2):
                    sp.wait_ge(s["used"], 2 * i + u - 1)
                    sp.dma_start(W[:, u], A["w_in_t"][l, 2 * i + u]).then_inc(ready[u], 16)

        @block.tensor
        def _(pe):
            def chunk(n, u, i):
                pe.wait_ge(ready[u], 16 * i + 16)
                pe.wait_ge(s["psum_free"], n + 1)
                for k in range(KD):
                    mm = nc.tensor.matmul(M.PS[:, u, :], W[:, u, k, :], M.hT[:, k, 0:T],
                                          start=(k == 0), stop=(k == KD - 1))
                mm.then_inc(s["used"], 1)

            def rotate(n, u):
                pe.wait_ge(s["raw_done"], n + 1)
                pe.wait_ge(s["turned"], n + 1)
                nc.tensor.matmul(M.PS[:, 2 + u, :], M.K[:, K_ROT:K_ROT + P], B.PT[:, n, :] if isinstance(n, int)
                                 else B.PT[:, bass.ds(n, 1), :], start=True, stop=True).then_inc(s["rot_done"], 1)

            pe.wait_ge(s["h_done"], KD)
            with pe.Fori(0, PAIRS) as i:
                for u in range(2):
                    chunk(2 * i + u, u, i)
                for u in range(2):
                    rotate(2 * i + u, u)
            chunk(2 * PAIRS, 0, PAIRS)
            rotate(2 * PAIRS, 0)
            chunk(2 * PAIRS + 1, 1, PAIRS)
            with pe.Fori(PAIRS + 1, N_CH // 2) as i:
                for u in range(2):
                    chunk(2 * i + u, u, i)
            pe.wait_ge(s["wv"], 32)
            for n in range(2 * TT):
                g, t = n // TT, n % TT
                if n >= 2:
                    pe.wait_ge(s["tok_free"], n - 1)
                for k in range(KD):
                    mm = nc.tensor.matmul(M.PS[:, 4 + n % 2, :], M.hT[:, k, t * P:(t + 1) * P], WV[:, g, k, :],
                                          start=(k == 0), stop=(k == KD - 1))
                mm.then_inc(s["tok_done"], 1)
            pe.wait_ge(s["wi"], 16)
            for t in range(TT):
                for k in range(KD):
                    mm = nc.tensor.matmul(M.PS[:, 6, t * NH_I:(t + 1) * NH_I], M.hT[:, k, t * P:(t + 1) * P],
                                          WI[:, k, :], start=(k == 0), stop=(k == KD - 1))
            mm.then_inc(s["tok_done"], 1)

        @block.scalar
        def _(act):
            act.sem_inc(s["psum_free"], 2)
            for k in range(KD):
                nc.scalar.activation(M.hT[:, k, 0:T], M.xT[:, k, 0:T], ACT.Identity,
                                     bias=modcol(M, 0, k), scale=modcol(M, 1, k)).then_inc(s["h_done"], 1)

            def copy(n, u, done):
                act.wait_ge(s["used"], n + 1)
                out = B.PT[:, n, :] if isinstance(n, int) else B.PT[:, bass.ds(n, 1), :]
                nc.scalar.activation(out, M.PS[:, u, :], ACT.Copy).then_inc(done, 1)
                act.wait_ge(done, n + 1)
                act.sem_inc(s["psum_free"], 1)

            with act.Fori(0, N_CH // 2) as i:
                for u in range(2):
                    copy(2 * i + u, u, s["raw_done"])
            for n in range(2 * TT):
                g, t = n // TT, n % TT
                act.wait_ge(s["tok_done"], n + 1)
                nc.scalar.activation(B.V[:, t, g * 512:(g + 1) * 512], M.PS[:, 4 + n % 2, :],
                                     ACT.Copy).then_inc(s["tok_free"], 1)
            act.wait_ge(s["tok_done"], 2 * TT + 1)
            nc.scalar.activation(B.iw[:], M.PS[:, 6, 0:TT * NH_I], ACT.Copy, scale=NH_I ** -0.5 * HD ** -0.5)

        @block.vector
        def _(dve):
            dve.sem_inc(s["turned"], 2)

            def turn(n, u):
                x = B.PT[:, n, :] if isinstance(n, int) else B.PT[:, bass.ds(n, 1), :]
                c = M.cos[:] if isinstance(n, int) else M.cos[:].rearrange("p (a t) -> p a t", a=1)
                a = t1[:, u] if isinstance(n, int) else t1[:, u:u + 1]
                b = t2[:, u] if isinstance(n, int) else t2[:, u:u + 1]
                dve.wait_ge(s["rot_done"], n + 1)
                nc.vector.tensor_tensor(a, x, c, ALU.mult).then_inc(s["t1"], 1)
                nc.vector.tensor_tensor(t2[:, u], M.PS[:, 2 + u, :], M.sin[:], ALU.mult).then_inc(s["t2"], 1)
                dve.wait_ge(s["t1"], n + 1)
                dve.wait_ge(s["t2"], n + 1)
                nc.vector.tensor_tensor(x, a, b, ALU.add).then_inc(s["turned"], 1)

            with dve.Fori(0, PAIRS) as i:
                for u in range(2):
                    turn(2 * i + u, u)
            turn(2 * PAIRS, 0)
    give(nc, s)


def convolve(nc, M, A, l, B):
    s = take(M, "par step conv gates sig act_step ab_done tr cp")
    rows = NH_M
    with ExitStack() as ctx:
        cw = ctx.enter_context(M.nc.sbuf_tensor(f"{M.blocks}_conv_w", [P, 4, CONV + 1], F32))
        gb = ctx.enter_context(M.nc.sbuf_tensor(f"{M.blocks}_gate_b", [rows, 2], F32))
        acc = ctx.enter_context(M.nc.sbuf_tensor(f"{M.blocks}_conv_acc", [P, 4, T], F32))
        z = ctx.enter_context(M.nc.sbuf_tensor(f"{M.blocks}_f_pre", [rows, T], F32))
        e = ctx.enter_context(M.nc.sbuf_tensor(f"{M.blocks}_f_exp", [rows, T], F32))
        lf = ctx.enter_context(M.nc.sbuf_tensor(f"{M.blocks}_log_f", [rows, T], F32))
        one = ctx.enter_context(M.nc.sbuf_tensor(f"{M.blocks}_one_row", [rows, T], F32))
        bs = ctx.enter_context(M.nc.sbuf_tensor(f"{M.blocks}_f_sum", [rows, T], F32))
        a = ctx.enter_context(M.nc.sbuf_tensor(f"{M.blocks}_i_rel", [rows, T], F32))
        am = ctx.enter_context(M.nc.sbuf_tensor(f"{M.blocks}_i_max", [rows, T], F32))
        th = ctx.enter_context(M.nc.sbuf_tensor(f"{M.blocks}_floor", [rows, T], F32))
        block = ctx.enter_context(nc.Block())

        @block.sync
        def _(sp):
            sp.dma_start(cw[:], A["conv"][l]).then_inc(s["par"], 16)
            sp.dma_start(gb[:], A["gate_b"][l]).then_inc(s["par"], 16)

        @block.vector
        def _(dve):
            step = Steps(dve, s["step"])
            dve.wait_ge(s["par"], 32)
            step(nc.vector.tensor_scalar(z[:], B.PT[32:32 + rows, C_G, :], gb[:, 1:2], None, ALU.add))
            nc.vector.scalar_tensor_tensor(out=lf[:], in0=z[:], scalar=-1.0, in1=z[:], op0=ALU.mult,
                                           op1=ALU.max).then_inc(s["gates"], 1)
            step(nc.vector.memset(one[:], 1.0))
            for c in range(4):
                x = B.PT[:, C_MQ + c, :]
                step(nc.vector.tensor_scalar(acc[:, c, :], x, cw[:, c, CONV - 1:CONV], cw[:, c, CONV:CONV + 1],
                                             ALU.mult, ALU.add))
                for back in range(1, CONV):
                    ins = nc.vector.scalar_tensor_tensor(
                        out=acc[:, c, back:T], in0=x[:, 0:T - back], scalar=cw[:, c, CONV - 1 - back:CONV - back],
                        in1=acc[:, c, back:T], op0=ALU.mult, op1=ALU.add)
                    if back < CONV - 1:
                        step(ins)
                    else:
                        ins.then_inc(s["conv"], 1)
            dve.wait_ge(s["sig"], 1)
            step(nc.vector.scalar_tensor_tensor(out=lf[:], in0=z[:], scalar=0.0, in1=e[:], op0=ALU.min,
                                                op1=ALU.subtract))
            step(nc.vector.tensor_tensor_scan(out=bs[:], data0=one[:], data1=lf[:], initial=0.0,
                                              op0=ALU.mult, op1=ALU.add))
            step(nc.vector.scalar_tensor_tensor(out=a[:], in0=B.PT[0:rows, C_G, :], scalar=gb[:, 0:1], in1=bs[:],
                                                op0=ALU.add, op1=ALU.subtract))
            step(nc.vector.tensor_tensor_scan(out=am[:], data0=a[:], data1=a[:], initial=0.0,
                                              op0=ALU.max, op1=ALU.max))
            step(nc.vector.tensor_tensor(th[:], bs[:], am[:], ALU.add))
            nc.vector.tensor_scalar(th[:], th[:], -1.0, 80.0, ALU.mult, ALU.min).then_inc(s["ab_done"], 1)

        @block.scalar
        def _(act):
            act.wait_ge(s["gates"], 1)
            nc.scalar.activation(e[:], lf[:], ACT.Exp, scale=-1.0).then_inc(s["act_step"], 1)
            act.wait_ge(s["act_step"], 1)
            nc.scalar.activation(e[:], e[:], ACT.Ln, bias=1.0).then_inc(s["sig"], 1)
            for c in range(2):
                nc.scalar.activation(B.PT[:, C_MO + c, :], B.PT[:, C_MO + c, :], ACT.Sigmoid)
            for c in range(2):
                nc.scalar.activation(B.PT[:, C_RG + c, :], B.PT[:, C_RG + c, :], ACT.Silu)
            for c in range(4):
                act.wait_ge(s["conv"], c + 1)
                nc.scalar.activation(B.PT[:, C_MQ + c, :], acc[:, c, :], ACT.Silu)
            act.wait_ge(s["ab_done"], 1)
            nc.scalar.activation(th[:], th[:], ACT.Exp).then_inc(s["act_step"], 1)
            for h in range(NH_M):
                act.wait_ge(s["tr"], h + 1)
                nc.scalar.activation(B.Amax[:, h, :], M.PS[:, h, :], ACT.Copy).then_inc(s["cp"], 1)
            for p in range(NH_M // 2):
                act.wait_ge(s["tr"], NH_M + p + 1)
                nc.scalar.activation(B.floor[:, p, :], M.PS[:, NH_M + p, :], ACT.Copy).then_inc(s["cp"], 1)
            act.wait_ge(s["tr"], NH_M + NH_M // 2 + 1)
            nc.scalar.activation(B.acol[:], M.PS[:, 6, 0:TT * NH_M], ACT.Copy).then_inc(s["cp"], 1)

        @block.tensor
        def _(pe):
            pe.wait_ge(s["ab_done"], 1)
            for h in range(NH_M):
                nc.tensor.matmul(M.PS[:, h, :], M.K[0:rows, K_SELH + h * P:K_SELH + (h + 1) * P], am[:],
                                 start=True, stop=True).then_inc(s["tr"], 1)
            pe.wait_ge(s["act_step"], 2)
            for p in range(NH_M // 2):
                nc.tensor.matmul(M.PS[:, NH_M + p, :], M.K[0:rows, K_SELP + p * P:K_SELP + (p + 1) * P], th[:],
                                 start=True, stop=True).then_inc(s["tr"], 1)
            for t in range(TT):
                mm = nc.tensor.transpose(M.PS[:, 6, t * NH_M:(t + 1) * NH_M], a[:, t * P:(t + 1) * P],
                                         M.K[0:rows, K_ID:K_ID + rows])
            mm.then_inc(s["tr"], 1)
    give(nc, s)


def select_keys(nc, M, B):
    s = take(M, "scored used step")
    N = TT * NH_I
    with ExitStack() as ctx:
        sc = ctx.enter_context(M.nc.sbuf_tensor(f"{M.blocks}_score", [P, T], F32))
        tmp = ctx.enter_context(M.nc.sbuf_tensor(f"{M.blocks}_score_h", [P, T], F32))
        work = ctx.enter_context(M.nc.sbuf_tensor(f"{M.blocks}_score_left", [P, T], F32))
        best = ctx.enter_context(M.nc.sbuf_tensor(f"{M.blocks}_best8", [P, 8], F32))
        block = ctx.enter_context(nc.Block())

        @block.tensor
        def _(pe):
            for n in range(N):
                t, h = n // NH_I, n % NH_I
                w, b = P * (t + 1), HD * (h % 2)
                if n >= 4:
                    pe.wait_ge(s["used"], n - 3)
                nc.tensor.matmul(M.PS[:, n % 4, 0:w], B.PT[b:b + HD, C_IQ + h // 2, t * P:(t + 1) * P],
                                 B.PT[b:b + HD, C_IK, 0:w], start=True, stop=True).then_inc(s["scored"], 1)

        @block.vector
        def _(dve):
            step = Steps(dve, s["step"])
            for t in range(TT):
                w = P * (t + 1)
                for h in range(NH_I):
                    n = t * NH_I + h
                    dve.wait_ge(s["scored"], n + 1)
                    out = tmp if h else sc
                    nc.vector.tensor_scalar(out[:, 0:w], M.PS[:, n % 4, 0:w], 0.0, B.iw[:, n:n + 1],
                                            ALU.max, ALU.mult).then_inc(s["used"], 1)
                    if h:
                        dve.wait_ge(s["used"], n + 1)
                        step(nc.vector.tensor_tensor(sc[:, 0:w], sc[:, 0:w], tmp[:, 0:w], ALU.add))
                if t == 0:
                    step(nc.vector.memset(B.bias[:, 0, 0:w], 0.0))
                    step(nc.vector.memset(B.bias[0:64, 0, 64:w], NEG))
                    continue
                step(nc.vector.memset(sc[0:64, w - 64:w], -3.0e38))
                src = sc
                for r in range(TOPK // 8):
                    step(nc.vector.max(best[:], src[:, 0:w]))
                    step(nc.vector.match_replace(work[:, 0:w], best[:], src[:, 0:w], -1.0e38))
                    src = work
                step(nc.vector.tensor_tensor(tmp[:, 0:w], work[:, 0:w], sc[:, 0:w], ALU.is_equal))
                step(nc.vector.tensor_scalar(B.bias[:, t, 0:w], tmp[:, 0:w], NEG, None, ALU.mult))
    give(nc, s)


def attend(nc, M, items, scale):
    s = take(M, "s_done sm_done nm_done exp_done p_done t_done pt_done pv_done o_done step")
    N = len(items)
    WM = max(sum(w for _, w, _ in it.segs) for it in items)
    with ExitStack() as ctx:
        sm = ctx.enter_context(M.nc.sbuf_tensor(f"{M.blocks}_att_s", [P, 2, WM], F32))
        pr = ctx.enter_context(M.nc.sbuf_tensor(f"{M.blocks}_att_p", [P, 2, WM], F32))
        pt = ctx.enter_context(M.nc.sbuf_tensor(f"{M.blocks}_att_pT", [P, 2, WM], F32))
        mx = ctx.enter_context(M.nc.sbuf_tensor(f"{M.blocks}_att_max", [P, N], F32))
        nm = ctx.enter_context(M.nc.sbuf_tensor(f"{M.blocks}_att_nmax", [P, N], F32))
        su = ctx.enter_context(M.nc.sbuf_tensor(f"{M.blocks}_att_sum", [P, N], F32))
        ri = ctx.enter_context(M.nc.sbuf_tensor(f"{M.blocks}_att_rsum", [P, N], F32))
        block = ctx.enter_context(nc.Block())

        def width(n):
            return sum(w for _, w, _ in items[n].segs)

        @block.tensor
        def _(pe):
            def scores(n):
                if n >= 2:
                    pe.wait_ge(s["sm_done"], n - 1)
                for j, (k, w, _) in enumerate(items[n].segs):
                    mm = nc.tensor.matmul(M.PS[:, 2 * (n % 2) + j, 0:w], items[n].q, k, start=True, stop=True)
                mm.then_inc(s["s_done"], 1)

            def turn(n):
                pe.wait_ge(s["p_done"], n + 1)
                if n >= 1:
                    pe.wait_ge(s["pt_done"], n)
                for b in range(width(n) // P):
                    mm = nc.tensor.transpose(M.PS[:, 4 + b // 4, (b % 4) * P:(b % 4 + 1) * P],
                                             pr[:, n % 2, b * P:(b + 1) * P], M.K[:, K_ID:K_ID + P])
                mm.then_inc(s["t_done"], 1)

            def values(n):
                pe.wait_ge(s["pt_done"], n + 1)
                m, c = n // 2, HD * (n % 2)
                if m >= 2:
                    pe.wait_ge(s["o_done"], m - 1)
                B_ = width(n) // P
                for b in range(B_):
                    mm = nc.tensor.matmul(M.PS[c:c + HD, 6 + m % 2, 0:P], items[n].vs[b],
                                          pt[:, n % 2, b * P:(b + 1) * P], start=(b == 0), stop=(b == B_ - 1))
                mm.then_inc(s["pv_done"], 1)

            for n in range(N + 2):
                if n < N:
                    scores(n)
                if 1 <= n <= N:
                    turn(n - 1)
                if n >= 2:
                    values(n - 2)

        @block.vector
        def _(dve):
            step = Steps(dve, s["step"])

            def front(n):
                dve.wait_ge(s["s_done"], n + 1)
                if n >= 2:
                    dve.wait_ge(s["exp_done"], n - 1)
                at = 0
                for j, (_, w, bias) in enumerate(items[n].segs):
                    src, out = M.PS[:, 2 * (n % 2) + j, 0:w], sm[:, n % 2, at:at + w]
                    if bias is None:
                        ins = nc.vector.tensor_scalar(out, src, scale, None, ALU.mult)
                    else:
                        ins = nc.vector.scalar_tensor_tensor(out=out, in0=src, scalar=scale, in1=bias,
                                                             op0=ALU.mult, op1=ALU.add)
                    at += w
                    if j < len(items[n].segs) - 1:
                        step(ins)
                ins.then_inc(s["sm_done"], 1)
                dve.wait_ge(s["sm_done"], n + 1)
                step(nc.vector.tensor_reduce(mx[:, n:n + 1], sm[:, n % 2, 0:at], AX.X, ALU.max))
                nc.vector.tensor_scalar(nm[:, n:n + 1], mx[:, n:n + 1], -1.0, None, ALU.mult).then_inc(s["nm_done"], 1)

            def back(n):
                dve.wait_ge(s["exp_done"], n + 1)
                step(nc.vector.reciprocal(ri[:, n:n + 1], su[:, n:n + 1]))
                w = width(n)
                nc.vector.tensor_scalar(pr[:, n % 2, 0:w], pr[:, n % 2, 0:w], ri[:, n:n + 1], None,
                                        ALU.mult).then_inc(s["p_done"], 1)

            for n in range(N + 1):
                if n < N:
                    front(n)
                if n >= 1:
                    back(n - 1)

        @block.scalar
        def _(act):
            def exps(n):
                act.wait_ge(s["nm_done"], n + 1)
                if n >= 2:
                    act.wait_ge(s["t_done"], n - 1)
                w = width(n)
                nc.scalar.activation(pr[:, n % 2, 0:w], sm[:, n % 2, 0:w], ACT.Exp, bias=nm[:, n:n + 1],
                                     accum_out=su[:, n:n + 1]).then_inc(s["exp_done"], 1)

            def copy_turned(n):
                act.wait_ge(s["t_done"], n + 1)
                if n >= 2:
                    act.wait_ge(s["pv_done"], n - 1)
                w = width(n)
                ins = nc.scalar.activation(pt[:, n % 2, 0:min(w, 512)], M.PS[:, 4, 0:min(w, 512)], ACT.Copy)
                if w > 512:
                    ins = nc.scalar.activation(pt[:, n % 2, 512:w], M.PS[:, 5, 0:w - 512], ACT.Copy)
                ins.then_inc(s["pt_done"], 1)

            def copy_out(m):
                act.wait_ge(s["pv_done"], 2 * m + 2)
                nc.scalar.activation(items[2 * m].o, M.PS[:, 6 + m % 2, 0:P], ACT.Copy).then_inc(s["o_done"], 1)

            for n in range(N + 2):
                if n < N:
                    exps(n)
                if 1 <= n <= N:
                    copy_turned(n - 1)
                if n >= 2 and n % 2 == 1:
                    copy_out((n - 3) // 2)
    give(nc, s)


def attend1(nc, M, B):
    items = []
    for t in range(TT):
        w = P * (t + 1)
        for h in range(NH_A):
            b, c = HD * (h % 2), h // 2
            items.append(Item(
                q=B.PT[b:b + HD, C_AQ + c, t * P:(t + 1) * P],
                segs=[(B.PT[b:b + HD, C_AK + c, 0:w], w, B.bias[:, t, 0:w])],
                vs=[B.V[:, j, V_A + h * HD:V_A + (h + 1) * HD] for j in range(t + 1)],
                o=B.mixT[:, c, t * P:(t + 1) * P]))
    attend(nc, M, items, HD ** -0.5)


def linear_mixers(nc, M, B):
    s = take(M, "s_done p_done pv_done e_in e_done y_done step e_step")
    N = 2 * NH_R * TT
    G = N // 8
    with ExitStack() as ctx:
        pb = ctx.enter_context(M.nc.sbuf_tensor(f"{M.blocks}_lin_p", [P, 2, T], F32))
        eb = ctx.enter_context(M.nc.sbuf_tensor(f"{M.blocks}_lin_e", [P, 2, T], F32))
        den = ctx.enter_context(M.nc.sbuf_tensor(f"{M.blocks}_lin_den", [P, T], F32))
        block = ctx.enter_context(nc.Block())

        def item(n):
            kind, h, t = n // (NH_R * TT), n // TT % NH_R, n % TT
            return kind, h, t, T - P * t

        @block.tensor
        def _(pe):
            def scores(n):
                kind, h, t, w = item(n)
                b = HD * (h % 2)
                q, k = (C_MQ, C_MK) if kind else (C_RQ, C_RK)
                if n >= 2:
                    pe.wait_ge(s["p_done"], n - 1)
                nc.tensor.matmul(M.PS[:, n % 2, 0:w], B.PT[b:b + HD, k + h // 2, t * P:(t + 1) * P],
                                 B.PT[b:b + HD, q + h // 2, t * P:T], start=True, stop=True).then_inc(s["s_done"], 1)

            def values(n):
                kind, h, t, w = item(n)
                b, g = HD * (h % 2), n // 8
                pe.wait_ge(s["p_done"], n + 1)
                if n % 8 == 0 and g >= 2:
                    pe.wait_ge(s["y_done"], g - 1)
                v0 = (V_M if kind else V_R) + h * HD
                mm = nc.tensor.matmul(M.PS[b:b + HD, 2 + g % 2, T - w:T], B.V[:, t, v0:v0 + HD], pb[:, n % 2, 0:w],
                                      start=(t == 0), stop=(t == TT - 1))
                if kind:
                    mm = nc.tensor.matmul(M.PS[b:b + HD, 4 + g % 2, T - w:T], M.K[:, K_ONE:K_ONE + HD],
                                          pb[:, n % 2, 0:w], start=(t == 0), stop=(t == TT - 1))
                mm.then_inc(s["pv_done"], 1)

            for n in range(N + 1):
                if n < N:
                    scores(n)
                if n >= 1:
                    values(n - 1)

        @block.vector
        def _(dve):
            step = Steps(dve, s["step"])

            def weigh(n):
                kind, h, t, w = item(n)
                if n >= 2:
                    dve.wait_ge(s["pv_done"], n - 1)
                if kind:
                    m = n - NH_R * TT
                    dve.wait_ge(s["e_done"], m + 1)
                    dve.wait_ge(s["s_done"], n + 1)
                    step(nc.vector.scalar_tensor_tensor(out=pb[:, n % 2, 0:w], in0=M.PS[:, n % 2, 0:w],
                                                        scalar=HD ** -0.5, in1=eb[:, m % 2, 0:w],
                                                        op0=ALU.mult, op1=ALU.mult))
                    nc.vector.tensor_tensor(pb[:, n % 2, 0:P], pb[:, n % 2, 0:P], M.K[:, K_UP:K_UP + P],
                                            ALU.mult).then_inc(s["p_done"], 1)
                else:
                    dve.wait_ge(s["s_done"], n + 1)
                    nc.vector.scalar_tensor_tensor(out=pb[:, n % 2, 0:w], in0=M.PS[:, n % 2, 0:w],
                                                   scalar=HD ** -0.5, in1=M.K[:, K_DEC + h * T:K_DEC + h * T + w],
                                                   op0=ALU.mult, op1=ALU.mult).then_inc(s["p_done"], 1)

            def exponent(m):
                h, t = m // TT, m % TT
                w = T - P * t
                if m >= 2:
                    dve.wait_ge(s["p_done"], NH_R * TT + m - 1)
                nc.vector.tensor_scalar(eb[:, m % 2, 0:w], B.Amax[:, h, T - w:T],
                                        B.acol[:, t * NH_M + h:t * NH_M + h + 1], 0.0,
                                        ALU.subtract, ALU.max).then_inc(s["e_in"], 1)

            def take_pair(g):
                dve.wait_ge(s["pv_done"], 8 * g + 8)
                if g < 2:
                    nc.vector.tensor_copy(B.Y[:, g, :], M.PS[:, 2 + g % 2, :]).then_inc(s["y_done"], 1)
                    return
                step(nc.vector.tensor_scalar(den[:], M.PS[:, 4 + g % 2, :], -1.0, None, ALU.mult))
                step(nc.vector.tensor_tensor(den[:], M.PS[:, 4 + g % 2, :], den[:], ALU.max))
                step(nc.vector.tensor_tensor(den[:], den[:], B.floor[:, g - 2, :], ALU.max))
                step(nc.vector.reciprocal(den[:], den[:]))
                step(nc.vector.tensor_tensor(den[:], den[:], B.PT[:, C_MO + g - 2, :], ALU.mult))
                nc.vector.tensor_tensor(B.Y[:, g, :], M.PS[:, 2 + g % 2, :], den[:], ALU.mult).then_inc(s["y_done"], 1)

            half = NH_R * TT
            for n in range(N + 1):
                if half - 1 <= n < N - 1:
                    exponent(n + 1 - half)
                if n < N:
                    weigh(n)
                if n >= 1 and n % 8 == 0:
                    take_pair(n // 8 - 1)

        @block.scalar
        def _(act):
            for m in range(NH_M * TT):
                w = T - P * (m % TT)
                act.wait_ge(s["e_in"], m + 1)
                nc.scalar.activation(eb[:, m % 2, 0:w], eb[:, m % 2, 0:w], ACT.Exp, scale=-1.0).then_inc(s["e_done"], 1)
    give(nc, s)


def head_norm(nc, M, B):
    s = take(M, "mean cen sq var sd norm rstd done")
    with ExitStack() as ctx:
        cen = ctx.enter_context(M.nc.sbuf_tensor(f"{M.blocks}_hn_cen", [P, 4, T], F32))
        sq = ctx.enter_context(M.nc.sbuf_tensor(f"{M.blocks}_hn_sq", [P, 4, T], F32))
        block = ctx.enter_context(nc.Block())
        heads = M.K[:, K_HEAD:K_HEAD + P]

        @block.tensor
        def _(pe):
            for c in range(4):
                nc.tensor.matmul(M.PS[:, c, :], heads, B.Y[:, c, :], start=True, stop=True).then_inc(s["mean"], 1)
            for c in range(4):
                pe.wait_ge(s["sq"], c + 1)
                nc.tensor.matmul(M.PS[:, 4 + c, :], heads, sq[:, c, :], start=True, stop=True).then_inc(s["var"], 1)

        @block.vector
        def _(dve):
            for c in range(4):
                dve.wait_ge(s["mean"], c + 1)
                nc.vector.tensor_tensor(cen[:, c, :], B.Y[:, c, :], M.PS[:, c, :], ALU.subtract).then_inc(s["cen"], 1)
            for c in range(4):
                dve.wait_ge(s["sd"], c + 1)
                nc.vector.reciprocal(sq[:, c, :], sq[:, c, :]).then_inc(s["rstd"], 1)
                dve.wait_ge(s["rstd"], c + 1)
                out = B.mixT[:, 4 + c, :] if c >= 2 else cen[:, c, :]
                nc.vector.tensor_tensor(out, cen[:, c, :], sq[:, c, :], ALU.mult).then_inc(s["norm"], 1)
                if c < 2:
                    dve.wait_ge(s["norm"], c + 1)
                    nc.vector.tensor_tensor(B.mixT[:, 4 + c, :], cen[:, c, :], B.PT[:, C_RG + c, :],
                                            ALU.mult).then_inc(s["done"], 1)

        @block.scalar
        def _(act):
            for c in range(4):
                act.wait_ge(s["cen"], c + 1)
                nc.scalar.activation(sq[:, c, :], cen[:, c, :], ACT.Square).then_inc(s["sq"], 1)
            for c in range(4):
                act.wait_ge(s["var"], c + 1)
                nc.scalar.activation(sq[:, c, :], M.PS[:, 4 + c, :], ACT.Sqrt, bias=M.eps[:, 0:1]).then_inc(s["sd"], 1)
    give(nc, s)


def gemm_residual(nc, M, w, src, J, KP, spans, gate, alpha):
    s = take(M, "used psum_free scaled " + " ".join(f"w{j}" for j in range(2 * J)))
    ready = [s[f"w{j}"] for j in range(2 * J)]
    ncol = spans[0][3]
    NS = len(spans)
    TW = sum(n for _, n, _, _ in spans)
    with ExitStack() as ctx:
        W = ctx.enter_context(M.nc.sbuf_tensor(f"{M.blocks}_out_w", [P, 2 * J, KP, P], F32))
        tmp = ctx.enter_context(M.nc.sbuf_tensor(f"{M.blocks}_out_t", [P, 2, TW], F32))
        block = ctx.enter_context(nc.Block())

        @block.sync
        def _(sp):
            for j in range(2 * J):
                sp.dma_start(W[:, j], w(j)).then_inc(ready[j], 16)
            with sp.Fori(1, KD // 2) as i:
                for j in range(2 * J):
                    sp.wait_ge(s["used"], 2 * J * i + j - 2 * J + 1)
                    sp.dma_start(W[:, j], w(2 * J * i + j)).then_inc(ready[j], 16)

        @block.tensor
        def _(pe):
            with pe.Fori(0, KD // 2) as i:
                for u in range(2):
                    pe.wait_ge(s["psum_free"], 2 * NS * i + NS * (u + 1))
                    for j in range(J):
                        pe.wait_ge(ready[u * J + j], 16 * i + 16)
                        for k in range(KP):
                            for a, (t0, nt, _, _) in enumerate(spans):
                                mm = nc.tensor.matmul(M.PS[:, 4 * u + a, 0:nt], W[:, u * J + j, k, :],
                                                      src[:, j * KP + k, t0:t0 + nt],
                                                      start=(j + k == 0), stop=(j == J - 1 and k == KP - 1))
                        mm.then_inc(s["used"], 1)

        @block.vector
        def _(dve):
            dve.sem_inc(s["psum_free"], 2 * NS)
            with dve.Fori(0, KD // 2) as i:
                for u in range(2):
                    dve.wait_ge(s["used"], 2 * J * i + (u + 1) * J)
                    at = 0
                    for a, (t0, nt, c, _) in enumerate(spans):
                        g = M.mod[:, bass.ds((gate * KD + 2 * i + u) * ncol + c, 1)]
                        nc.vector.tensor_scalar(tmp[:, u, at:at + nt], M.PS[:, 4 * u + a, 0:nt], g, None,
                                                ALU.mult).then_inc(s["psum_free"], 1)
                        at += nt
                    at = 0
                    for a, (t0, nt, c, _) in enumerate(spans):
                        dve.wait_ge(s["psum_free"], 2 * NS + 2 * NS * i + NS * u + a + 1)
                        x = M.xT[:, bass.ds(2 * i + u, 1), t0:t0 + nt]
                        nc.vector.scalar_tensor_tensor(out=x, in0=x, scalar=float(alpha),
                                                       in1=tmp[:, u:u + 1, at:at + nt],
                                                       op0=ALU.mult, op1=ALU.add).then_inc(s["scaled"], 1)
                        at += nt
    give(nc, s)


def layer_norm(nc, M, gb):
    s = take(M, "par mean cen sq var sd rstd norm done")
    with ExitStack() as ctx:
        GB = ctx.enter_context(M.nc.sbuf_tensor(f"{M.blocks}_ln_gb", [P, 2, KD], F32))
        sq = ctx.enter_context(M.nc.sbuf_tensor(f"{M.blocks}_ln_sq", [P, 4, T], F32))
        rs = ctx.enter_context(M.nc.sbuf_tensor(f"{M.blocks}_ln_rs", [P, T], F32))
        block = ctx.enter_context(nc.Block())
        mean = M.K[:, K_MEAN:K_MEAN + P]

        @block.sync
        def _(sp):
            sp.dma_start(GB[:], gb).then_inc(s["par"], 16)

        @block.tensor
        def _(pe):
            for k in range(KD):
                mm = nc.tensor.matmul(M.PS[:, 0, :], mean, M.xT[:, k, 0:T], start=(k == 0), stop=(k == KD - 1))
            mm.then_inc(s["mean"], 1)
            for k in range(KD):
                pe.wait_ge(s["sq"], k + 1)
                nc.tensor.matmul(M.PS[:, 1, :], mean, sq[:, k % 4, :], start=(k == 0),
                                 stop=(k == KD - 1)).then_inc(s["var"], 1)

        @block.vector
        def _(dve):
            dve.wait_ge(s["mean"], 1)
            for k in range(KD):
                nc.vector.tensor_tensor(M.xT[:, k, 0:T], M.xT[:, k, 0:T], M.PS[:, 0, :],
                                        ALU.subtract).then_inc(s["cen"], 1)
            dve.wait_ge(s["sd"], 1)
            nc.vector.reciprocal(rs[:], rs[:]).then_inc(s["rstd"], 1)
            dve.wait_ge(s["rstd"], 1)
            for k in range(KD):
                nc.vector.tensor_tensor(M.xT[:, k, 0:T], M.xT[:, k, 0:T], rs[:], ALU.mult).then_inc(s["norm"], 1)

        @block.scalar
        def _(act):
            for k in range(KD):
                act.wait_ge(s["cen"], k + 1)
                if k >= 4:
                    act.wait_ge(s["var"], k - 3)
                nc.scalar.activation(sq[:, k % 4, :], M.xT[:, k, 0:T], ACT.Square).then_inc(s["sq"], 1)
            act.wait_ge(s["var"], KD)
            nc.scalar.activation(rs[:], M.PS[:, 1, :], ACT.Sqrt, bias=M.eps[:, 0:1]).then_inc(s["sd"], 1)
            act.wait_ge(s["par"], 16)
            for k in range(KD):
                act.wait_ge(s["norm"], k + 1)
                nc.scalar.activation(M.xT[:, k, 0:T], M.xT[:, k, 0:T], ACT.Identity, bias=GB[:, 1, k:k + 1],
                                     scale=GB[:, 0, k:k + 1]).then_inc(s["done"], 1)
    give(nc, s)


def route(nc, M, A, gates):
    s = take(M, "par h_done logits sig step gated tr row bc_free bc")
    with ExitStack() as ctx:
        wr = ctx.enter_context(M.nc.sbuf_tensor(f"{M.blocks}_router_w", [P, KD, NE], F32))
        br = ctx.enter_context(M.nc.sbuf_tensor(f"{M.blocks}_router_b", [P, NE], F32))
        sel = ctx.enter_context(M.nc.sbuf_tensor(f"{M.blocks}_sel_e", [NE, NE, P], F32))
        sc = ctx.enter_context(M.nc.sbuf_tensor(f"{M.blocks}_r_score", [P, TT, NE], F32))
        bi = ctx.enter_context(M.nc.sbuf_tensor(f"{M.blocks}_r_biased", [P, TT, NE], F32))
        v = ctx.enter_context(M.nc.sbuf_tensor(f"{M.blocks}_r_cand", [P, TT, NE], F32))
        eq = ctx.enter_context(M.nc.sbuf_tensor(f"{M.blocks}_r_eq", [P, TT, NE], F32))
        chosen = ctx.enter_context(M.nc.sbuf_tensor(f"{M.blocks}_r_chosen", [P, TT, NE], F32))
        pair = ctx.enter_context(M.nc.sbuf_tensor(f"{M.blocks}_r_pair", [P, TT * NG, 6], F32))
        gs = ctx.enter_context(M.nc.sbuf_tensor(f"{M.blocks}_r_group", [P, TT, NG], F32))
        ge = ctx.enter_context(M.nc.sbuf_tensor(f"{M.blocks}_r_geq", [P, TT, NG], F32))
        m1 = ctx.enter_context(M.nc.sbuf_tensor(f"{M.blocks}_r_m1", [P, TT], F32))
        gT = ctx.enter_context(M.nc.sbuf_tensor(f"{M.blocks}_gate_rows", [NE, T], F32))
        block = ctx.enter_context(nc.Block())

        @block.sync
        def _(sp):
            sp.dma_start(wr[:], A["w_router"]).then_inc(s["par"], 16)
            sp.dma_start(br[:], A["b_router"].partition_broadcast(P)).then_inc(s["par"], 16)
            sp.dma_start(sel[:], A["sel_e"]).then_inc(s["par"], 16)

        @block.tensor
        def _(pe):
            pe.wait_ge(s["par"], 48)
            pe.wait_ge(s["h_done"], KD)
            for t in range(TT):
                for k in range(KD):
                    mm = nc.tensor.matmul(M.PS[:, 0, t * NE:(t + 1) * NE], M.hT[:, k, t * P:(t + 1) * P], wr[:, k, :],
                                          start=(k == 0), stop=(k == KD - 1))
            mm.then_inc(s["logits"], 1)
            pe.wait_ge(s["gated"], 1)
            for t in range(TT):
                mm = nc.tensor.transpose(M.PS[0:NE, 1, t * P:(t + 1) * P], v[:, t, :], M.K[:, K_ID:K_ID + P])
            mm.then_inc(s["tr"], 1)
            pe.wait_ge(s["row"], 1)
            for e in range(NE):
                if e >= 4:
                    pe.wait_ge(s["bc_free"], e - 3)
                nc.tensor.matmul(M.PS[:, 2 + e % 4, :], sel[:, e, :], gT[:], start=True, stop=True).then_inc(s["bc"], 1)

        @block.scalar
        def _(act):
            for k in range(KD):
                nc.scalar.activation(M.hT[:, k, 0:T], M.xT[:, k, 0:T], ACT.Identity,
                                     bias=modcol(M, 3, k), scale=modcol(M, 4, k)).then_inc(s["h_done"], 1)
            act.wait_ge(s["logits"], 1)
            nc.scalar.activation(sc[:], M.PS[:, 0, 0:TT * NE].rearrange("p (t e) -> p t e", t=TT),
                                 ACT.Sigmoid).then_inc(s["sig"], 1)
            act.wait_ge(s["tr"], 1)
            nc.scalar.activation(gT[:], M.PS[0:NE, 1, :], ACT.Copy).then_inc(s["row"], 1)
            for e in range(NE):
                act.wait_ge(s["bc"], e + 1)
                nc.scalar.activation(gates[:, e, :], M.PS[:, 2 + e % 4, :], ACT.Copy).then_inc(s["bc_free"], 1)

        @block.vector
        def _(dve):
            step = Steps(dve, s["step"])
            rank_e = M.K[:, K_RANK:K_RANK + NE].unsqueeze(1).to_broadcast([P, TT, NE])
            rank_g = M.K[:, K_RANK + NE:K_RANK + NE + NG].unsqueeze(1).to_broadcast([P, TT, NG])
            over_e = lambda a, n: a[:].unsqueeze(2).to_broadcast([P, TT, n])
            tt = nc.vector.tensor_tensor
            dve.wait_ge(s["par"], 48)
            dve.wait_ge(s["sig"], 1)
            step(tt(bi[:], sc[:], br[:].unsqueeze(1).to_broadcast([P, TT, NE]), ALU.add))
            quad = bi[:].rearrange("p t (g e) -> p (t g) e", e=EPG)
            at = 0
            for a in range(EPG - 1):
                for b in range(a + 1, EPG):
                    step(tt(pair[:, :, at:at + 1], quad[:, :, a:a + 1], quad[:, :, b:b + 1], ALU.add))
                    at += 1
            step(nc.vector.tensor_reduce(gs[:].rearrange("p t g -> p (t g)"), pair[:], AX.X, ALU.max))

            def first_best(out, val, n, rank):
                step(nc.vector.tensor_reduce(m1[:], val[:], AX.X, ALU.max))
                step(tt(out[:], val[:], over_e(m1, n), ALU.is_equal))
                step(tt(out[:], out[:], rank, ALU.mult))
                step(nc.vector.tensor_reduce(m1[:], out[:], AX.X, ALU.max))
                step(tt(out[:], out[:], over_e(m1, n), ALU.is_equal))

            first_best(ge, gs, NG, rank_g)
            geb = ge[:].rearrange("p t g -> p (t g)").unsqueeze(2).to_broadcast([P, TT * NG, EPG])
            step(tt(v[:].rearrange("p t (g e) -> p (t g) e", e=EPG), quad, geb, ALU.mult))
            step(nc.vector.tensor_scalar(ge[:], ge[:], -1.0, -NEG, ALU.add, ALU.mult))
            vq = v[:].rearrange("p t (g e) -> p (t g) e", e=EPG)
            step(tt(vq, vq, geb, ALU.add))
            first_best(chosen, v, NE, rank_e)
            step(nc.vector.scalar_tensor_tensor(out=v[:].rearrange("p t e -> p (t e)"),
                                                in0=chosen[:].rearrange("p t e -> p (t e)"), scalar=NEG,
                                                in1=v[:].rearrange("p t e -> p (t e)"), op0=ALU.mult, op1=ALU.add))
            first_best(eq, v, NE, rank_e)
            step(tt(chosen[:], chosen[:], eq[:], ALU.add))
            step(tt(v[:], chosen[:], sc[:], ALU.mult))
            step(nc.vector.tensor_reduce(m1[:], v[:], AX.X, ALU.add))
            step(nc.vector.reciprocal(m1[:], m1[:]))
            tt(v[:], v[:], over_e(m1, NE), ALU.mult).then_inc(s["gated"], 1)
    give(nc, s)


def gated_up(nc, M, wg, wu, hid, NF, spans, gates=None):
    s = take(M, "g0 g1 u0 u1 gate_used up_used silu_done psum_free prod_done hid_done")
    gr, ur = (s["g0"], s["g1"]), (s["u0"], s["u1"])
    NS = len(spans)
    TW = sum(n for _, n in spans)
    with ExitStack() as ctx:
        WG = ctx.enter_context(M.nc.sbuf_tensor(f"{M.blocks}_gate_w", [P, 2, KD, P], F32))
        WU = ctx.enter_context(M.nc.sbuf_tensor(f"{M.blocks}_up_w", [P, 2, KD, P], F32))
        sl = ctx.enter_context(M.nc.sbuf_tensor(f"{M.blocks}_silu", [P, 2, TW], F32))
        pr = ctx.enter_context(M.nc.sbuf_tensor(f"{M.blocks}_silu_up", [P, 2, TW], F32))
        block = ctx.enter_context(nc.Block())

        @block.sync
        def _(sp):
            for u in range(2):
                sp.dma_start(WG[:, u], wg(u)).then_inc(gr[u], 16)
                sp.dma_start(WU[:, u], wu(u)).then_inc(ur[u], 16)
            with sp.Fori(1, NF // 2) as i:
                for u in range(2):
                    sp.wait_ge(s["gate_used"], 2 * i + u - 1)
                    sp.dma_start(WG[:, u], wg(2 * i + u)).then_inc(gr[u], 16)
                    sp.wait_ge(s["up_used"], 2 * i + u - 1)
                    sp.dma_start(WU[:, u], wu(2 * i + u)).then_inc(ur[u], 16)

        @block.tensor
        def _(pe):
            with pe.Fori(0, NF // 2) as i:
                for u in range(2):
                    pe.wait_ge(s["psum_free"], 2 * i + u + 1)
                    for W, ready, used, bank in ((WG, gr, s["gate_used"], 4 * u), (WU, ur, s["up_used"], 4 * u + 2)):
                        pe.wait_ge(ready[u], 16 * i + 16)
                        for k in range(KD):
                            for a, (t0, nt) in enumerate(spans):
                                mm = nc.tensor.matmul(M.PS[:, bank + a, 0:nt], W[:, u, k, :],
                                                      M.hT[:, k, t0:t0 + nt], start=(k == 0), stop=(k == KD - 1))
                        mm.then_inc(used, 1)

        @block.scalar
        def _(act):
            with act.Fori(0, NF // 2) as i:
                for u in range(2):
                    act.wait_ge(s["gate_used"], 2 * i + u + 1)
                    at = 0
                    for a, (_, nt) in enumerate(spans):
                        ins = nc.scalar.activation(sl[:, u, at:at + nt], M.PS[:, 4 * u + a, 0:nt], ACT.Silu)
                        at += nt
                    ins.then_inc(s["silu_done"], 1)

        @block.vector
        def _(dve):
            dve.sem_inc(s["psum_free"], 2)
            with dve.Fori(0, NF // 2) as i:
                for u in range(2):
                    dve.wait_ge(s["silu_done"], 2 * i + u + 1)
                    dve.wait_ge(s["up_used"], 2 * i + u + 1)
                    at = 0
                    for a, (_, nt) in enumerate(spans):
                        if gates is not None:
                            ins = nc.vector.tensor_tensor(pr[:, u, at:at + nt], sl[:, u, at:at + nt],
                                                          M.PS[:, 4 * u + 2 + a, 0:nt], ALU.mult)
                        else:
                            ins = nc.vector.tensor_tensor(hid[:, bass.ds(2 * i + u, 1), at:at + nt],
                                                          sl[:, u:u + 1, at:at + nt],
                                                          M.PS[:, 4 * u + 2 + a:4 * u + 3 + a, 0:nt], ALU.mult)
                        at += nt
                    ins.then_inc(s["psum_free"], 1)
                    if gates is not None:
                        dve.wait_ge(s["psum_free"], 2 * i + u + 3)
                        nc.vector.tensor_tensor(hid[:, bass.ds(2 * i + u, 1), 0:TW], pr[:, u:u + 1, :],
                                                gates[:, bass.ds(i, 1), :], ALU.mult).then_inc(s["hid_done"], 1)
    give(nc, s)


def block_one(nc, M, A):
    with nc.Fori(0, DEPTH) as l:
        ada(nc, M, lambda n: A["w_ada"][l, n], A["b_ada"][l], 0, 1, (1, 2, 4, 5))
        with ExitStack() as ctx:
            def sb(name, shape):
                return ctx.enter_context(nc.sbuf_tensor(name, shape, F32))

            B = Buffers()
            B.mixT = sb("mixT", [P, KD, T])
            B.PT = sb("projT", [P, N_CH, T])
            B.V = sb("values", [P, TT, N_V])
            B.iw = sb("index_w", [P, TT * NH_I])
            proj1(nc, M, A, l, B)
            B.Amax = sb("i_max_all", [P, NH_M, T])
            B.floor = sb("floor_all", [P, NH_M // 2, T])
            B.acol = sb("i_rel_col", [P, TT * NH_M])
            B.bias = sb("key_bias", [P, TT, T])
            B.Y = sb("lin_y", [P, 4, T])
            convolve(nc, M, A, l, B)
            select_keys(nc, M, B)
            attend1(nc, M, B)
            linear_mixers(nc, M, B)
            head_norm(nc, M, B)
            gemm_residual(nc, M, lambda p: A["w_out"][l, p], B.mixT, 1, KD, [(0, T, 0, 1)], 2, ALPHA)
        layer_norm(nc, M, A["ln_mix"][l])
        with ExitStack() as ctx:
            hid = ctx.enter_context(M.nc.sbuf_tensor(f"{M.blocks}_hidden", [P, NE * FE // P, T], F32))
            with nc.sbuf_tensor("expert_gates", [P, NE, T], F32) as gates:
                route(nc, M, A, gates)
                gated_up(nc, M, lambda n: A["w_gate"][l, n], lambda n: A["w_up"][l, n], hid, NE * FE // P,
                         [(0, T)], gates)
            gemm_residual(nc, M, lambda p: A["w_down"][l, p], hid, 4, KD, [(0, T, 0, 1)], 5, ALPHA)
        layer_norm(nc, M, A["ln_ffn"][l])


def rms_modulate(nc, M, w, spans, shift=None, scale=None):
    s = take(M, "par ws step sq sum sd rstd norm done")
    NS = len(spans)
    with ExitStack() as ctx:
        nw = ctx.enter_context(M.nc.sbuf_tensor(f"{M.blocks}_norm_w", [P, KD], F32))
        ws = ctx.enter_context(M.nc.sbuf_tensor(f"{M.blocks}_norm_ws", [P, 2, KD], F32))
        sq = ctx.enter_context(M.nc.sbuf_tensor(f"{M.blocks}_rms_sq", [P, 4, T], F32))
        rs = ctx.enter_context(M.nc.sbuf_tensor(f"{M.blocks}_rms_rs", [P, 2, T], F32))
        block = ctx.enter_context(nc.Block())

        @block.sync
        def _(sp):
            sp.dma_start(nw[:], w).then_inc(s["par"], 16)

        @block.tensor
        def _(pe):
            for a, (t0, nt, c) in enumerate(spans):
                for k in range(KD):
                    n = a * KD + k
                    pe.wait_ge(s["sq"], n + 1)
                    nc.tensor.matmul(M.PS[:, a, 0:nt], M.K[:, K_MEAN:K_MEAN + P], sq[:, n % 4, 0:nt],
                                     start=(k == 0), stop=(k == KD - 1)).then_inc(s["sum"], 1)

        @block.vector
        def _(dve):
            dve.wait_ge(s["par"], 16)
            for a, (t0, nt, c) in enumerate(spans):
                if scale is None:
                    nc.vector.tensor_copy(ws[:, a, :], nw[:]).then_inc(s["ws"], 1)
                else:
                    part = M.mod[:, scale * KD * 2:(scale + 1) * KD * 2].rearrange("p (k c) -> p k c", c=2)
                    nc.vector.tensor_tensor(ws[:, a, :], nw[:], part[:, :, c], ALU.mult).then_inc(s["ws"], 1)
            for a, (t0, nt, c) in enumerate(spans):
                dve.wait_ge(s["sd"], a + 1)
                nc.vector.reciprocal(rs[:, a, 0:nt], rs[:, a, 0:nt]).then_inc(s["rstd"], 1)
                dve.wait_ge(s["rstd"], a + 1)
                for k in range(KD):
                    nc.vector.tensor_tensor(M.hT[:, k, t0:t0 + nt], M.xT[:, k, t0:t0 + nt], rs[:, a, 0:nt],
                                            ALU.mult).then_inc(s["norm"], 1)

        @block.scalar
        def _(act):
            for a, (t0, nt, c) in enumerate(spans):
                for k in range(KD):
                    n = a * KD + k
                    if n >= 4:
                        act.wait_ge(s["sum"], n - 3)
                    nc.scalar.activation(sq[:, n % 4, 0:nt], M.xT[:, k, t0:t0 + nt], ACT.Square).then_inc(s["sq"], 1)
                act.wait_ge(s["sum"], (a + 1) * KD)
                nc.scalar.activation(rs[:, a, 0:nt], M.PS[:, a, 0:nt], ACT.Sqrt, bias=M.eps[:, 1:2]).then_inc(s["sd"], 1)
            act.wait_ge(s["ws"], NS)
            for a, (t0, nt, c) in enumerate(spans):
                for k in range(KD):
                    act.wait_ge(s["norm"], a * KD + k + 1)
                    h = M.hT[:, k, t0:t0 + nt]
                    bias = 0.0 if shift is None else modcol(M, shift, k, 2, c)
                    nc.scalar.activation(h, h, ACT.Identity, bias=bias, scale=ws[:, a, k:k + 1]).then_inc(s["done"], 1)
    give(nc, s)


def project(nc, M, wt, n_t, out, spans, wv=None, n_v=0, outv=None, tiles=0, loads=()):
    s = take(M, "w0 w1 used psum_free copied wv tok_done tok_free more")
    ready = (s["w0"], s["w1"])
    PAIRS = n_t // 2
    with ExitStack() as ctx:
        W = ctx.enter_context(M.nc.sbuf_tensor(f"{M.blocks}_proj_w", [P, 2, KD, P], F32))
        WV = ctx.enter_context(M.nc.sbuf_tensor(f"{M.blocks}_proj_wv", [P, max(n_v, 1), KD, 512], F32))
        block = ctx.enter_context(nc.Block())

        @block.sync
        def _(sp):
            for u in range(2):
                sp.dma_start(W[:, u], wt(u)).then_inc(ready[u], 16)
            for g in range(n_v):
                sp.dma_start(WV[:, g], wv[g]).then_inc(s["wv"], 16)
            if PAIRS > 1:
                with sp.Fori(1, PAIRS) as i:
                    for u in range(2):
                        sp.wait_ge(s["used"], 2 * i + u - 1)
                        sp.dma_start(W[:, u], wt(2 * i + u)).then_inc(ready[u], 16)
            if n_t % 2:
                sp.wait_ge(s["used"], n_t - 2)
                sp.dma_start(W[:, 0], wt(n_t - 1)).then_inc(s["w0"], 16)
            for dst, src in loads:
                sp.dma_start(dst, src).then_inc(s["more"], 16)
            if loads:
                sp.wait_ge(s["more"], 16 * len(loads))

        @block.tensor
        def _(pe):
            def chunk(n, u, i):
                pe.wait_ge(ready[u], 16 * i + 16)
                pe.wait_ge(s["psum_free"], n + 1)
                for k in range(KD):
                    for a, (t0, nt) in enumerate(spans):
                        mm = nc.tensor.matmul(M.PS[:, 4 * u + a, 0:nt], W[:, u, k, :], M.hT[:, k, t0:t0 + nt],
                                              start=(k == 0), stop=(k == KD - 1))
                mm.then_inc(s["used"], 1)

            with pe.Fori(0, PAIRS) as i:
                for u in range(2):
                    chunk(2 * i + u, u, i)
            if n_t % 2:
                chunk(n_t - 1, 0, PAIRS)
            if n_v:
                pe.wait_ge(s["wv"], 16 * n_v)
            for n in range(n_v * tiles):
                g, t = n // tiles, n % tiles
                if n >= 2:
                    pe.wait_ge(s["tok_free"], n - 1)
                for k in range(KD):
                    mm = nc.tensor.matmul(M.PS[:, 2 + n % 2, :], M.hT[:, k, t * P:(t + 1) * P], WV[:, g, k, :],
                                          start=(k == 0), stop=(k == KD - 1))
                mm.then_inc(s["tok_done"], 1)

        @block.scalar
        def _(act):
            act.sem_inc(s["psum_free"], 2)

            def copy(n, u):
                act.wait_ge(s["used"], n + 1)
                at = 0
                for a, (_, nt) in enumerate(spans):
                    o = out[:, n, at:at + nt] if isinstance(n, int) else out[:, bass.ds(n, 1), at:at + nt]
                    ins = nc.scalar.activation(o, M.PS[:, 4 * u + a, 0:nt], ACT.Copy)
                    at += nt
                ins.then_inc(s["copied"], 1)
                act.wait_ge(s["copied"], n + 1)
                act.sem_inc(s["psum_free"], 1)

            with act.Fori(0, PAIRS) as i:
                for u in range(2):
                    copy(2 * i + u, u)
            if n_t % 2:
                copy(n_t - 1, 0)
            for n in range(n_v * tiles):
                g, t = n // tiles, n % tiles
                act.wait_ge(s["tok_done"], n + 1)
                nc.scalar.activation(outv[:, t, g * 512:(g + 1) * 512], M.PS[:, 2 + n % 2, :],
                                     ACT.Copy).then_inc(s["tok_free"], 1)
    give(nc, s)


def spatial_gate(nc, M, A, B):
    s = take(M, "par gelu_v ssq sd rstd normed gelu_u gate biased done")
    NT = TA // P
    with ExitStack() as ctx:
        sw = ctx.enter_context(M.nc.sbuf_tensor(f"{M.blocks}_sgu_w", [P, 4, P], F32))
        sb_ = ctx.enter_context(M.nc.sbuf_tensor(f"{M.blocks}_sgu_b", [P, 4 * P], F32))
        nw = ctx.enter_context(M.nc.sbuf_tensor(f"{M.blocks}_sgu_nw", [P, 4], F32))
        ssq = ctx.enter_context(M.nc.sbuf_tensor(f"{M.blocks}_sgu_ssq", [P, NT], F32))
        junk = ctx.enter_context(M.nc.sbuf_tensor(f"{M.blocks}_sgu_sq", [P, NT, 512], F32))
        g_ = ctx.enter_context(M.nc.sbuf_tensor(f"{M.blocks}_sgu_gate", [P, 2, 512], F32))
        block = ctx.enter_context(nc.Block())

        @block.sync
        def _(sp):
            sp.dma_start(sw[:], A["sgu_w"]).then_inc(s["par"], 16)
            sp.dma_start(sb_[:], A["sgu_b"].partition_broadcast(P)).then_inc(s["par"], 16)
            sp.dma_start(nw[:], A["sgu_nw"]).then_inc(s["par"], 16)

        @block.scalar
        def _(act):
            for t in range(NT):
                v = B.V[:, t, 0:512]
                nc.scalar.activation(v, v, ACT.Gelu_apprx_tanh).then_inc(s["gelu_v"], 1)
            for c in range(4):
                u = B.PT[:, c, :]
                nc.scalar.activation(u, u, ACT.Gelu_apprx_tanh).then_inc(s["gelu_u"], 1)
            for t in range(NT):
                act.wait_ge(s["gelu_v"], t + 1)
                nc.scalar.activation(junk[:, t, :], B.V[:, t, 0:512], ACT.Square,
                                     accum_out=ssq[:, t:t + 1]).then_inc(s["ssq"], 1)
            act.wait_ge(s["ssq"], NT)
            nc.scalar.activation(ssq[:], ssq[:], ACT.Sqrt, bias=M.eps[:, 1:2], scale=1.0 / 512).then_inc(s["sd"], 1)

        @block.vector
        def _(dve):
            dve.wait_ge(s["sd"], 1)
            nc.vector.reciprocal(ssq[:], ssq[:]).then_inc(s["rstd"], 1)
            dve.wait_ge(s["rstd"], 1)
            for t in range(NT):
                v = B.V[:, t, 0:512]
                nc.vector.tensor_scalar(v, v, ssq[:, t:t + 1], None, ALU.mult).then_inc(s["normed"], 1)
            dve.wait_ge(s["par"], 48)
            n = 0
            for g in range(4):
                dve.wait_ge(s["gate"], g + 1)
                dve.wait_ge(s["gelu_u"], g + 1)
                for a, (t0, nt) in enumerate(((0, T), (T, TC))):
                    out = g_[:, a, 0:nt].rearrange("p (t q) -> p t q", q=P)
                    bias = sb_[:, g * P:(g + 1) * P].unsqueeze(1).to_broadcast([P, nt // P, P])
                    nc.vector.scalar_tensor_tensor(out=out, in0=M.PS[:, 2 * g + a, 0:nt].rearrange("p (t q) -> p t q", q=P),
                                                   scalar=nw[:, g:g + 1], in1=bias, op0=ALU.mult,
                                                   op1=ALU.add).then_inc(s["biased"], 1)
                    n += 1
                    dve.wait_ge(s["biased"], n)
                    nc.vector.tensor_tensor(B.mixT[:, g, t0:t0 + nt], g_[:, a, 0:nt], B.PT[:, g, t0:t0 + nt],
                                            ALU.mult).then_inc(s["done"], 1)

        @block.tensor
        def _(pe):
            pe.wait_ge(s["par"], 48)
            pe.wait_ge(s["normed"], NT)
            for g in range(4):
                for t in range(NT):
                    mm = nc.tensor.matmul(M.PS[:, 2 * g + t // 4, (t % 4) * P:(t % 4 + 1) * P],
                                          B.V[:, t, g * P:(g + 1) * P], sw[:, g, :], start=True, stop=True)
                mm.then_inc(s["gate"], 1)
    give(nc, s)


def attend2(nc, M, B):
    items = []
    for t in range(TA // P):
        for h in range(8):
            b, c = HD * (h % 2), h // 2
            ctx_keys = (B.PT[b:b + HD, 8 + c, T:TA], TC, None)
            grid_keys = (B.PT[b:b + HD, 8 + c, 0:T], T, B.rel[:, h, (7 - 2 * t) * 64:(15 - 2 * t) * 64])
            latent = t < TT
            items.append(Item(
                q=B.PT[b:b + HD, 4 + c, t * P:(t + 1) * P],
                segs=[grid_keys, ctx_keys] if latent else [ctx_keys],
                vs=[B.V[:, j, 512 + h * HD:512 + (h + 1) * HD] for j in range(0 if latent else TT, TA // P)],
                o=B.mixT[:, 4 + c, t * P:(t + 1) * P]))
    attend(nc, M, items, HD ** -0.5)


def fourier(nc, M, A, B):
    s = take(M, "tab ch ch_out tok tok_out")
    with ExitStack() as ctx:
        FT = ctx.enter_context(M.nc.sbuf_tensor(f"{M.blocks}_dft_t", [P, 2, TT, T], F32))
        G = ctx.enter_context(M.nc.sbuf_tensor(f"{M.blocks}_dft_g", [P, 16, 2 * P], F32))
        block = ctx.enter_context(nc.Block())

        @block.sync
        def _(sp):
            sp.dma_start(FT[:], A["dft_t"]).then_inc(s["tab"], 16)

        @block.tensor
        def _(pe):
            for n in range(16):
                g, t = n // TT, n % TT
                if n >= 4:
                    pe.wait_ge(s["ch_out"], n - 3)
                nc.tensor.matmul(M.PS[:, n % 4, 0:2 * P], B.PT[:, g, t * P:(t + 1) * P], B.K2[:, J_DFT:J_DFT + 2 * P],
                                 start=True, stop=True).then_inc(s["ch"], 1)
            pe.wait_ge(s["tab"], 16)
            for g in range(4):
                pe.wait_ge(s["ch_out"], 4 * g + 4)
                for t in range(TT):
                    for j in range(2):
                        mm = nc.tensor.matmul(M.PS[:, 4 + g, :], G[:, g * TT + t, j * P:(j + 1) * P], FT[:, j, t, :],
                                              start=(t + j == 0), stop=(t == TT - 1 and j == 1))
                mm.then_inc(s["tok"], 1)

        @block.scalar
        def _(act):
            for n in range(16):
                act.wait_ge(s["ch"], n + 1)
                nc.scalar.activation(G[:, n, :], M.PS[:, n % 4, 0:2 * P], ACT.Copy).then_inc(s["ch_out"], 1)
            for g in range(4):
                act.wait_ge(s["tok"], g + 1)
                nc.scalar.activation(B.mixT[:, g, :], M.PS[:, 4 + g, :], ACT.Copy).then_inc(s["tok_out"], 1)
    give(nc, s)


def gla_prepare(nc, M, A, B):
    s = take(M, "par rot turned step z lin e1 la ex exd step2")
    NC = TA // 64
    with ExitStack() as ctx:
        dw = ctx.enter_context(M.nc.sbuf_tensor(f"{M.blocks}_dec_w", [48, 256], F32))
        db = ctx.enter_context(M.nc.sbuf_tensor(f"{M.blocks}_dec_b", [P, 4], F32))
        t1 = ctx.enter_context(M.nc.sbuf_tensor(f"{M.blocks}_ax1", [P, T], F32))
        t2 = ctx.enter_context(M.nc.sbuf_tensor(f"{M.blocks}_ax2", [P, T], F32))
        la = ctx.enter_context(M.nc.sbuf_tensor(f"{M.blocks}_log_a", [P, 4, TA], F32))
        z = ctx.enter_context(M.nc.sbuf_tensor(f"{M.blocks}_dec_z", [P, 4, TA], F32))
        pre = ctx.enter_context(M.nc.sbuf_tensor(f"{M.blocks}_dec_pre", [P, 4, TA], F32))
        block = ctx.enter_context(nc.Block())

        @block.sync
        def _(sp):
            sp.dma_start(dw[0:16], A["dec_w"][0]).then_inc(s["par"], 16)
            sp.dma_start(dw[32:48], A["dec_w"][1]).then_inc(s["par"], 16)
            sp.dma_start(db[:], A["dec_b"]).then_inc(s["par"], 16)

        @block.tensor
        def _(pe):
            pe.wait_ge(s["par"], 48)
            for j in range(4):
                d, c = j // 2, j % 2
                if j >= 1:
                    pe.wait_ge(s["lin"], j)
                nc.tensor.matmul(M.PS[:, 0, :], dw[32 * d:32 * d + 16, c * P:(c + 1) * P],
                                 B.KA[32 * d:32 * d + 16, 2, 0:T], start=True, stop=True)
                nc.tensor.matmul(M.PS[:, 1, 0:TC], dw[32 * d:32 * d + 16, c * P:(c + 1) * P],
                                 B.KA[32 * d:32 * d + 16, 2, T:TA], start=True, stop=True).then_inc(s["z"], 1)
            for j in range(4):
                x = B.PT[:, 4 + j, 0:T] if j < 2 else B.KA[:, j - 2, 0:T]
                nc.tensor.matmul(M.PS[:, 2 + j, :], B.K2[:, J_ROT:J_ROT + P], x, start=True,
                                 stop=True).then_inc(s["rot"], 1)

        @block.vector
        def _(dve):
            step = Steps(dve, s["step"])
            tt, ts, stt = nc.vector.tensor_tensor, nc.vector.tensor_scalar, nc.vector.scalar_tensor_tensor
            dve.wait_ge(s["par"], 48)
            for j in range(4):
                dve.wait_ge(s["z"], j + 1)
                step(ts(z[:, j, 0:T], M.PS[:, 0, :], db[:, j:j + 1], None, ALU.add))
                ts(z[:, j, T:TA], M.PS[:, 1, 0:TC], db[:, j:j + 1], None, ALU.add).then_inc(s["lin"], 1)
                dve.wait_ge(s["lin"], j + 1)
                stt(out=la[:, j, :], in0=z[:, j, :], scalar=-1.0, in1=z[:, j, :], op0=ALU.mult,
                    op1=ALU.max).then_inc(s["e1"], 1)
            for j in range(4):
                x = B.PT[:, 4 + j, 0:T] if j < 2 else B.KA[:, j - 2, 0:T]
                dve.wait_ge(s["rot"], j + 1)
                step(tt(t1[:], x, B.K2[:, J_COS:J_COS + T], ALU.mult))
                step(tt(t2[:], M.PS[:, 2 + j, :], B.K2[:, J_SIN:J_SIN + T], ALU.mult))
                step(tt(x, t1[:], t2[:], ALU.add))
            for j in range(4):
                d = j // 2
                dve.wait_ge(s["la"], j + 1)
                step(stt(out=la[:, j, :], in0=z[:, j, :], scalar=0.0, in1=la[:, j, :], op0=ALU.min, op1=ALU.subtract))
                step(ts(la[:, j, :], la[:, j, :], 1.0 / 16, None, ALU.mult))
                step(nc.vector.tensor_tensor_scan(out=pre[:, j, :], data0=B.K2[:, J_RST:J_RST + TA], data1=la[:, j, :],
                                                  initial=0.0, op0=ALU.mult, op1=ALU.add))
                p3 = pre[:, j, :].rearrange("p (n l) -> p n l", l=64)
                z3 = z[:, j, :].rearrange("p (n l) -> p n l", l=64)
                total = p3[:, :, 63:64].to_broadcast([P, NC, 64])
                step(nc.vector.tensor_copy(B.dec[:, j, :], p3[:, :, 63]))
                if d == 0:
                    tt(z3, total, p3, ALU.subtract).then_inc(s["ex"], 1)
                else:
                    step(tt(z3, total, p3, ALU.subtract))
                    step(tt(t1[:], z[:, j, 0:T], la[:, j, 0:T], ALU.add))
                    step(tt(z[:, j, :], pre[:, j, :], la[:, j, :], ALU.subtract))
                    nc.vector.tensor_copy(pre[:, j, 0:T], t1[:]).then_inc(s["ex"], 1)
            for j in range(4):
                c = j % 2
                dve.wait_ge(s["exd"], j + 1)
                step(stt(out=B.qe[:, j, :], in0=B.PT[:, 4 + c, 0:T], scalar=64 ** -0.5, in1=B.qe[:, j, :],
                         op0=ALU.mult, op1=ALU.mult))
                step(tt(B.ke[:, j, :], B.KA[:, c, 0:T], B.ke[:, j, :], ALU.mult))
                step(tt(B.kd[:, j, :], B.KA[:, c, :], B.kd[:, j, :], ALU.mult))

        @block.scalar
        def _(act):
            step = Steps(act, s["step2"])
            for j in range(4):
                act.wait_ge(s["e1"], j + 1)
                step(nc.scalar.activation(la[:, j, :], la[:, j, :], ACT.Exp, scale=-1.0))
            for j in range(4):
                nc.scalar.activation(la[:, j, :], la[:, j, :], ACT.Ln, bias=1.0).then_inc(s["la"], 1)
            for j in range(4):
                act.wait_ge(s["ex"], j + 1)
                step(nc.scalar.activation(B.dec[:, j, :], B.dec[:, j, :], ACT.Exp))
                step(nc.scalar.activation(B.qe[:, j, :], pre[:, j, 0:T], ACT.Exp))
                step(nc.scalar.activation(B.ke[:, j, :], pre[:, j, 0:T], ACT.Exp, scale=-1.0))
                nc.scalar.activation(B.kd[:, j, :], z[:, j, :], ACT.Exp).then_inc(s["exd"], 1)
            for c in range(4):
                nc.scalar.activation(B.PT[:, 6 + c, 0:T], B.PT[:, 6 + c, 0:T], ACT.Silu)
    give(nc, s)


def gla_states(nc, M, B):
    s = take(M, "tr tr_out kv kv_free state")
    NT = TA // P
    with ExitStack() as ctx:
        kt = ctx.enter_context(M.nc.sbuf_tensor(f"{M.blocks}_kd_tok", [P, 2, NT, 256], F32))
        S = ctx.enter_context(M.nc.sbuf_tensor(f"{M.blocks}_state", [P, 2, 2, P], F32))
        block = ctx.enter_context(nc.Block())

        def bank(c, n):
            m = n // 2
            return M.PS[:, 4 * (n % 2) + 2 * c + m // 4, (m % 4) * P:(m % 4 + 1) * P]

        @block.tensor
        def _(pe):
            for d in range(2):
                if d:
                    pe.wait_ge(s["kv_free"], 1)
                for t in range(NT):
                    n = d * NT + t
                    if t >= 2:
                        pe.wait_ge(s["tr_out"], n - 1)
                    for c in range(2):
                        mm = nc.tensor.transpose(M.PS[:, t % 2, c * P:(c + 1) * P], B.kd[:, 2 * d + c, t * P:(t + 1) * P],
                                                 M.K[:, K_ID:K_ID + P])
                    mm.then_inc(s["tr"], 1)
                pe.wait_ge(s["tr_out"], (d + 1) * NT)
                for odd in range(2):
                    for n in range(odd, 2 * NT, 2):
                        for h in range(4):
                            b, r = 64 * (h % 2), 64 * odd
                            mm = nc.tensor.matmul(bank(h // 2, n)[b:b + 64], kt[r:r + 64, d, n // 2, h * 64:(h + 1) * 64],
                                                  B.V[r:r + 64, n // 2, h * P:(h + 1) * P], start=True, stop=True)
                mm.then_inc(s["kv"], 1)

        @block.scalar
        def _(act):
            for d in range(2):
                for t in range(NT):
                    act.wait_ge(s["tr"], d * NT + t + 1)
                    nc.scalar.activation(kt[:, d, t, :], M.PS[:, t % 2, 0:256], ACT.Copy).then_inc(s["tr_out"], 1)

        @block.vector
        def _(dve):
            done = 0
            for d in range(2):
                dve.wait_ge(s["kv"], d + 1)
                order = [8, 9, 10, 11] + list(range(8))
                if d:
                    order = [11, 10, 9, 8] + list(range(7, -1, -1))
                for i, n in enumerate(order[:-1]):
                    nxt = order[i + 1]
                    for c in range(2):
                        out = B.Sp[:, d, c, nxt, :] if nxt < 8 else S[:, c, i % 2, :]
                        if i == 0:
                            ins = nc.vector.tensor_copy(out, bank(c, n))
                        else:
                            cur = B.Sp[:, d, c, n, :] if n < 8 else S[:, c, (i - 1) % 2, :]
                            dve.wait_ge(s["state"], done - 1)
                            ins = nc.vector.scalar_tensor_tensor(out=out, in0=cur, scalar=B.dec[:, 2 * d + c, n:n + 1],
                                                                 in1=bank(c, n), op0=ALU.mult, op1=ALU.add)
                        ins.then_inc(s["state"], 1)
                        done += 1
                dve.wait_ge(s["state"], done)
                dve.sem_inc(s["kv_free"], 1)
    give(nc, s)


def gla_outputs(nc, M, A, B):
    s = take(M, "par att masked pv sq ssum sd rstd norm done")
    with ExitStack() as ctx:
        am = ctx.enter_context(M.nc.sbuf_tensor(f"{M.blocks}_gla_att", [P, 2, 2 * P], F32))
        hw = ctx.enter_context(M.nc.sbuf_tensor(f"{M.blocks}_gla_hw", [P, 2], F32))
        sq = ctx.enter_context(M.nc.sbuf_tensor(f"{M.blocks}_gla_sq", [P, 4, T], F32))
        nm = ctx.enter_context(M.nc.sbuf_tensor(f"{M.blocks}_gla_nm", [P, 4, T], F32))
        block = ctx.enter_context(nc.Block())
        N = 4 * TT

        @block.sync
        def _(sp):
            sp.dma_start(hw[:, 0:1], A["head_w"]).then_inc(s["par"], 16)

        @block.tensor
        def _(pe):
            def scores(n):
                h, t = n // TT, n % TT
                b, c = 64 * (h % 2), h // 2
                if n >= 2:
                    pe.wait_ge(s["masked"], n - 1)
                for d in range(2):
                    mm = nc.tensor.matmul(M.PS[:, n % 2, d * P:(d + 1) * P], B.ke[b:b + 64, 2 * d + c, t * P:(t + 1) * P],
                                          B.qe[b:b + 64, 2 * d + c, t * P:(t + 1) * P], start=True, stop=True)
                mm.then_inc(s["att"], 1)

            def values(n):
                h, t = n // TT, n % TT
                b, c = 64 * (h % 2), h // 2
                pe.wait_ge(s["masked"], n + 1)
                for d in range(2):
                    nc.tensor.matmul(M.PS[:, 2 + h, t * P:(t + 1) * P], B.V[:, t, h * P:(h + 1) * P],
                                     am[:, n % 2, d * P:(d + 1) * P], start=(d == 0), stop=False)
                for d in range(2):
                    for j in range(2):
                        at = t * P + j * 64
                        last = d == 1 and j == 1
                        mm = nc.tensor.matmul(M.PS[:, 2 + h, at:at + 64], B.Sp[b:b + 64, d, c, 2 * t + j, :],
                                              B.qe[b:b + 64, 2 * d + c, at:at + 64], start=False, stop=last)
                mm.then_inc(s["pv"], 1)

            for n in range(N + 1):
                if n < N:
                    scores(n)
                if n >= 1:
                    values(n - 1)
            for h in range(4):
                pe.wait_ge(s["sq"], h + 1)
                if h >= 2:
                    pe.wait_ge(s["sd"], h - 1)
                nc.tensor.matmul(M.PS[:, 6 + h % 2, :], M.K[:, K_ONE:K_ONE + P], sq[:, h, :], start=True,
                                 stop=True).then_inc(s["ssum"], 1)

        @block.vector
        def _(dve):
            for n in range(N):
                dve.wait_ge(s["att"], n + 1)
                if n >= 2:
                    dve.wait_ge(s["pv"], n - 1)
                nc.vector.tensor_tensor(am[:, n % 2, :], M.PS[:, n % 2, 0:2 * P], B.K2[:, J_MASK:J_MASK + 2 * P],
                                        ALU.mult).then_inc(s["masked"], 1)
            dve.wait_ge(s["par"], 16)
            for h in range(4):
                dve.wait_ge(s["sd"], h + 1)
                nc.vector.reciprocal(sq[:, h, :], sq[:, h, :]).then_inc(s["rstd"], 1)
                dve.wait_ge(s["rstd"], h + 1)
                nc.vector.tensor_tensor(nm[:, h, :], M.PS[:, 2 + h, :], sq[:, h, :], ALU.mult).then_inc(s["norm"], 1)
                dve.wait_ge(s["norm"], h + 1)
                nc.vector.scalar_tensor_tensor(out=B.mixT[:, 4 + h, :], in0=nm[:, h, :], scalar=hw[:, 0:1],
                                               in1=B.PT[:, 6 + h, 0:T], op0=ALU.mult, op1=ALU.mult).then_inc(s["done"], 1)

        @block.scalar
        def _(act):
            for h in range(4):
                act.wait_ge(s["pv"], TT * (h + 1))
                nc.scalar.activation(sq[:, h, :], M.PS[:, 2 + h, :], ACT.Square).then_inc(s["sq"], 1)
            for h in range(4):
                act.wait_ge(s["ssum"], h + 1)
                nc.scalar.activation(sq[:, h, :], M.PS[:, 6 + h % 2, :], ACT.Sqrt, bias=M.eps[:, 1:2],
                                     scale=1.0 / P).then_inc(s["sd"], 1)
    give(nc, s)


def feed_forward(nc, M, A, i, spans):
    rms_modulate(nc, M, A["norm_ffn"][i], spans, 3, 4)
    with ExitStack() as ctx:
        NF = FFN // P
        hid = ctx.enter_context(M.nc.sbuf_tensor(f"ffn_hidden{i}", [P, NF, sum(n for _, n, _ in spans)], F32))
        gated_up(nc, M, lambda n: A["f_gate"][i, n], lambda n: A["f_up"][i, n], hid, NF, [(t, n) for t, n, _ in spans])
        gemm_residual(nc, M, lambda p: A["f_down"][i, p], hid, 2, NF // 2, [(t, n, c, 2) for t, n, c in spans], 5, 1.0)


def block_two(nc, M, A):
    both = [(0, T, 0), (T, TC, 1)]
    latent = both[:1]
    ada(nc, M, lambda n: A["ada_w2"][0, n], A["ada_b2"][0], 1, 2, (1, 4))
    rms_modulate(nc, M, A["norm_mix"][0], both, 0, 1)
    with ExitStack() as ctx:
        def sb(name, shape):
            return ctx.enter_context(M.nc.sbuf_tensor("ab_" + name, shape, F32))

        B = Buffers()
        B.PT, B.V = sb("projT", [P, 12, TA]), sb("values", [P, TA // P, 1024])
        B.rel = sb("rel", [P, 8, 16 * 64])
        project(nc, M, lambda n: A["ab_t"][n], 12, B.PT, [(0, T), (T, TC)], A["ab_v"], 2, B.V, TA // P,
                [(B.rel[:], A["rel"])])
        B.mixT = sb("mixT", [P, KD, TA])
        spatial_gate(nc, M, A, B)
        attend2(nc, M, B)
        gemm_residual(nc, M, lambda p: A["ab_out"][p], B.mixT, 1, KD, [(0, T, 0, 2), (T, TC, 1, 2)], 2, 1.0)
    feed_forward(nc, M, A, 0, both)

    ada(nc, M, lambda n: A["ada_w2"][1, n], A["ada_b2"][1], 1, 2, (1, 4))
    rms_modulate(nc, M, A["norm_mix"][1], both, 0, 1)
    with ExitStack() as ctx:
        def sb(name, shape):
            return ctx.enter_context(M.nc.sbuf_tensor("cd_" + name, shape, F32))

        B = Buffers()
        B.PT, B.KA, B.V = sb("projT", [P, 10, T]), sb("keysT", [P, 3, TA]), sb("values", [P, TA // P, 512])
        B.K2, B.mixT = sb("consts", [P, J_N]), sb("mixT", [P, KD, T])
        project(nc, M, lambda n: A["cd_t"][n], 10, B.PT, [(0, T)])
        project(nc, M, lambda n: A["cd_k"][n], 3, B.KA, [(0, T), (T, TC)], A["cd_v"], 1, B.V, TA // P,
                [(B.K2[:], A["consts2"])])
        fourier(nc, M, A, B)
        B.qe, B.ke, B.kd = sb("qe", [P, 4, T]), sb("ke", [P, 4, T]), sb("kd", [P, 4, TA])
        B.dec = sb("dec", [P, 4, TA // 64])
        gla_prepare(nc, M, A, B)
        B.Sp = sb("Sp", [P, 2, 2, 8, P])
        gla_states(nc, M, B)
        gla_outputs(nc, M, A, B)
        gemm_residual(nc, M, lambda p: A["cd_out"][p], B.mixT, 1, KD, [(0, T, 0, 2)], 2, 1.0)
    feed_forward(nc, M, A, 1, latent)
    rms_modulate(nc, M, A["final_w"], latent)


def program(nc, A, out, parts=2):
    with ExitStack() as ctx:
        def sb(name, shape):
            return ctx.enter_context(nc.sbuf_tensor(name, shape, F32))

        M = Buffers()
        M.nc, M.blocks = nc, 0
        M.PS = ctx.enter_context(nc.psum_tensor("PS", [P, 8, 512], F32))
        M.xT = sb("xT", [P, KD, TA])
        M.hT = sb("hT", [P, KD, TA])
        M.K = sb("consts", [P, K_N])
        M.cos, M.sin = sb("cosT", [P, T]), sb("sinT", [P, T])
        M.cond = sb("cond", [P, 3, KD])
        M.condT = M.cond[:].rearrange("p c k -> p k c")
        M.mod = sb("mod", [P, 96])
        M.eps = sb("eps", [P, 2])
        s = take(M, "eps_in stored")
        with nc.Block() as block:
            @block.vector
            def _(dve):
                nc.vector.memset(M.eps[:, 0:1], EPS).then_inc(s["eps_in"], 1)
                nc.vector.memset(M.eps[:, 1:2], RMS_EPS).then_inc(s["eps_in"], 1)
        give(nc, s)
        setup(nc, M, A)
        block_one(nc, M, A)
        if parts > 1:
            block_two(nc, M, A)
        s = take(M, "stored")
        with nc.Block() as block:
            @block.sync
            def _(sp):
                sp.dma_start(out, M.hT[:, :, 0:T]).then_inc(s["stored"], 16)
                sp.wait_ge(s["stored"], 16)
        give(nc, s)



def consts():
    K = np.zeros((P, K_N), np.float32)
    i = np.arange(P)
    K[:, K_ID:K_ID + P] = np.eye(P)
    rot = np.zeros((P, P))
    for m in range(P):
        rot[m + HALF if m % HD < HALF else m - HALF, m] = -1.0 if m % HD < HALF else 1.0
    K[:, K_ROT:K_ROT + P] = rot
    K[:, K_HEAD:K_HEAD + P] = (i[:, None] // HD == i[None] // HD) / HD
    K[:, K_ONE:K_ONE + P] = 1.0
    K[:, K_MEAN:K_MEAN + P] = 1.0 / D
    K[:, K_UP:K_UP + P] = i[:, None] <= i[None]
    d = np.arange(T)[None] - i[:, None]
    for h in range(NH_R):
        K[:, K_DEC + h * T:K_DEC + (h + 1) * T] = np.where(d >= 0, np.exp(np.maximum(d, 0) * math.log1p(-2.0 ** (-5 - h))), 0)
    for h in range(NH_M):
        K[h, K_SELH + h * P:K_SELH + (h + 1) * P] = 1.0
        K[h, K_SELP + h * HD:K_SELP + (h + 1) * HD] = 1.0
    K[:, K_RANK:K_RANK + NE] = NE - np.arange(NE)
    K[:, K_RANK + NE:K_RANK + NE + NG] = NG - np.arange(NG)
    K[:, K_FREQ] = np.float32(10000.0) ** (-(i % HALF).astype(np.float32) / np.float32(HALF))
    return K


def consts2():
    K = np.zeros((P, J_N), np.float32)
    i = np.arange(P)
    for m in range(P):
        K[m + 16 if m % 32 < 16 else m - 16, J_ROT + m] = -1.0 if m % 32 < 16 else 1.0
    same = i[:, None] // 64 == i[None] // 64
    K[:, J_MASK:J_MASK + P] = same & (i[:, None] <= i[None])
    K[:, J_MASK + P:J_MASK + 2 * P] = same & (i[:, None] >= i[None])
    t = np.arange(T, dtype=np.float32)
    pos = np.where((i % 64 < 32)[:, None], t[None] // 64, t[None] % 64).astype(np.float32)
    freq = (np.float32(10000.0) ** (-(i % 16).astype(np.float32) / np.float32(16))).astype(np.float32)
    ang = (pos * freq[:, None]).astype(np.float32).astype(np.float64)
    K[:, J_COS:J_COS + T], K[:, J_SIN:J_SIN + T] = np.cos(ang), np.sin(ang)
    K[:, J_RST:J_RST + TA] = np.arange(TA) % 64 != 0
    ang = 2 * np.pi * ((i[:, None] * i[None]) % P) / P
    K[:, J_DFT:J_DFT + P] = np.cos(ang) / 256
    K[:, J_DFT + P:J_DFT + 2 * P] = -np.sin(ang) / 256
    return K


def chunks(w, width=P):
    *lead, r, c = w.shape
    w = w.reshape(*lead, r // P, P, c // width, width)
    n = len(lead)
    return np.ascontiguousarray(w.transpose(*range(n), n + 2, n + 1, n, n + 3))


def cols(v):
    return np.ascontiguousarray(np.swapaxes(v.reshape(*v.shape[:-1], -1, P), -1, -2))


def feats(x):
    return np.ascontiguousarray(x.T.reshape(-1, P, x.shape[0]).transpose(1, 0, 2))


def layout(i):
    a = {}
    w = i["w_in"]
    o = np.cumsum([0, 512, 512, 512, 256, 64, 4, 256, 256, 256, 256, 256, 256, 256, 256, 4, 4])
    aq, ak, av, iq, ik, iw, rq, rk, rv, rg, mq, mk, mv, mo, mi, mf = (w[:, :, o[j]:o[j + 1]] for j in range(16))
    gates = np.zeros((DEPTH, D, P), np.float32)
    gates[:, :, 0:4], gates[:, :, 32:36] = mi, mf
    a["w_in_t"] = chunks(np.concatenate([aq, ak, iq, ik, ik, rq, rk, rg, mq, mk, mo, gates], axis=2))
    a["w_in_v"] = chunks(np.concatenate([av, rv, mv], axis=2), 512)
    a["w_in_i"] = chunks(iw, NH_I)[:, 0]
    a["w_ada"] = chunks(i["w_ada"], 512)
    a["b_ada"] = cols(i["b_ada"])
    cw = np.concatenate([i["conv_w"], i["conv_b"][:, None]], axis=1)
    a["conv"] = np.ascontiguousarray(cw.reshape(DEPTH, CONV + 1, 4, P).transpose(0, 3, 2, 1))
    a["gate_b"] = np.ascontiguousarray(np.stack([i["i_bias"], i["f_bias"]], axis=2))
    a["w_out"] = chunks(i["w_out"])
    for n in ("mix", "ffn"):
        a["ln_" + n] = np.ascontiguousarray(np.stack([cols(i[f"ln_{n}_g"]), cols(i[f"ln_{n}_b"])], axis=2))
    a["w_router"] = chunks(i["w_router"], NE)[0]
    a["b_router"] = i["b_router"]
    a["w_gate"] = chunks(i["w_gate"]).reshape(DEPTH, NE * 2, P, KD, P)
    a["w_up"] = chunks(i["w_up"]).reshape(DEPTH, NE * 2, P, KD, P)
    wd = chunks(i["w_down"].reshape(DEPTH, NE * FE, D))
    a["w_down"] = np.ascontiguousarray(
        wd.reshape(DEPTH, KD, P, 4, 8, P).transpose(0, 1, 3, 2, 4, 5)).reshape(DEPTH, KD * 4, P, 8, P)
    sel = np.zeros((NE, NE, P), np.float32)
    sel[np.arange(NE), np.arange(NE)] = 1.0
    a["sel_e"] = sel
    a["consts"] = consts()
    a["positions"] = i["positions"][0]
    a["cond"] = np.ascontiguousarray(np.stack([cols(i["c"][0]), cols(i["c_2"][0]), cols(i["c_ctx_2"])], axis=1))
    a["x"] = feats(i["x"][0])
    a["ctx"] = feats(i["ctx_2"][0])
    a["ada_w2"], a["ada_b2"] = chunks(i["ada_w_2"], 512), cols(i["ada_b_2"])
    a["norm_mix"], a["norm_ffn"] = cols(i["norm_mix_w_2"]), cols(i["norm_ffn_w_2"])
    a["final_w"] = cols(i["final_norm_w_2"])
    u, v, q, k, nv = np.split(i["ab_w_in_2"][0], 5, axis=1)
    a["ab_t"] = chunks(np.concatenate([u, q, k], axis=1))
    a["ab_v"] = chunks(np.concatenate([v, nv], axis=1), 512)
    a["ab_out"] = chunks(i["ab_w_out_2"][0])
    a["sgu_w"] = np.ascontiguousarray(i["ab_sgu_w_2"][0].transpose(2, 0, 1))
    a["sgu_b"] = np.ascontiguousarray(i["ab_sgu_b_2"][0].reshape(-1))
    a["sgu_nw"] = cols(i["ab_sgu_norm_w_2"][0])
    c = np.arange(64)
    start = np.clip(c - 8, 0, 48)
    seen = (c[None] >= start[:, None]) & (c[None] < start[:, None] + 16)
    rel = i["ab_rel_bias_2"][0][:, :, np.clip(c[None] - c[:, None] + 15, 0, 30)]
    rel = np.where(seen, rel, np.float32(NEG)).transpose(2, 0, 1, 3)
    a["rel"] = np.zeros((P, 8, 16, 64), np.float32)
    a["rel"][0:64, :, 0:15] = rel
    a["rel"][64:, :, 1:16] = rel
    a["rel"] = a["rel"].reshape(P, 8, 1024)
    w = i["cd_w_in_2"][0]
    f, q, k, v, g, al = np.split(w, np.cumsum([512, 256, 256, 512, 512]), axis=1)
    a["cd_t"] = chunks(np.concatenate([f, q, g], axis=1))
    low = np.zeros((D, P), np.float32)
    low[:, 0:16], low[:, 32:48] = al[:, 0:16], al[:, 16:32]
    a["cd_k"] = chunks(np.concatenate([k, low], axis=1))
    a["cd_v"] = chunks(v, 512)
    a["cd_out"] = chunks(i["cd_w_out_2"][0])
    a["dec_w"] = np.ascontiguousarray(np.stack([i["cd_decay_w_fwd_2"][0], i["cd_decay_w_bwd_2"][0]]))
    a["dec_b"] = cols(np.concatenate([i["cd_decay_b_fwd_2"][0], i["cd_decay_b_bwd_2"][0]]))
    a["head_w"] = np.ascontiguousarray(i["cd_head_norm_w_2"].reshape(P, 1))
    a["f_gate"], a["f_up"] = chunks(i["ffn_w_gate_2"]), chunks(i["ffn_w_up_2"])
    fd = chunks(i["ffn_w_down_2"])
    a["f_down"] = np.ascontiguousarray(
        fd.reshape(DEPTH, KD, P, 2, 11, P).transpose(0, 1, 3, 2, 4, 5)).reshape(DEPTH, KD * 2, P, 11, P)
    a["consts2"] = consts2()
    ang = 2 * np.pi * ((np.arange(T)[:, None] * np.arange(T)[None]) % T) / T
    dft = np.stack([np.cos(ang), np.sin(ang)]).astype(np.float32)
    a["dft_t"] = np.ascontiguousarray(dft.reshape(2, TT, P, T).transpose(2, 0, 1, 3))
    return a


def kernel(**inputs):
    import concourse.bacc as bacc
    from concourse.bass_utils import run_bass_kernel_spmd as run

    arrays = layout({k: np.asarray(v) for k, v in inputs.items()})
    nc = bacc.Bacc("TRN2", target_bir_lowering=False, num_devices=1)
    A = {n: nc.dram_tensor("in_" + n, a.shape, mybir.dt.from_np(a.dtype), kind="ExternalInput").ap()
                           for n, a in arrays.items()}
    out = nc.dram_tensor("out_x", (P, KD, T), F32, kind="ExternalOutput").ap()
    program(nc, A, out)
    r = run(nc, [{"in_" + n: a for n, a in arrays.items()}], core_ids=[0])
    y = r.results[0]["out_x"]
    return np.ascontiguousarray(y.transpose(2, 1, 0)).reshape(1, T, D)
```

```python
import math
from contextlib import ExitStack

import numpy as np
import concourse.bass as bass
from concourse import mybir

F32 = mybir.dt.float32
I32 = mybir.dt.int32
F32R = mybir.dt.float32r
ALU = mybir.AluOpType
ACT = mybir.ActivationFunctionType
AX = mybir.AxisListType

P = 128
D = 1024
KD = D // P
T = 512
TT = T // P
TC = 256
TA = T + TC
DEPTH = 2
HD = 64
HALF = HD // 2
NH_A, NH_I, NH_R, NH_M = 8, 4, 4, 4
TOPK = 128
CONV = 4
NE, NG, EPG, FE = 16, 4, 4, 256
EPS = 1e-5
RMS_EPS = 1e-6
ALPHA = (2.0 * DEPTH) ** 0.25
NEG = -1.0e30
MAGIC = 12582912.0
TWO_PI = (6.28125, 0.0019350051879882812, 3.019915981956753e-07)
PI_IN = 3.1415925

C_AQ, C_AK, C_IQ, C_IK, C_RQ, C_RK, C_RG, C_MQ, C_MK, C_MO, C_G = 0, 4, 8, 10, 11, 13, 15, 17, 19, 21, 23
N_ROPE = 15
N_CH = 24
N_MOD = 6 * KD
N_V = 1024
V_A, V_R, V_M = 0, 512, 768

K_ID, K_ROT, K_ONE, K_MEAN = (P * i for i in range(4))
K_RANK = 4 * P
K_FREQ = K_RANK + NE + NG
K_N = K_FREQ + 1

L_HEAD = NH_R * T
L_UP = L_HEAD + P
L_SELH = L_UP + P
L_SELP = L_SELH + NH_M * P
L_N = L_SELP + NH_M // 2 * P

J_ROT, J_MASK, J_COS, J_SIN, J_RST = 0, P, 3 * P, 3 * P + T, 3 * P + 2 * T
J_DFT = J_RST + TA
J_N = J_DFT + 2 * P
FFN = 2816


class Buffers:
    pass


class Item:

    def __init__(self, q, segs, vs, o):
        self.q, self.segs, self.vs, self.o = q, segs, vs, o


class Steps:

    def __init__(self, eng, sem):
        self.eng, self.sem, self.n = eng, sem, 0

    def __call__(self, ins):
        ins.then_inc(self.sem, 1)
        self.n += 1
        self.eng.wait_ge(self.sem, self.n)


def take(M, names):
    M.blocks += 1
    return {n: M.nc.alloc_semaphore(f"b{M.blocks}_{n}") for n in names.split()}


def give(nc, s):
    nc.clear_and_free_semaphores(list(s.values()))
    nc.all_engine_barrier()


def setup(nc, M, A):
    s = take(M, "loaded stream step table sines kept")
    with ExitStack() as ctx:
        pi = ctx.enter_context(M.nc.sbuf_tensor(f"{M.blocks}_pos_int", [P, T], I32))
        ang = ctx.enter_context(M.nc.sbuf_tensor(f"{M.blocks}_angle", [P, T], F32))
        turns = ctx.enter_context(M.nc.sbuf_tensor(f"{M.blocks}_turns", [P, T], F32))
        r = ctx.enter_context(M.nc.sbuf_tensor(f"{M.blocks}_reduced", [P, 2, T], F32))
        block = ctx.enter_context(nc.Block())

        @block.sync
        def _(sp):
            sp.dma_start(M.K[:], A["consts"]).then_inc(s["loaded"], 16)
            sp.dma_start(pi[:], A["positions"].partition_broadcast(P)).then_inc(s["loaded"], 16)
            sp.dma_start(M.xT[:, :, 0:T], A["x"]).then_inc(s["stream"], 16)
            sp.dma_start(M.xT[:, :, T:TA], A["ctx"]).then_inc(s["stream"], 16)
            sp.wait_ge(s["stream"], 32)
            sp.wait_ge(s["sines"], 2)
            sp.dma_start(M.rope, r[:]).then_inc(s["kept"], 16)
            sp.wait_ge(s["kept"], 16)

        @block.vector
        def _(dve):
            step = Steps(dve, s["step"])
            dve.wait_ge(s["loaded"], 32)
            step(nc.vector.tensor_copy(r[:, 0, :], pi[:]))
            step(nc.vector.tensor_scalar(ang[:], r[:, 0, :], M.K[:, K_FREQ:K_FREQ + 1], None, ALU.mult))
            for j, quarter in enumerate((0.25, 0.0)):
                step(nc.vector.tensor_scalar(turns[:], ang[:], float(1 / (2 * math.pi)), quarter, ALU.mult, ALU.add))
                step(nc.vector.tensor_scalar(turns[:], turns[:], MAGIC, None, ALU.add))
                step(nc.vector.tensor_scalar(turns[:], turns[:], -MAGIC, None, ALU.add))
                src = ang[:]
                for c in TWO_PI:
                    step(nc.vector.scalar_tensor_tensor(out=r[:, j, :], in0=turns[:], scalar=-c, in1=src,
                                                        op0=ALU.mult, op1=ALU.add))
                    src = r[:, j, :]
                if quarter:
                    step(nc.vector.tensor_scalar(r[:, j, :], r[:, j, :], math.pi / 2, None, ALU.add))
                step(nc.vector.tensor_scalar(r[:, j, :], r[:, j, :], -PI_IN, PI_IN, ALU.max, ALU.min))
            nc.vector.tensor_scalar(r[:, 0, :], r[:, 0, :], 1.0, None, ALU.mult).then_inc(s["table"], 1)

        @block.scalar
        def _(act):
            act.wait_ge(s["table"], 1)
            nc.scalar.activation(r[:, 0, :], r[:, 0, :], ACT.Sin).then_inc(s["sines"], 1)
            nc.scalar.activation(r[:, 1, :], r[:, 1, :], ACT.Sin).then_inc(s["sines"], 1)
    give(nc, s)


def ada(nc, M, A):
    s = take(M, "r0 r1 bias_in cond_in sig summed added")
    NB = 4
    with ExitStack() as ctx:
        R = Modulation(nc, M, ctx, s, modulation(A, 0, NB), A["b_ada"][0], A["cond"][0], 0, NB, 1)
        block = ctx.enter_context(nc.Block())
        PAIRS = N_MOD // NB // 2

        @block.sync
        def _(sp):
            R.load_first(sp)
            R.load(sp)
            with sp.Fori(1, PAIRS) as i:
                for u in range(2):
                    R.load_next(sp, i, u)

        @block.scalar
        def _(act):
            R.sigmoid(act)

        @block.vector
        def _(dve):
            R.conditions(dve)
            with dve.Fori(0, PAIRS) as i:
                for u in range(2):
                    R.chunks(dve, i, u)
    give(nc, s)


def modulation(A, layer, n):
    def w(c):
        return A["w_ada"][bass.ds(c + layer * N_MOD, n)].rearrange("c p k -> p c k")
    return w


def modcol(M, part, k, c=0):
    j = (part * KD + k) * 2 + c
    return M.mod[:, j:j + 1]


def halves(t):
    return t[:, 0], t[:, 1]


def product(nc, out, w, x, first, last):
    nc.tensor.matmul(out, w[0], x[0], start=first, stop=False)
    nc.tensor.matmul(out, w[0], x[1], start=False, stop=False)
    return nc.tensor.matmul(out, w[1], x[0], start=False, stop=last)


STREAM = "w0 w1 used high_done split_done "


class Stream:

    def __init__(self, nc, M, ctx, s, w, N, KP):
        self.nc, self.s, self.w, self.N, self.KP = nc, s, w, N, KP
        self.raw = ctx.enter_context(nc.sbuf_tensor(f"{M.blocks}_w_raw", [P, 2, KP, P], F32))
        self.part = ctx.enter_context(nc.sbuf_tensor(f"{M.blocks}_w_part", [P, 2, 2, KP, P], F32R))
        self.ready = (s["w0"], s["w1"])
        self.pairs = N // 2

    def load(self, sp):
        for u in range(2):
            sp.dma_start(self.raw[:, u], self.w(u)).then_inc(self.ready[u], 16)

    def load_rest(self, sp):
        if self.pairs > 1:
            with sp.Fori(1, self.pairs) as i:
                for u in range(2):
                    sp.wait_ge(self.s["split_done"], 2 * i + u - 1)
                    sp.dma_start(self.raw[:, u], self.w(2 * i + u)).then_inc(self.ready[u], 16)
        if self.N % 2:
            sp.wait_ge(self.s["split_done"], self.N - 2)
            sp.dma_start(self.raw[:, 0], self.w(self.N - 1)).then_inc(self.ready[0], 16)

    def high(self, act, n, u, loads):
        act.wait_ge(self.ready[u], 16 * loads)
        act.wait_ge(self.s["used"], n + 1)
        self.nc.scalar.activation(self.part[:, u, 0], self.raw[:, u], ACT.Copy).then_inc(self.s["high_done"], 1)

    def highs(self, act, out):
        self.high(act, 0, 0, 1)
        whole = self.pairs if self.N % 2 else self.pairs - 1
        if whole:
            with act.Fori(0, whole) as i:
                self.high(act, 2 * i + 1, 1, i + 1)
                out(2 * i, 0)
                self.high(act, 2 * i + 2, 0, i + 2)
                out(2 * i + 1, 1)
        if self.N % 2:
            out(self.N - 1, 0)
        else:
            self.high(act, self.N - 1, 1, self.pairs)
            out(self.N - 2, 0)
            out(self.N - 1, 1)

    def lows(self, pool, also=None):
        def low(n, u):
            pool.wait_ge(self.s["high_done"], n + 1)
            self.nc.gpsimd.tensor_tensor(self.part[:, u, 1], self.raw[:, u], self.part[:, u, 0].bitcast(F32),
                                         ALU.subtract).then_inc(self.s["split_done"], 1)

        low(0, 0)
        low(1, 1)
        if self.pairs > 1:
            with pool.Fori(1, self.pairs) as i:
                for u in range(2):
                    low(2 * i + u, u)
                    if also:
                        also(pool, i, u)
        if self.N % 2:
            low(self.N - 1, 0)

    def multiply(self, pe, chunk, after=None, n_after=0, between=None):
        pe.sem_inc(self.s["used"], 2)

        def one(n, u):
            pe.wait_ge(self.s["split_done"], n + 1)
            chunk(n, u, halves(self.part[:, u])).then_inc(self.s["used"], 1)

        def loop(a, z, tail):
            with pe.Fori(a, z) as i:
                for u in range(2):
                    one(2 * i + u, u)
                    if between:
                        between(i, u)
                if tail:
                    tail(i)

        if n_after:
            loop(0, n_after, after)
        if n_after < self.pairs:
            loop(n_after, self.pairs, None)
        if self.N % 2:
            one(self.N - 1, 0)


def at(t, n, *rest):
    return t[(slice(None), bass.ds(n, 1)) + rest]


def split_rows(nc, s, dst, k, src, eng):
    eng.wait_ge(s["h_high"], k + 1)
    nc.vector.tensor_tensor(dst[:, 1, k], src, dst[:, 0, k].bitcast(F32), ALU.subtract).then_inc(s["h_done"], 1)


def proj1(nc, M, A, l, B):
    s = take(M, STREAM + "h_f32 h_high h_done psum_free raw_done rot_done t1 t2 turned wv wi "
             "tok_done tok_free rope_in")
    with ExitStack() as ctx:
        h, hp = M.hT, M.hR
        S = Stream(nc, M, ctx, s, lambda n: A["w_in_t"][l, n], N_CH, KD)
        WV = ctx.enter_context(nc.sbuf_tensor(f"{M.blocks}_proj_wv", [P, KD, 512], F32))
        rope = ctx.enter_context(nc.sbuf_tensor(f"{M.blocks}_rope", [P, 2, T], F32))
        WI = ctx.enter_context(nc.sbuf_tensor(f"{M.blocks}_proj_wi", [P, KD, NH_I], F32))
        t1 = ctx.enter_context(nc.sbuf_tensor(f"{M.blocks}_rope_cos", [P, 2, T], F32))
        t2 = ctx.enter_context(nc.sbuf_tensor(f"{M.blocks}_rope_sin", [P, 2, T], F32))
        block = ctx.enter_context(nc.Block())
        PAIRS = (N_ROPE + 1) // 2

        @block.sync
        def _(sp):
            S.load(sp)
            sp.dma_start(WV[:], A["w_in_v"][l, 0]).then_inc(s["wv"], 16)
            sp.dma_start(WI[:], A["w_in_i"][l]).then_inc(s["wi"], 16)
            sp.dma_start(rope[:], M.rope).then_inc(s["rope_in"], 16)
            S.load_rest(sp)
            sp.wait_ge(s["tok_done"], TT)
            sp.dma_start(WV[:], A["w_in_v"][l, 1]).then_inc(s["wv"], 16)

        @block.tensor
        def _(pe):
            def chunk(n, u, w):
                pe.wait_ge(s["psum_free"], n + 1)
                for k in range(KD):
                    mm = product(nc, M.PS[:, u, :], (w[0][:, k], w[1][:, k]), (hp[:, 0, k], hp[:, 1, k]),
                                 k == 0, k == KD - 1)
                return mm

            def rotate(i):
                for u in range(2):
                    pe.wait_ge(s["raw_done"], 2 * i + u + 1)
                    pe.wait_ge(s["turned"], 2 * i + u + 1)
                    nc.tensor.matmul(M.PS[:, 2 + u, :], M.K[:, K_ROT:K_ROT + P], at(B.PT, 2 * i + u, slice(None)),
                                     start=True, stop=True).then_inc(s["rot_done"], 1)

            def values(g):
                pe.wait_ge(s["wv"], 16 * (g + 1))
                for t in range(TT):
                    n = g * TT + t
                    if n >= 2:
                        pe.wait_ge(s["tok_free"], n - 1)
                    for k in range(KD):
                        mm = nc.tensor.matmul(M.PS[:, 4 + n % 2, :], h[:, k, t * P:(t + 1) * P], WV[:, k, :],
                                              start=(k == 0), stop=(k == KD - 1))
                    mm.then_inc(s["tok_done"], 1)

            pe.wait_ge(s["h_done"], KD)
            S.multiply(pe, chunk, rotate, PAIRS)
            values(0)
            pe.wait_ge(s["wi"], 16)
            for t in range(TT):
                for k in range(KD):
                    mm = nc.tensor.matmul(M.PS[:, 6, t * NH_I:(t + 1) * NH_I], h[:, k, t * P:(t + 1) * P],
                                          WI[:, k, :], start=(k == 0), stop=(k == KD - 1))
            values(1)

        @block.gpsimd
        def _(pool):
            S.lows(pool)

        @block.scalar
        def _(act):
            act.sem_inc(s["psum_free"], 2)
            for k in range(KD):
                nc.scalar.activation(h[:, k, :], M.xT[:, k, 0:T], ACT.Identity,
                                     bias=modcol(M, 0, k), scale=modcol(M, 1, k)).then_inc(s["h_f32"], 1)
            for k in range(KD):
                act.wait_ge(s["h_f32"], k + 1)
                nc.scalar.activation(hp[:, 0, k], h[:, k, :], ACT.Copy).then_inc(s["h_high"], 1)

            def copy(n, u):
                act.wait_ge(s["used"], n + 3)
                nc.scalar.activation(at(B.PT, n, slice(None)), M.PS[:, u, :], ACT.Copy).then_inc(s["raw_done"], 1)
                act.wait_ge(s["raw_done"], n + 1)
                act.sem_inc(s["psum_free"], 1)

            S.highs(act, copy)
            for n in range(2 * TT):
                g, t = n // TT, n % TT
                act.wait_ge(s["tok_done"], n + 1)
                nc.scalar.activation(B.V[:, t, g * 512:(g + 1) * 512], M.PS[:, 4 + n % 2, :],
                                     ACT.Copy).then_inc(s["tok_free"], 1)
            nc.scalar.activation(B.iw[:], M.PS[:, 6, 0:TT * NH_I], ACT.Copy, scale=NH_I ** -0.5 * HD ** -0.5)

        @block.vector
        def _(dve):
            dve.sem_inc(s["turned"], 2)
            for k in range(KD):
                split_rows(nc, s, hp, k, h[:, k, :], dve)

            dve.wait_ge(s["rope_in"], 16)

            def turn(n, u):
                x = at(B.PT, n, slice(None))
                dve.wait_ge(s["rot_done"], n + 1)
                nc.vector.tensor_tensor(t1[:, u:u + 1], x, rope[:, 0:1],
                                        ALU.mult).then_inc(s["t1"], 1)
                nc.vector.tensor_tensor(t2[:, u], M.PS[:, 2 + u, :], rope[:, 1], ALU.mult).then_inc(s["t2"], 1)
                dve.wait_ge(s["t1"], n + 1)
                dve.wait_ge(s["t2"], n + 1)
                nc.vector.tensor_tensor(x, t1[:, u:u + 1], t2[:, u:u + 1], ALU.add).then_inc(s["turned"], 1)

            with dve.Fori(0, N_ROPE // 2) as i:
                for u in range(2):
                    turn(2 * i + u, u)
            turn(N_ROPE - 1, 0)
            dve.wait_ge(s["rot_done"], N_ROPE + 1)
    give(nc, s)


def convolve(nc, M, A, l, B):
    s = take(M, "par step conv gates sig act_step ab_done tr cp dec_in")
    rows = NH_M
    with ExitStack() as ctx:
        cw = ctx.enter_context(M.nc.sbuf_tensor(f"{M.blocks}_conv_w", [P, 4, CONV + 1], F32))
        gb = ctx.enter_context(M.nc.sbuf_tensor(f"{M.blocks}_gate_b", [rows, 2], F32))
        acc = ctx.enter_context(M.nc.sbuf_tensor(f"{M.blocks}_conv_acc", [P, 4, T], F32))
        z = ctx.enter_context(M.nc.sbuf_tensor(f"{M.blocks}_f_pre", [rows, T], F32))
        e = ctx.enter_context(M.nc.sbuf_tensor(f"{M.blocks}_f_exp", [rows, T], F32))
        lf = ctx.enter_context(M.nc.sbuf_tensor(f"{M.blocks}_log_f", [rows, T], F32))
        one = ctx.enter_context(M.nc.sbuf_tensor(f"{M.blocks}_one_row", [rows, T], F32))
        bs = ctx.enter_context(M.nc.sbuf_tensor(f"{M.blocks}_f_sum", [rows, T], F32))
        a = ctx.enter_context(M.nc.sbuf_tensor(f"{M.blocks}_i_rel", [rows, T], F32))
        am = ctx.enter_context(M.nc.sbuf_tensor(f"{M.blocks}_i_max", [rows, T], F32))
        th = ctx.enter_context(M.nc.sbuf_tensor(f"{M.blocks}_floor", [rows, T], F32))
        block = ctx.enter_context(nc.Block())

        @block.sync
        def _(sp):
            sp.dma_start(cw[:], A["conv"][l]).then_inc(s["par"], 16)
            sp.dma_start(gb[:], A["gate_b"][l]).then_inc(s["par"], 16)
            sp.dma_start(B.L[:], A["mixer_consts"]).then_inc(s["dec_in"], 16)
            sp.wait_ge(s["dec_in"], 16)

        @block.vector
        def _(dve):
            step = Steps(dve, s["step"])
            dve.wait_ge(s["par"], 32)
            step(nc.vector.tensor_scalar(z[:], B.PT[32:32 + rows, C_G, :], gb[:, 1:2], None, ALU.add))
            nc.vector.scalar_tensor_tensor(out=lf[:], in0=z[:], scalar=-1.0, in1=z[:], op0=ALU.mult,
                                           op1=ALU.max).then_inc(s["gates"], 1)
            step(nc.vector.memset(one[:], 1.0))
            for c in range(4):
                x = B.PT[:, C_MQ + c, :]
                step(nc.vector.tensor_scalar(acc[:, c, :], x, cw[:, c, CONV - 1:CONV], cw[:, c, CONV:CONV + 1],
                                             ALU.mult, ALU.add))
                for back in range(1, CONV):
                    ins = nc.vector.scalar_tensor_tensor(
                        out=acc[:, c, back:T], in0=x[:, 0:T - back], scalar=cw[:, c, CONV - 1 - back:CONV - back],
                        in1=acc[:, c, back:T], op0=ALU.mult, op1=ALU.add)
                    if back < CONV - 1:
                        step(ins)
                    else:
                        ins.then_inc(s["conv"], 1)
            dve.wait_ge(s["sig"], 1)
            step(nc.vector.scalar_tensor_tensor(out=lf[:], in0=z[:], scalar=0.0, in1=e[:], op0=ALU.min,
                                                op1=ALU.subtract))
            step(nc.vector.tensor_tensor_scan(out=bs[:], data0=one[:], data1=lf[:], initial=0.0,
                                              op0=ALU.mult, op1=ALU.add))
            step(nc.vector.scalar_tensor_tensor(out=a[:], in0=B.PT[0:rows, C_G, :], scalar=gb[:, 0:1], in1=bs[:],
                                                op0=ALU.add, op1=ALU.subtract))
            step(nc.vector.tensor_tensor_scan(out=am[:], data0=a[:], data1=a[:], initial=0.0,
                                              op0=ALU.max, op1=ALU.max))
            step(nc.vector.tensor_tensor(th[:], bs[:], am[:], ALU.add))
            nc.vector.tensor_scalar(th[:], th[:], -1.0, 80.0, ALU.mult, ALU.min).then_inc(s["ab_done"], 1)

        @block.scalar
        def _(act):
            act.wait_ge(s["gates"], 1)
            nc.scalar.activation(e[:], lf[:], ACT.Exp, scale=-1.0).then_inc(s["act_step"], 1)
            act.wait_ge(s["act_step"], 1)
            nc.scalar.activation(e[:], e[:], ACT.Ln, bias=1.0).then_inc(s["sig"], 1)
            for c in range(2):
                nc.scalar.activation(B.PT[:, C_MO + c, :], B.PT[:, C_MO + c, :], ACT.Sigmoid)
            for c in range(2):
                nc.scalar.activation(B.PT[:, C_RG + c, :], B.PT[:, C_RG + c, :], ACT.Silu)
            for c in range(4):
                act.wait_ge(s["conv"], c + 1)
                nc.scalar.activation(B.PT[:, C_MQ + c, :], acc[:, c, :], ACT.Silu)
            act.wait_ge(s["ab_done"], 1)
            nc.scalar.activation(th[:], th[:], ACT.Exp).then_inc(s["act_step"], 1)
            for h in range(NH_M):
                act.wait_ge(s["tr"], h + 1)
                nc.scalar.activation(B.Amax[:, h, :], M.PS[:, h, :], ACT.Copy).then_inc(s["cp"], 1)
            for p in range(NH_M // 2):
                act.wait_ge(s["tr"], NH_M + p + 1)
                nc.scalar.activation(B.floor[:, p, :], M.PS[:, NH_M + p, :], ACT.Copy).then_inc(s["cp"], 1)
            act.wait_ge(s["tr"], NH_M + NH_M // 2 + 1)
            nc.scalar.activation(B.acol[:], M.PS[:, 6, 0:TT * NH_M], ACT.Copy).then_inc(s["cp"], 1)

        @block.tensor
        def _(pe):
            pe.wait_ge(s["dec_in"], 16)
            pe.wait_ge(s["ab_done"], 1)
            for h in range(NH_M):
                nc.tensor.matmul(M.PS[:, h, :], B.L[0:rows, L_SELH + h * P:L_SELH + (h + 1) * P], am[:],
                                 start=True, stop=True).then_inc(s["tr"], 1)
            pe.wait_ge(s["act_step"], 2)
            for p in range(NH_M // 2):
                nc.tensor.matmul(M.PS[:, NH_M + p, :], B.L[0:rows, L_SELP + p * P:L_SELP + (p + 1) * P], th[:],
                                 start=True, stop=True).then_inc(s["tr"], 1)
            for t in range(TT):
                mm = nc.tensor.transpose(M.PS[:, 6, t * NH_M:(t + 1) * NH_M], a[:, t * P:(t + 1) * P],
                                         M.K[0:rows, K_ID:K_ID + rows])
            mm.then_inc(s["tr"], 1)
    give(nc, s)


def select_keys(nc, M, B):
    s = take(M, "scored used step")
    N = TT * NH_I
    with ExitStack() as ctx:
        sc = ctx.enter_context(M.nc.sbuf_tensor(f"{M.blocks}_score", [P, T], F32))
        tmp = ctx.enter_context(M.nc.sbuf_tensor(f"{M.blocks}_score_h", [P, T], F32))
        work = ctx.enter_context(M.nc.sbuf_tensor(f"{M.blocks}_score_left", [P, T], F32))
        best = ctx.enter_context(M.nc.sbuf_tensor(f"{M.blocks}_best8", [P, 8], F32))
        block = ctx.enter_context(nc.Block())

        @block.tensor
        def _(pe):
            for n in range(N):
                t, h = n // NH_I, n % NH_I
                w, b = P * (t + 1), HD * (h % 2)
                if n >= 4:
                    pe.wait_ge(s["used"], n - 3)
                nc.tensor.matmul(M.PS[:, n % 4, 0:w], B.PT[b:b + HD, C_IQ + h // 2, t * P:(t + 1) * P],
                                 B.PT[b:b + HD, C_IK, 0:w], start=True, stop=True).then_inc(s["scored"], 1)

        @block.vector
        def _(dve):
            step = Steps(dve, s["step"])
            for t in range(TT):
                w = P * (t + 1)
                for h in range(NH_I):
                    n = t * NH_I + h
                    dve.wait_ge(s["scored"], n + 1)
                    out = tmp if h else sc
                    nc.vector.tensor_scalar(out[:, 0:w], M.PS[:, n % 4, 0:w], 0.0, B.iw[:, n:n + 1],
                                            ALU.max, ALU.mult).then_inc(s["used"], 1)
                    if h:
                        dve.wait_ge(s["used"], n + 1)
                        step(nc.vector.tensor_tensor(sc[:, 0:w], sc[:, 0:w], tmp[:, 0:w], ALU.add))
                if t == 0:
                    step(nc.vector.memset(B.bias[:, 0, 0:w], 0.0))
                    step(nc.vector.memset(B.bias[0:64, 0, 64:w], NEG))
                    continue
                step(nc.vector.memset(sc[0:64, w - 64:w], -3.0e38))
                src = sc
                for r in range(TOPK // 8):
                    step(nc.vector.max(best[:], src[:, 0:w]))
                    step(nc.vector.match_replace(work[:, 0:w], best[:], src[:, 0:w], -1.0e38))
                    src = work
                step(nc.vector.tensor_tensor(tmp[:, 0:w], work[:, 0:w], sc[:, 0:w], ALU.is_equal))
                step(nc.vector.tensor_scalar(B.bias[:, t, 0:w], tmp[:, 0:w], NEG, None, ALU.mult))
    give(nc, s)


def attend(nc, M, items, scale):
    s = take(M, "s_done sm_done nm_done exp_done p_done t_done pt_done pv_done o_done step")
    N = len(items)
    WM = max(sum(w for _, w, _ in it.segs) for it in items)
    with ExitStack() as ctx:
        sm = ctx.enter_context(M.nc.sbuf_tensor(f"{M.blocks}_att_s", [P, 2, WM], F32))
        pr = ctx.enter_context(M.nc.sbuf_tensor(f"{M.blocks}_att_p", [P, 2, WM], F32))
        pt = ctx.enter_context(M.nc.sbuf_tensor(f"{M.blocks}_att_pT", [P, 2, WM], F32))
        mx = ctx.enter_context(M.nc.sbuf_tensor(f"{M.blocks}_att_max", [P, N], F32))
        nm = ctx.enter_context(M.nc.sbuf_tensor(f"{M.blocks}_att_nmax", [P, N], F32))
        su = ctx.enter_context(M.nc.sbuf_tensor(f"{M.blocks}_att_sum", [P, N], F32))
        ri = ctx.enter_context(M.nc.sbuf_tensor(f"{M.blocks}_att_rsum", [P, N], F32))
        block = ctx.enter_context(nc.Block())

        def width(n):
            return sum(w for _, w, _ in items[n].segs)

        @block.tensor
        def _(pe):
            def scores(n):
                if n >= 2:
                    pe.wait_ge(s["sm_done"], n - 1)
                for j, (k, w, _) in enumerate(items[n].segs):
                    mm = nc.tensor.matmul(M.PS[:, 2 * (n % 2) + j, 0:w], items[n].q, k, start=True, stop=True)
                mm.then_inc(s["s_done"], 1)

            def turn(n):
                pe.wait_ge(s["p_done"], n + 1)
                if n >= 1:
                    pe.wait_ge(s["pt_done"], n)
                for b in range(width(n) // P):
                    mm = nc.tensor.transpose(M.PS[:, 4 + b // 4, (b % 4) * P:(b % 4 + 1) * P],
                                             pr[:, n % 2, b * P:(b + 1) * P], M.K[:, K_ID:K_ID + P])
                mm.then_inc(s["t_done"], 1)

            def values(n):
                pe.wait_ge(s["pt_done"], n + 1)
                m, c = n // 2, HD * (n % 2)
                if m >= 2:
                    pe.wait_ge(s["o_done"], m - 1)
                B_ = width(n) // P
                for b in range(B_):
                    mm = nc.tensor.matmul(M.PS[c:c + HD, 6 + m % 2, 0:P], items[n].vs[b],
                                          pt[:, n % 2, b * P:(b + 1) * P], start=(b == 0), stop=(b == B_ - 1))
                mm.then_inc(s["pv_done"], 1)

            scores(0)
            for n in range(N + 2):
                if n + 1 < N:
                    scores(n + 1)
                if 1 <= n <= N:
                    turn(n - 1)
                if n >= 2:
                    values(n - 2)

        @block.vector
        def _(dve):
            step = Steps(dve, s["step"])

            def front(n):
                dve.wait_ge(s["s_done"], n + 1)
                if n >= 2:
                    dve.wait_ge(s["exp_done"], n - 1)
                at = 0
                for j, (_, w, bias) in enumerate(items[n].segs):
                    src, out = M.PS[:, 2 * (n % 2) + j, 0:w], sm[:, n % 2, at:at + w]
                    if bias is None:
                        ins = nc.vector.tensor_scalar(out, src, scale, None, ALU.mult)
                    else:
                        ins = nc.vector.scalar_tensor_tensor(out=out, in0=src, scalar=scale, in1=bias,
                                                             op0=ALU.mult, op1=ALU.add)
                    at += w
                    if j < len(items[n].segs) - 1:
                        step(ins)
                ins.then_inc(s["sm_done"], 1)
                dve.wait_ge(s["sm_done"], n + 1)
                step(nc.vector.tensor_reduce(mx[:, n:n + 1], sm[:, n % 2, 0:at], AX.X, ALU.max))
                nc.vector.tensor_scalar(nm[:, n:n + 1], mx[:, n:n + 1], -1.0, None, ALU.mult).then_inc(s["nm_done"], 1)

            def back(n):
                dve.wait_ge(s["exp_done"], n + 1)
                step(nc.vector.reciprocal(ri[:, n:n + 1], su[:, n:n + 1]))
                w = width(n)
                nc.vector.tensor_scalar(pr[:, n % 2, 0:w], pr[:, n % 2, 0:w], ri[:, n:n + 1], None,
                                        ALU.mult).then_inc(s["p_done"], 1)

            for n in range(N + 1):
                if n < N:
                    front(n)
                if n >= 1:
                    back(n - 1)

        @block.scalar
        def _(act):
            def exps(n):
                act.wait_ge(s["nm_done"], n + 1)
                if n >= 2:
                    act.wait_ge(s["t_done"], n - 1)
                w = width(n)
                nc.scalar.activation(pr[:, n % 2, 0:w], sm[:, n % 2, 0:w], ACT.Exp, bias=nm[:, n:n + 1],
                                     accum_out=su[:, n:n + 1]).then_inc(s["exp_done"], 1)

            def copy_turned(n):
                act.wait_ge(s["t_done"], n + 1)
                if n >= 2:
                    act.wait_ge(s["pv_done"], n - 1)
                w = width(n)
                ins = nc.scalar.activation(pt[:, n % 2, 0:min(w, 512)], M.PS[:, 4, 0:min(w, 512)], ACT.Copy)
                if w > 512:
                    ins = nc.scalar.activation(pt[:, n % 2, 512:w], M.PS[:, 5, 0:w - 512], ACT.Copy)
                ins.then_inc(s["pt_done"], 1)

            def copy_out(m):
                act.wait_ge(s["pv_done"], 2 * m + 2)
                nc.scalar.activation(items[2 * m].o, M.PS[:, 6 + m % 2, 0:P], ACT.Copy).then_inc(s["o_done"], 1)

            for n in range(N + 2):
                if n < N:
                    exps(n)
                if 1 <= n <= N:
                    copy_turned(n - 1)
                if n >= 2 and n % 2 == 1:
                    copy_out((n - 3) // 2)
    give(nc, s)


def attend1(nc, M, B):
    items = []
    for t in range(TT):
        w = P * (t + 1)
        for h in range(NH_A):
            b, c = HD * (h % 2), h // 2
            items.append(Item(
                q=B.PT[b:b + HD, C_AQ + c, t * P:(t + 1) * P],
                segs=[(B.PT[b:b + HD, C_AK + c, 0:w], w, B.bias[:, t, 0:w])],
                vs=[B.V[:, j, V_A + h * HD:V_A + (h + 1) * HD] for j in range(t + 1)],
                o=B.mixT[:, c, t * P:(t + 1) * P]))
    attend(nc, M, items, HD ** -0.5)


def linear_mixers(nc, M, B):
    s = take(M, "s_done p_done pv_done e_in e_done y_done step e_step")
    N = 2 * NH_R * TT
    G = N // 8
    with ExitStack() as ctx:
        pb = ctx.enter_context(M.nc.sbuf_tensor(f"{M.blocks}_lin_p", [P, 2, T], F32))
        eb = ctx.enter_context(M.nc.sbuf_tensor(f"{M.blocks}_lin_e", [P, 2, T], F32))
        den = ctx.enter_context(M.nc.sbuf_tensor(f"{M.blocks}_lin_den", [P, T], F32))
        block = ctx.enter_context(nc.Block())

        def item(n):
            kind, h, t = n // (NH_R * TT), n // TT % NH_R, n % TT
            return kind, h, t, T - P * t

        @block.tensor
        def _(pe):
            def scores(n):
                kind, h, t, w = item(n)
                b = HD * (h % 2)
                q, k = (C_MQ, C_MK) if kind else (C_RQ, C_RK)
                if n >= 2:
                    pe.wait_ge(s["p_done"], n - 1)
                nc.tensor.matmul(M.PS[:, n % 2, 0:w], B.PT[b:b + HD, k + h // 2, t * P:(t + 1) * P],
                                 B.PT[b:b + HD, q + h // 2, t * P:T], start=True, stop=True).then_inc(s["s_done"], 1)

            def values(n):
                kind, h, t, w = item(n)
                b, g = HD * (h % 2), n // 8
                pe.wait_ge(s["p_done"], n + 1)
                if n % 8 == 0 and g >= 2:
                    pe.wait_ge(s["y_done"], g - 1)
                v0 = (V_M if kind else V_R) + h * HD
                mm = nc.tensor.matmul(M.PS[b:b + HD, 2 + g % 2, T - w:T], B.V[:, t, v0:v0 + HD], pb[:, n % 2, 0:w],
                                      start=(t == 0), stop=(t == TT - 1))
                if kind:
                    mm = nc.tensor.matmul(M.PS[b:b + HD, 4 + g % 2, T - w:T], M.K[:, K_ONE:K_ONE + HD],
                                          pb[:, n % 2, 0:w], start=(t == 0), stop=(t == TT - 1))
                mm.then_inc(s["pv_done"], 1)

            for n in range(N + 1):
                if n < N:
                    scores(n)
                if n >= 1:
                    values(n - 1)

        @block.vector
        def _(dve):
            step = Steps(dve, s["step"])

            def weigh(n):
                kind, h, t, w = item(n)
                if n >= 2:
                    dve.wait_ge(s["pv_done"], n - 1)
                if kind:
                    m = n - NH_R * TT
                    dve.wait_ge(s["e_done"], m + 1)
                    dve.wait_ge(s["s_done"], n + 1)
                    step(nc.vector.scalar_tensor_tensor(out=pb[:, n % 2, 0:w], in0=M.PS[:, n % 2, 0:w],
                                                        scalar=HD ** -0.5, in1=eb[:, m % 2, 0:w],
                                                        op0=ALU.mult, op1=ALU.mult))
                    nc.vector.tensor_tensor(pb[:, n % 2, 0:P], pb[:, n % 2, 0:P], B.L[:, L_UP:L_UP + P],
                                            ALU.mult).then_inc(s["p_done"], 1)
                else:
                    dve.wait_ge(s["s_done"], n + 1)
                    nc.vector.scalar_tensor_tensor(out=pb[:, n % 2, 0:w], in0=M.PS[:, n % 2, 0:w],
                                                   scalar=HD ** -0.5, in1=B.L[:, h * T:h * T + w],
                                                   op0=ALU.mult, op1=ALU.mult).then_inc(s["p_done"], 1)

            def exponent(m):
                h, t = m // TT, m % TT
                w = T - P * t
                if m >= 2:
                    dve.wait_ge(s["p_done"], NH_R * TT + m - 1)
                nc.vector.tensor_scalar(eb[:, m % 2, 0:w], B.Amax[:, h, T - w:T],
                                        B.acol[:, t * NH_M + h:t * NH_M + h + 1], 0.0,
                                        ALU.subtract, ALU.max).then_inc(s["e_in"], 1)

            def take_pair(g):
                dve.wait_ge(s["pv_done"], 8 * g + 8)
                if g < 2:
                    nc.vector.tensor_copy(B.Y[:, g, :], M.PS[:, 2 + g % 2, :]).then_inc(s["y_done"], 1)
                    return
                step(nc.vector.tensor_scalar(den[:], M.PS[:, 4 + g % 2, :], -1.0, None, ALU.mult))
                step(nc.vector.tensor_tensor(den[:], M.PS[:, 4 + g % 2, :], den[:], ALU.max))
                step(nc.vector.tensor_tensor(den[:], den[:], B.floor[:, g - 2, :], ALU.max))
                step(nc.vector.reciprocal(den[:], den[:]))
                step(nc.vector.tensor_tensor(den[:], den[:], B.PT[:, C_MO + g - 2, :], ALU.mult))
                nc.vector.tensor_tensor(B.Y[:, g, :], M.PS[:, 2 + g % 2, :], den[:], ALU.mult).then_inc(s["y_done"], 1)

            half = NH_R * TT
            for n in range(N + 1):
                if half - 1 <= n < N - 1:
                    exponent(n + 1 - half)
                if n < N:
                    weigh(n)
                if n >= 1 and n % 8 == 0:
                    take_pair(n // 8 - 1)

        @block.scalar
        def _(act):
            for m in range(NH_M * TT):
                w = T - P * (m % TT)
                act.wait_ge(s["e_in"], m + 1)
                nc.scalar.activation(eb[:, m % 2, 0:w], eb[:, m % 2, 0:w], ACT.Exp, scale=-1.0).then_inc(s["e_done"], 1)
    give(nc, s)


def head_norm(nc, M, B):
    s = take(M, "mean cen sq var sd norm rstd done")
    with ExitStack() as ctx:
        cen = ctx.enter_context(M.nc.sbuf_tensor(f"{M.blocks}_hn_cen", [P, 4, T], F32))
        sq = ctx.enter_context(M.nc.sbuf_tensor(f"{M.blocks}_hn_sq", [P, 4, T], F32))
        block = ctx.enter_context(nc.Block())
        heads = B.L[:, L_HEAD:L_HEAD + P]

        @block.tensor
        def _(pe):
            for c in range(4):
                nc.tensor.matmul(M.PS[:, c, :], heads, B.Y[:, c, :], start=True, stop=True).then_inc(s["mean"], 1)
            for c in range(4):
                pe.wait_ge(s["sq"], c + 1)
                nc.tensor.matmul(M.PS[:, 4 + c, :], heads, sq[:, c, :], start=True, stop=True).then_inc(s["var"], 1)

        @block.vector
        def _(dve):
            for c in range(4):
                dve.wait_ge(s["mean"], c + 1)
                nc.vector.tensor_tensor(cen[:, c, :], B.Y[:, c, :], M.PS[:, c, :], ALU.subtract).then_inc(s["cen"], 1)
            for c in range(4):
                dve.wait_ge(s["sd"], c + 1)
                nc.vector.reciprocal(sq[:, c, :], sq[:, c, :]).then_inc(s["rstd"], 1)
                dve.wait_ge(s["rstd"], c + 1)
                out = B.mixT[:, 4 + c, :] if c >= 2 else cen[:, c, :]
                nc.vector.tensor_tensor(out, cen[:, c, :], sq[:, c, :], ALU.mult).then_inc(s["norm"], 1)
                if c < 2:
                    dve.wait_ge(s["norm"], c + 1)
                    nc.vector.tensor_tensor(B.mixT[:, 4 + c, :], cen[:, c, :], B.PT[:, C_RG + c, :],
                                            ALU.mult).then_inc(s["done"], 1)

        @block.scalar
        def _(act):
            for c in range(4):
                act.wait_ge(s["cen"], c + 1)
                nc.scalar.activation(sq[:, c, :], cen[:, c, :], ACT.Square).then_inc(s["sq"], 1)
            for c in range(4):
                act.wait_ge(s["var"], c + 1)
                nc.scalar.activation(sq[:, c, :], M.PS[:, 4 + c, :], ACT.Sqrt, bias=M.eps[:, 0:1]).then_inc(s["sd"], 1)
    give(nc, s)


class Modulation:

    def __init__(self, nc, M, ctx, s, w, b, cond, first, n, conds=2):
        self.nc, self.M, self.s, self.w, self.first, self.n = nc, M, s, w, first, n
        self.b, self.cond, self.conds = b, cond, conds
        self.W = ctx.enter_context(nc.sbuf_tensor(f"{M.blocks}_mod_w", [P, 2, n, D], F32))
        self.B = ctx.enter_context(nc.sbuf_tensor(f"{M.blocks}_mod_b", [P, 2 * N_MOD], F32))
        self.J = ctx.enter_context(nc.sbuf_tensor(f"{M.blocks}_mod_c", [P, D], F32))
        self.acc = ctx.enter_context(nc.sbuf_tensor(f"{M.blocks}_mod_acc", [P, 2, 2 * n], F32))
        self.ready = (s["r0"], s["r1"])

    def silu_cond(self, c):
        return self.M.PS[:, 2 + 4 * c:4 + 4 * c, :].rearrange("p a b -> p (a b)")

    def load(self, sp):
        s = self.s
        sp.dma_start(self.B[:], self.b).then_inc(s["bias_in"], 16)
        for c in range(self.conds):
            if c:
                sp.wait_ge(s["summed"], c)
            sp.dma_start(self.J[:], self.cond[c].partition_broadcast(P)).then_inc(s["cond_in"], 16)

    def load_first(self, eng):
        for u in range(2):
            eng.dma_start(self.W[:, u], self.w(self.first + u * self.n)).then_inc(self.ready[u], 16)

    def load_next(self, sp, i, u):
        sp.wait_ge(self.s["added"], 2 * i + u - 1)
        sp.dma_start(self.W[:, u], self.w(2 * i * self.n + (self.first + u * self.n))).then_inc(self.ready[u], 16)

    def sigmoid(self, act):
        for c in range(self.conds):
            act.wait_ge(self.s["cond_in"], 16 * (c + 1))
            for j in range(2):
                self.nc.scalar.activation(self.M.PS[:, 2 + 4 * c + j, :], self.J[:, j * 512:(j + 1) * 512],
                                          ACT.Sigmoid).then_inc(self.s["sig"], 1)

    def conditions(self, dve):
        self.nc.vector.memset(self.acc[:], 0.0).then_inc(self.s["bias_in"], 16)
        for c in range(self.conds):
            dve.wait_ge(self.s["sig"], 2 * c + 2)
            self.nc.vector.tensor_tensor(self.silu_cond(c), self.J[:], self.silu_cond(c),
                                         ALU.mult).then_inc(self.s["summed"], 1)
        dve.wait_ge(self.s["summed"], self.conds)
        dve.wait_ge(self.s["bias_in"], 32)

    def chunks(self, dve, i, u):
        nc, s, C = self.nc, self.s, self.conds
        K = C * self.n
        dve.wait_ge(self.ready[u], 16 * i + 16)
        for j in range(K):
            a = j // C * 2 + j % C
            nc.vector.tensor_tensor_reduce(out=self.J[:], in0=self.W[:, u, j // C], in1=self.silu_cond(j % C),
                                           scale=1.0, scalar=0.0, op0=ALU.mult, op1=ALU.add,
                                           accum_out=self.acc[:, u, a:a + 1]).then_inc(s["summed"], 1)
            dve.wait_ge(s["summed"], 2 * K * i + (C + u * K + j + 1))
        col = 2 * self.n * (2 * i + u) + 2 * self.first
        nc.vector.tensor_tensor(self.M.mod_next[:, bass.ds(col, 2 * self.n)], self.acc[:, u, :],
                                self.B[:, bass.ds(col, 2 * self.n)], ALU.add).then_inc(s["added"], 1)


def gemm_residual(nc, M, w, src, KP, spans, gate, alpha, mix=None, ride=None):
    s = take(M, STREAM + "h_high h_done psum_free scaled r0 r1 bias_in cond_in sig summed added")
    NS = len(spans)
    TW = sum(n for _, n, _ in spans)
    with ExitStack() as ctx:
        S = Stream(nc, M, ctx, s, w, KD, KP)
        tmp = ctx.enter_context(nc.sbuf_tensor(f"{M.blocks}_out_t", [P, 1, TW], F32))
        if ride:
            rw, rb, cond, r_first, r_n = ride
            R = Modulation(nc, M, ctx, s, rw, rb, cond, r_first, r_n)
        block = ctx.enter_context(nc.Block())

        @block.sync
        def _(sp):
            S.load(sp)
            if ride:
                R.load(sp)
            S.load_rest(sp)

        @block.tensor
        def _(pe):
            def chunk(n, u, w):
                pe.wait_ge(s["psum_free"], NS * n + NS)
                for k in range(KP):
                    for a, (t0, nt, _) in enumerate(spans):
                        mm = product(nc, M.PS[:, 4 * u + a, 0:nt], (w[0][:, k], w[1][:, k]),
                                     (src[:, 0, k, t0:t0 + nt], src[:, 1, k, t0:t0 + nt]), k == 0, k == KP - 1)
                return mm

            if mix is not None:
                pe.wait_ge(s["h_done"], KD)
            S.multiply(pe, chunk)

        @block.gpsimd
        def _(pool):
            if ride:
                R.load_first(pool)
            S.lows(pool, R.load_next if ride else None)

        @block.scalar
        def _(act):
            if mix is not None:
                for k in range(KD):
                    nc.scalar.activation(src[:, 0, k], mix[:, k, :], ACT.Copy).then_inc(s["h_high"], 1)
            if ride:
                R.sigmoid(act)
            S.highs(act, lambda n, u: None)

        @block.vector
        def _(dve):
            dve.sem_inc(s["psum_free"], 2 * NS)
            dve.sem_inc(s["scaled"], NS)
            if mix is not None:
                for k in range(KD):
                    split_rows(nc, s, src, k, mix[:, k, :], dve)
            if ride:
                R.conditions(dve)
            with dve.Fori(0, KD // 2) as i:
                for u in range(2):
                    dve.wait_ge(s["used"], 2 * i + u + 3)
                    dve.wait_ge(s["scaled"], 2 * NS * i + NS * (u + 1))
                    off = 0
                    for a, (t0, nt, c) in enumerate(spans):
                        g = M.mod[:, bass.ds((gate * KD + 2 * i + u) * 2 + c, 1)]
                        nc.vector.tensor_scalar(tmp[:, 0, off:off + nt], M.PS[:, 4 * u + a, 0:nt], g, None,
                                                ALU.mult).then_inc(s["psum_free"], 1)
                        off += nt
                    off = 0
                    for a, (t0, nt, c) in enumerate(spans):
                        dve.wait_ge(s["psum_free"], 2 * NS + 2 * NS * i + NS * u + a + 1)
                        x = M.xT[:, bass.ds(2 * i + u, 1), t0:t0 + nt]
                        nc.vector.scalar_tensor_tensor(out=x, in0=x, scalar=float(alpha),
                                                       in1=tmp[:, 0:1, off:off + nt],
                                                       op0=ALU.mult, op1=ALU.add).then_inc(s["scaled"], 1)
                        off += nt
                    if ride:
                        R.chunks(dve, i, u)
    give(nc, s)


def adopt(nc, M, plus_one):
    s = take(M, "copied done")
    with nc.Block() as block:
        @block.vector
        def _(dve):
            nc.vector.tensor_copy(M.mod[:], M.mod_next[:]).then_inc(s["copied"], 1)
            dve.wait_ge(s["copied"], 1)
            for part in plus_one:
                m = M.mod[:, part * KD * 2:(part + 1) * KD * 2]
                nc.vector.tensor_scalar(m, m, 1.0, None, ALU.add).then_inc(s["done"], 1)
    give(nc, s)


def layer_norm(nc, M, gb):
    s = take(M, "par mean cen sq var sd rstd norm done")
    with ExitStack() as ctx:
        GB = ctx.enter_context(M.nc.sbuf_tensor(f"{M.blocks}_ln_gb", [P, 2, KD], F32))
        sq = ctx.enter_context(M.nc.sbuf_tensor(f"{M.blocks}_ln_sq", [P, 4, T], F32))
        rs = ctx.enter_context(M.nc.sbuf_tensor(f"{M.blocks}_ln_rs", [P, T], F32))
        block = ctx.enter_context(nc.Block())
        mean = M.K[:, K_MEAN:K_MEAN + P]

        @block.sync
        def _(sp):
            sp.dma_start(GB[:], gb).then_inc(s["par"], 16)

        @block.tensor
        def _(pe):
            for k in range(KD):
                mm = nc.tensor.matmul(M.PS[:, 0, :], mean, M.xT[:, k, 0:T], start=(k == 0), stop=(k == KD - 1))
            mm.then_inc(s["mean"], 1)
            for k in range(KD):
                pe.wait_ge(s["sq"], k + 1)
                nc.tensor.matmul(M.PS[:, 1, :], mean, sq[:, k % 4, :], start=(k == 0),
                                 stop=(k == KD - 1)).then_inc(s["var"], 1)

        @block.vector
        def _(dve):
            dve.wait_ge(s["mean"], 1)
            for k in range(KD):
                nc.vector.tensor_tensor(M.xT[:, k, 0:T], M.xT[:, k, 0:T], M.PS[:, 0, :],
                                        ALU.subtract).then_inc(s["cen"], 1)
            dve.wait_ge(s["sd"], 1)
            nc.vector.reciprocal(rs[:], rs[:]).then_inc(s["rstd"], 1)
            dve.wait_ge(s["rstd"], 1)
            for k in range(KD):
                nc.vector.tensor_tensor(M.xT[:, k, 0:T], M.xT[:, k, 0:T], rs[:], ALU.mult).then_inc(s["norm"], 1)

        @block.scalar
        def _(act):
            for k in range(KD):
                act.wait_ge(s["cen"], k + 1)
                if k >= 4:
                    act.wait_ge(s["var"], k - 3)
                nc.scalar.activation(sq[:, k % 4, :], M.xT[:, k, 0:T], ACT.Square).then_inc(s["sq"], 1)
            act.wait_ge(s["var"], KD)
            nc.scalar.activation(rs[:], M.PS[:, 1, :], ACT.Sqrt, bias=M.eps[:, 0:1]).then_inc(s["sd"], 1)
            act.wait_ge(s["par"], 16)
            for k in range(KD):
                act.wait_ge(s["norm"], k + 1)
                nc.scalar.activation(M.xT[:, k, 0:T], M.xT[:, k, 0:T], ACT.Identity, bias=GB[:, 1, k:k + 1],
                                     scale=GB[:, 0, k:k + 1]).then_inc(s["done"], 1)
    give(nc, s)


def route(nc, M, A, gT):
    s = take(M, "par h_f32 h_high h_done logits sig step gated tr")
    with ExitStack() as ctx:
        wr = ctx.enter_context(M.nc.sbuf_tensor(f"{M.blocks}_router_w", [P, KD, NE], F32))
        br = ctx.enter_context(M.nc.sbuf_tensor(f"{M.blocks}_router_b", [P, NE], F32))
        sc = ctx.enter_context(M.nc.sbuf_tensor(f"{M.blocks}_r_score", [P, TT, NE], F32))
        bi = ctx.enter_context(M.nc.sbuf_tensor(f"{M.blocks}_r_biased", [P, TT, NE], F32))
        v = ctx.enter_context(M.nc.sbuf_tensor(f"{M.blocks}_r_cand", [P, TT, NE], F32))
        eq = ctx.enter_context(M.nc.sbuf_tensor(f"{M.blocks}_r_eq", [P, TT, NE], F32))
        chosen = ctx.enter_context(M.nc.sbuf_tensor(f"{M.blocks}_r_chosen", [P, TT, NE], F32))
        pair = ctx.enter_context(M.nc.sbuf_tensor(f"{M.blocks}_r_pair", [P, TT * NG, 6], F32))
        gs = ctx.enter_context(M.nc.sbuf_tensor(f"{M.blocks}_r_group", [P, TT, NG], F32))
        ge = ctx.enter_context(M.nc.sbuf_tensor(f"{M.blocks}_r_geq", [P, TT, NG], F32))
        m1 = ctx.enter_context(M.nc.sbuf_tensor(f"{M.blocks}_r_m1", [P, TT], F32))
        block = ctx.enter_context(nc.Block())

        @block.sync
        def _(sp):
            sp.dma_start(wr[:], A["w_router"]).then_inc(s["par"], 16)
            sp.dma_start(br[:], A["b_router"].partition_broadcast(P)).then_inc(s["par"], 16)

        @block.tensor
        def _(pe):
            pe.wait_ge(s["par"], 32)
            pe.wait_ge(s["h_f32"], KD)
            for t in range(TT):
                for k in range(KD):
                    mm = nc.tensor.matmul(M.PS[:, 0, t * NE:(t + 1) * NE], M.hT[:, k, t * P:(t + 1) * P], wr[:, k, :],
                                          start=(k == 0), stop=(k == KD - 1))
            mm.then_inc(s["logits"], 1)
            pe.wait_ge(s["gated"], 1)
            for t in range(TT):
                mm = nc.tensor.transpose(M.PS[0:NE, 1, t * P:(t + 1) * P], v[:, t, :], M.K[:, K_ID:K_ID + P])
            mm.then_inc(s["tr"], 1)

        @block.scalar
        def _(act):
            for k in range(KD):
                nc.scalar.activation(M.hT[:, k, 0:T], M.xT[:, k, 0:T], ACT.Identity,
                                     bias=modcol(M, 3, k), scale=modcol(M, 4, k)).then_inc(s["h_f32"], 1)
            for k in range(KD):
                act.wait_ge(s["h_f32"], k + 1)
                nc.scalar.activation(M.hR[:, 0, k], M.hT[:, k, :], ACT.Copy).then_inc(s["h_high"], 1)
            act.wait_ge(s["logits"], 1)
            nc.scalar.activation(sc[:], M.PS[:, 0, 0:TT * NE].rearrange("p (t e) -> p t e", t=TT),
                                 ACT.Sigmoid).then_inc(s["sig"], 1)
            act.wait_ge(s["tr"], 1)
            nc.scalar.activation(gT[:], M.PS[0:NE, 1, :], ACT.Copy)

        @block.vector
        def _(dve):
            step = Steps(dve, s["step"])
            rank_e = M.K[:, K_RANK:K_RANK + NE].unsqueeze(1).to_broadcast([P, TT, NE])
            rank_g = M.K[:, K_RANK + NE:K_RANK + NE + NG].unsqueeze(1).to_broadcast([P, TT, NG])
            over_e = lambda a, n: a[:].unsqueeze(2).to_broadcast([P, TT, n])
            tt = nc.vector.tensor_tensor
            for k in range(KD):
                split_rows(nc, s, M.hR, k, M.hT[:, k, :], dve)
            dve.wait_ge(s["par"], 32)
            dve.wait_ge(s["sig"], 1)
            step(tt(bi[:], sc[:], br[:].unsqueeze(1).to_broadcast([P, TT, NE]), ALU.add))
            quad = bi[:].rearrange("p t (g e) -> p (t g) e", e=EPG)
            at = 0
            for a in range(EPG - 1):
                for b in range(a + 1, EPG):
                    step(tt(pair[:, :, at:at + 1], quad[:, :, a:a + 1], quad[:, :, b:b + 1], ALU.add))
                    at += 1
            step(nc.vector.tensor_reduce(gs[:].rearrange("p t g -> p (t g)"), pair[:], AX.X, ALU.max))

            def first_best(out, val, n, rank):
                step(nc.vector.tensor_reduce(m1[:], val[:], AX.X, ALU.max))
                step(tt(out[:], val[:], over_e(m1, n), ALU.is_equal))
                step(tt(out[:], out[:], rank, ALU.mult))
                step(nc.vector.tensor_reduce(m1[:], out[:], AX.X, ALU.max))
                step(tt(out[:], out[:], over_e(m1, n), ALU.is_equal))

            first_best(ge, gs, NG, rank_g)
            geb = ge[:].rearrange("p t g -> p (t g)").unsqueeze(2).to_broadcast([P, TT * NG, EPG])
            step(tt(v[:].rearrange("p t (g e) -> p (t g) e", e=EPG), quad, geb, ALU.mult))
            step(nc.vector.tensor_scalar(ge[:], ge[:], -1.0, -NEG, ALU.add, ALU.mult))
            vq = v[:].rearrange("p t (g e) -> p (t g) e", e=EPG)
            step(tt(vq, vq, geb, ALU.add))
            first_best(chosen, v, NE, rank_e)
            step(nc.vector.scalar_tensor_tensor(out=v[:].rearrange("p t e -> p (t e)"),
                                                in0=chosen[:].rearrange("p t e -> p (t e)"), scalar=NEG,
                                                in1=v[:].rearrange("p t e -> p (t e)"), op0=ALU.mult, op1=ALU.add))
            first_best(eq, v, NE, rank_e)
            step(tt(chosen[:], chosen[:], eq[:], ALU.add))
            step(tt(v[:], chosen[:], sc[:], ALU.mult))
            step(nc.vector.tensor_reduce(m1[:], v[:], AX.X, ALU.add))
            step(nc.vector.reciprocal(m1[:], m1[:]))
            tt(v[:], v[:], over_e(m1, NE), ALU.mult).then_inc(s["gated"], 1)
    give(nc, s)


def gated_up(nc, M, w, hid, NF, spans, gates=None, gT=None, e0=0):
    s = take(M, STREAM + "spread spread_out silu_done psum_free prod_done gated high_out low_out")
    TW = sum(n for _, n in spans)
    with ExitStack() as ctx:
        S = Stream(nc, M, ctx, s, w, NF, 2 * KD)
        sl = ctx.enter_context(nc.sbuf_tensor(f"{M.blocks}_silu", [P, 2, TW], F32))
        pr = ctx.enter_context(nc.sbuf_tensor(f"{M.blocks}_silu_up", [P, 2, TW], F32))
        block = ctx.enter_context(nc.Block())
        NG_ = NF // 2

        @block.sync
        def _(sp):
            S.load(sp)
            S.load_rest(sp)

        @block.gpsimd
        def _(pool):
            S.lows(pool)

        @block.tensor
        def _(pe):
            if gates is not None:
                for e in range(NG_):
                    if e >= 4:
                        pe.wait_ge(s["spread_out"], e - 3)
                    one = M.K[0:NE, K_ID + e0 + e:K_ID + e0 + e + 1].to_broadcast([NE, P])
                    nc.tensor.matmul(M.PS[:, e % 4, :], one, gT[:], start=True,
                                     stop=True).then_inc(s["spread"], 1)
                pe.wait_ge(s["spread_out"], NG_)

            def chunk(n, u, w):
                pe.wait_ge(s["psum_free"], n + 1)
                for part in range(2):
                    for k in range(KD):
                        for a, (t0, nt) in enumerate(spans):
                            j = part * KD + k
                            mm = product(nc, M.PS[:, 4 * u + 2 * part + a, 0:nt], (w[0][:, j], w[1][:, j]),
                                         (M.hR[:, 0, k, t0:t0 + nt], M.hR[:, 1, k, t0:t0 + nt]),
                                         k == 0, k == KD - 1)
                return mm

            S.multiply(pe, chunk)

        @block.scalar
        def _(act):
            if gates is not None:
                for e in range(NG_):
                    act.wait_ge(s["spread"], e + 1)
                    nc.scalar.activation(gates[:, e, :], M.PS[:, e % 4, :], ACT.Copy).then_inc(s["spread_out"], 1)

            def out(n, u):
                act.wait_ge(s["used"], n + 3)
                off = 0
                for a, (_, nt) in enumerate(spans):
                    ins = nc.scalar.activation(sl[:, u, off:off + nt], M.PS[:, 4 * u + a, 0:nt], ACT.Silu)
                    off += nt
                ins.then_inc(s["silu_done"], 1)

            S.highs(act, out)

        @block.vector
        def _(dve):
            dve.sem_inc(s["psum_free"], 2)
            with dve.Fori(0, NF // 2) as i:
                for u in range(2):
                    n = 2 * i + u
                    dve.wait_ge(s["silu_done"], n + 1)
                    off = 0
                    for a, (_, nt) in enumerate(spans):
                        ins = nc.vector.tensor_tensor(pr[:, u, off:off + nt], sl[:, u, off:off + nt],
                                                      M.PS[:, 4 * u + 2 + a, 0:nt], ALU.mult)
                        off += nt
                    ins.then_inc(s["psum_free"], 1)
                    dve.wait_ge(s["psum_free"], n + 3)
                    if gates is not None:
                        nc.vector.tensor_tensor(pr[:, u:u + 1], pr[:, u:u + 1], at(gates, i, slice(None)),
                                                ALU.mult).then_inc(s["gated"], 1)
                        dve.wait_ge(s["gated"], n + 1)
                    high = at(hid[:, 0], n, slice(None))
                    nc.vector.tensor_copy(high, pr[:, u:u + 1]).then_inc(s["high_out"], 1)
                    dve.wait_ge(s["high_out"], n + 1)
                    nc.vector.tensor_tensor(at(hid[:, 1], n, slice(None)), pr[:, u:u + 1], high.bitcast(F32),
                                            ALU.subtract).then_inc(s["low_out"], 1)
    give(nc, s)


def block_one(nc, M, A):
    def tensor(ctx, name, shape, dt=F32):
        return ctx.enter_context(M.nc.sbuf_tensor("one_" + name, shape, dt))

    with ExitStack() as outer:
        M.rope = nc.dram_tensor("rope_tables", (P, 2, T), F32).ap()
        setup(nc, M, A)
        M.hR = tensor(outer, "h_parts", [P, 2, KD, T], F32R)
        ada(nc, M, A)
        with nc.Fori(0, DEPTH) as l:
            adopt(nc, M, (1, 2, 4, 5))
            with ExitStack() as ctx:
                B = Buffers()
                B.PT = tensor(ctx, "projT", [P, N_CH, T])
                B.V = tensor(ctx, "values", [P, TT, N_V])
                B.iw = tensor(ctx, "index_w", [P, TT * NH_I])
                with ExitStack() as inner:
                    M.hT = tensor(inner, "hT_mix", [P, KD, T])
                    proj1(nc, M, A, l, B)
                B.mixT = tensor(ctx, "mixT", [P, KD, T])
                with ExitStack() as inner:
                    B.L = tensor(inner, "mixer_consts", [P, L_N])
                    B.Amax = tensor(inner, "i_max_all", [P, NH_M, T])
                    B.floor = tensor(inner, "floor_all", [P, NH_M // 2, T])
                    B.acol = tensor(inner, "i_rel_col", [P, TT * NH_M])
                    B.bias = tensor(inner, "key_bias", [P, TT, T])
                    B.Y = tensor(inner, "lin_y", [P, 4, T])
                    convolve(nc, M, A, l, B)
                    select_keys(nc, M, B)
                    attend1(nc, M, B)
                    linear_mixers(nc, M, B)
                    head_norm(nc, M, B)
                gemm_residual(nc, M, lambda n: A["w_out"][l, n], M.hR, KD, [(0, T, 0)], 2, ALPHA, mix=B.mixT)
            layer_norm(nc, M, A["ln_mix"][l])
            with ExitStack() as ctx:
                gT = tensor(ctx, "gate_rows", [NE, T])
                with ExitStack() as inner:
                    M.hT = tensor(inner, "hT_ffn", [P, KD, T])
                    route(nc, M, A, gT)
                ROUNDS = 2
                NF = NE * FE // P // ROUNDS
                hid = tensor(ctx, "hidden", [P, 2, NF, T], F32R)
                for r in range(ROUNDS):
                    with M.nc.sbuf_tensor(f"expert_gates{r}", [P, NE // ROUNDS, T], F32) as gates:
                        gated_up(nc, M, lambda n: A["w_gu"][l, n + r * NF], hid, NF, [(0, T)], gates, gT,
                                 r * NE // ROUNDS)
                    per = N_MOD // ROUNDS // KD
                    ride = (modulation(A, l + 1, per), A["b_ada"][l + 1], A["cond"][l], r * KD * per, per)
                    gemm_residual(nc, M, lambda n: A["w_down"][l, n, :, r * NF:(r + 1) * NF], hid, NF,
                                  [(0, T, 0)], 5, 1.0 if r else ALPHA, ride=ride)
            layer_norm(nc, M, A["ln_ffn"][l])


def rms_modulate(nc, M, w, spans, shift=None, scale=None):
    s = take(M, "par ws sq sum sd rstd norm h_f32 h_high h_done")
    NS = len(spans)
    with ExitStack() as ctx:
        nw = ctx.enter_context(M.nc.sbuf_tensor(f"{M.blocks}_norm_w", [P, KD], F32))
        ws = ctx.enter_context(M.nc.sbuf_tensor(f"{M.blocks}_norm_ws", [P, 2, KD], F32))
        sq = ctx.enter_context(M.nc.sbuf_tensor(f"{M.blocks}_rms_sq", [P, 4, T], F32))
        rs = ctx.enter_context(M.nc.sbuf_tensor(f"{M.blocks}_rms_rs", [P, 2, T], F32))
        block = ctx.enter_context(nc.Block())

        @block.sync
        def _(sp):
            sp.dma_start(nw[:], w).then_inc(s["par"], 16)

        @block.tensor
        def _(pe):
            for a, (t0, nt, c) in enumerate(spans):
                for k in range(KD):
                    n = a * KD + k
                    pe.wait_ge(s["sq"], n + 1)
                    nc.tensor.matmul(M.PS[:, a, 0:nt], M.K[:, K_MEAN:K_MEAN + P], sq[:, n % 4, 0:nt],
                                     start=(k == 0), stop=(k == KD - 1)).then_inc(s["sum"], 1)

        @block.vector
        def _(dve):
            dve.wait_ge(s["par"], 16)
            for a, (t0, nt, c) in enumerate(spans):
                if scale is None:
                    nc.vector.tensor_copy(ws[:, a, :], nw[:]).then_inc(s["ws"], 1)
                else:
                    part = M.mod[:, scale * KD * 2:(scale + 1) * KD * 2].rearrange("p (k c) -> p k c", c=2)
                    nc.vector.tensor_tensor(ws[:, a, :], nw[:], part[:, :, c], ALU.mult).then_inc(s["ws"], 1)
            for a, (t0, nt, c) in enumerate(spans):
                dve.wait_ge(s["sd"], a + 1)
                nc.vector.reciprocal(rs[:, a, 0:nt], rs[:, a, 0:nt]).then_inc(s["rstd"], 1)
                dve.wait_ge(s["rstd"], a + 1)
                for k in range(KD):
                    nc.vector.tensor_tensor(M.hT[:, k, t0:t0 + nt], M.xT[:, k, t0:t0 + nt], rs[:, a, 0:nt],
                                            ALU.mult).then_inc(s["norm"], 1)
            if scale is not None:
                for a, (t0, nt, c) in enumerate(spans):
                    for k in range(KD):
                        dve.wait_ge(s["h_high"], a * KD + k + 1)
                        nc.vector.tensor_tensor(M.hR[:, 1, k, t0:t0 + nt], M.hT[:, k, t0:t0 + nt],
                                                M.hR[:, 0, k, t0:t0 + nt].bitcast(F32),
                                                ALU.subtract).then_inc(s["h_done"], 1)

        @block.scalar
        def _(act):
            for a, (t0, nt, c) in enumerate(spans):
                for k in range(KD):
                    n = a * KD + k
                    if n >= 4:
                        act.wait_ge(s["sum"], n - 3)
                    nc.scalar.activation(sq[:, n % 4, 0:nt], M.xT[:, k, t0:t0 + nt], ACT.Square).then_inc(s["sq"], 1)
                act.wait_ge(s["sum"], (a + 1) * KD)
                nc.scalar.activation(rs[:, a, 0:nt], M.PS[:, a, 0:nt], ACT.Sqrt, bias=M.eps[:, 1:2]).then_inc(s["sd"], 1)
            act.wait_ge(s["ws"], NS)
            for a, (t0, nt, c) in enumerate(spans):
                for k in range(KD):
                    act.wait_ge(s["norm"], a * KD + k + 1)
                    h = M.hT[:, k, t0:t0 + nt]
                    bias = 0.0 if shift is None else modcol(M, shift, k, c)
                    nc.scalar.activation(h, h, ACT.Identity, bias=bias, scale=ws[:, a, k:k + 1]).then_inc(s["h_f32"], 1)
            if scale is not None:
                for a, (t0, nt, c) in enumerate(spans):
                    for k in range(KD):
                        act.wait_ge(s["h_f32"], a * KD + k + 1)
                        nc.scalar.activation(M.hR[:, 0, k, t0:t0 + nt], M.hT[:, k, t0:t0 + nt],
                                             ACT.Copy).then_inc(s["h_high"], 1)
    give(nc, s)


def project(nc, M, wt, n_t, out, spans, wv=None, n_v=0, outv=None, tiles=0, loads=()):
    s = take(M, STREAM + "psum_free copied wv tok_done tok_free more")
    with ExitStack() as ctx:
        S = Stream(nc, M, ctx, s, wt, n_t, KD)
        WV = ctx.enter_context(M.nc.sbuf_tensor(f"{M.blocks}_proj_wv", [P, KD, 512], F32)) if n_v else None
        block = ctx.enter_context(nc.Block())

        @block.sync
        def _(sp):
            S.load(sp)
            if n_v:
                sp.dma_start(WV[:], wv[0]).then_inc(s["wv"], 16)
            S.load_rest(sp)
            for dst, src in loads:
                sp.dma_start(dst, src).then_inc(s["more"], 16)
            for g in range(1, n_v):
                sp.wait_ge(s["tok_done"], g * tiles)
                sp.dma_start(WV[:], wv[g]).then_inc(s["wv"], 16)
            if loads:
                sp.wait_ge(s["more"], 16 * len(loads))

        @block.gpsimd
        def _(pool):
            S.lows(pool)

        @block.tensor
        def _(pe):
            def chunk(n, u, w):
                pe.wait_ge(s["psum_free"], n + 1)
                for k in range(KD):
                    for a, (t0, nt) in enumerate(spans):
                        mm = product(nc, M.PS[:, 4 * u + a, 0:nt], (w[0][:, k], w[1][:, k]),
                                     (M.hR[:, 0, k, t0:t0 + nt], M.hR[:, 1, k, t0:t0 + nt]), k == 0, k == KD - 1)
                return mm

            S.multiply(pe, chunk)
            for n in range(n_v * tiles):
                g, t = n // tiles, n % tiles
                if t == 0:
                    pe.wait_ge(s["wv"], 16 * (g + 1))
                if n >= 2:
                    pe.wait_ge(s["tok_free"], n - 1)
                for k in range(KD):
                    mm = nc.tensor.matmul(M.PS[:, 2 + n % 2, :], M.hT[:, k, t * P:(t + 1) * P], WV[:, k, :],
                                          start=(k == 0), stop=(k == KD - 1))
                mm.then_inc(s["tok_done"], 1)

        @block.scalar
        def _(act):
            act.sem_inc(s["psum_free"], 2)

            def copy(n, u):
                act.wait_ge(s["used"], n + 3)
                off = 0
                for a, (_, nt) in enumerate(spans):
                    ins = nc.scalar.activation(at(out, n, slice(off, off + nt)), M.PS[:, 4 * u + a, 0:nt], ACT.Copy)
                    off += nt
                ins.then_inc(s["copied"], 1)
                act.wait_ge(s["copied"], n + 1)
                act.sem_inc(s["psum_free"], 1)

            S.highs(act, copy)
            for n in range(n_v * tiles):
                g, t = n // tiles, n % tiles
                act.wait_ge(s["tok_done"], n + 1)
                nc.scalar.activation(outv[:, t, g * 512:(g + 1) * 512], M.PS[:, 2 + n % 2, :],
                                     ACT.Copy).then_inc(s["tok_free"], 1)
    give(nc, s)


def spatial_gate(nc, M, A, B):
    s = take(M, "rel_in par gelu_v ssq sd rstd normed gelu_u gate biased done")
    NT = TA // P
    with ExitStack() as ctx:
        sw = ctx.enter_context(M.nc.sbuf_tensor(f"{M.blocks}_sgu_w", [P, 4, P], F32))
        sb_ = ctx.enter_context(M.nc.sbuf_tensor(f"{M.blocks}_sgu_b", [P, 4 * P], F32))
        nw = ctx.enter_context(M.nc.sbuf_tensor(f"{M.blocks}_sgu_nw", [P, 4], F32))
        ssq = ctx.enter_context(M.nc.sbuf_tensor(f"{M.blocks}_sgu_ssq", [P, NT], F32))
        junk = ctx.enter_context(M.nc.sbuf_tensor(f"{M.blocks}_sgu_sq", [P, NT, 512], F32))
        g_ = ctx.enter_context(M.nc.sbuf_tensor(f"{M.blocks}_sgu_gate", [P, 2, 512], F32))
        block = ctx.enter_context(nc.Block())

        @block.sync
        def _(sp):
            sp.dma_start(sw[:], A["sgu_w"]).then_inc(s["par"], 16)
            sp.dma_start(sb_[:], A["sgu_b"].partition_broadcast(P)).then_inc(s["par"], 16)
            sp.dma_start(nw[:], A["sgu_nw"]).then_inc(s["par"], 16)
            sp.dma_start(B.rel[:], A["rel"]).then_inc(s["rel_in"], 16)
            sp.wait_ge(s["rel_in"], 16)

        @block.scalar
        def _(act):
            for t in range(NT):
                v = B.V[:, t, 0:512]
                nc.scalar.activation(v, v, ACT.Gelu_apprx_tanh).then_inc(s["gelu_v"], 1)
            for c in range(4):
                u = B.PT[:, c, :]
                nc.scalar.activation(u, u, ACT.Gelu_apprx_tanh).then_inc(s["gelu_u"], 1)
            for t in range(NT):
                act.wait_ge(s["gelu_v"], t + 1)
                nc.scalar.activation(junk[:, t, :], B.V[:, t, 0:512], ACT.Square,
                                     accum_out=ssq[:, t:t + 1]).then_inc(s["ssq"], 1)
            act.wait_ge(s["ssq"], NT)
            nc.scalar.activation(ssq[:], ssq[:], ACT.Sqrt, bias=M.eps[:, 1:2], scale=1.0 / 512).then_inc(s["sd"], 1)

        @block.vector
        def _(dve):
            dve.wait_ge(s["sd"], 1)
            nc.vector.reciprocal(ssq[:], ssq[:]).then_inc(s["rstd"], 1)
            dve.wait_ge(s["rstd"], 1)
            for t in range(NT):
                v = B.V[:, t, 0:512]
                nc.vector.tensor_scalar(v, v, ssq[:, t:t + 1], None, ALU.mult).then_inc(s["normed"], 1)
            dve.wait_ge(s["par"], 48)
            n = 0
            for g in range(4):
                dve.wait_ge(s["gate"], g + 1)
                dve.wait_ge(s["gelu_u"], g + 1)
                for a, (t0, nt) in enumerate(((0, T), (T, TC))):
                    out = g_[:, a, 0:nt].rearrange("p (t q) -> p t q", q=P)
                    bias = sb_[:, g * P:(g + 1) * P].unsqueeze(1).to_broadcast([P, nt // P, P])
                    nc.vector.scalar_tensor_tensor(out=out, in0=M.PS[:, 2 * g + a, 0:nt].rearrange("p (t q) -> p t q", q=P),
                                                   scalar=nw[:, g:g + 1], in1=bias, op0=ALU.mult,
                                                   op1=ALU.add).then_inc(s["biased"], 1)
                    n += 1
                    dve.wait_ge(s["biased"], n)
                    nc.vector.tensor_tensor(B.mixT[:, g, t0:t0 + nt], g_[:, a, 0:nt], B.PT[:, g, t0:t0 + nt],
                                            ALU.mult).then_inc(s["done"], 1)

        @block.tensor
        def _(pe):
            pe.wait_ge(s["par"], 48)
            pe.wait_ge(s["normed"], NT)
            for g in range(4):
                for t in range(NT):
                    mm = nc.tensor.matmul(M.PS[:, 2 * g + t // 4, (t % 4) * P:(t % 4 + 1) * P],
                                          B.V[:, t, g * P:(g + 1) * P], sw[:, g, :], start=True, stop=True)
                mm.then_inc(s["gate"], 1)
    give(nc, s)


def attend2(nc, M, B):
    items = []
    for t in range(TA // P):
        for h in range(8):
            b, c = HD * (h % 2), h // 2
            ctx_keys = (B.PT[b:b + HD, 8 + c, T:TA], TC, None)
            grid_keys = (B.PT[b:b + HD, 8 + c, 0:T], T, B.rel[:, h, (7 - 2 * t) * 64:(15 - 2 * t) * 64])
            latent = t < TT
            items.append(Item(
                q=B.PT[b:b + HD, 4 + c, t * P:(t + 1) * P],
                segs=[grid_keys, ctx_keys] if latent else [ctx_keys],
                vs=[B.V[:, j, 512 + h * HD:512 + (h + 1) * HD] for j in range(0 if latent else TT, TA // P)],
                o=B.mixT[:, 4 + c, t * P:(t + 1) * P]))
    attend(nc, M, items, HD ** -0.5)


def fourier(nc, M, A, B):
    s = take(M, "tab ch ch_out tok tok_out")
    with ExitStack() as ctx:
        FT = ctx.enter_context(M.nc.sbuf_tensor(f"{M.blocks}_dft_t", [P, 2, TT, T], F32))
        G = ctx.enter_context(M.nc.sbuf_tensor(f"{M.blocks}_dft_g", [P, 16, 2 * P], F32))
        block = ctx.enter_context(nc.Block())

        @block.sync
        def _(sp):
            sp.dma_start(FT[:], A["dft_t"]).then_inc(s["tab"], 16)

        @block.tensor
        def _(pe):
            for n in range(16):
                g, t = n // TT, n % TT
                if n >= 4:
                    pe.wait_ge(s["ch_out"], n - 3)
                nc.tensor.matmul(M.PS[:, n % 4, 0:2 * P], B.PT[:, g, t * P:(t + 1) * P], B.K2[:, J_DFT:J_DFT + 2 * P],
                                 start=True, stop=True).then_inc(s["ch"], 1)
            pe.wait_ge(s["tab"], 16)
            for g in range(4):
                pe.wait_ge(s["ch_out"], 4 * g + 4)
                for t in range(TT):
                    for j in range(2):
                        mm = nc.tensor.matmul(M.PS[:, 4 + g, :], G[:, g * TT + t, j * P:(j + 1) * P], FT[:, j, t, :],
                                              start=(t + j == 0), stop=(t == TT - 1 and j == 1))
                mm.then_inc(s["tok"], 1)

        @block.scalar
        def _(act):
            for n in range(16):
                act.wait_ge(s["ch"], n + 1)
                nc.scalar.activation(G[:, n, :], M.PS[:, n % 4, 0:2 * P], ACT.Copy).then_inc(s["ch_out"], 1)
            for g in range(4):
                act.wait_ge(s["tok"], g + 1)
                nc.scalar.activation(B.mixT[:, g, :], M.PS[:, 4 + g, :], ACT.Copy).then_inc(s["tok_out"], 1)
    give(nc, s)


def gla_prepare(nc, M, A, B):
    s = take(M, "par rot turned step z lin e1 la ex exd step2")
    NC = TA // 64
    with ExitStack() as ctx:
        dw = ctx.enter_context(M.nc.sbuf_tensor(f"{M.blocks}_dec_w", [48, 256], F32))
        db = ctx.enter_context(M.nc.sbuf_tensor(f"{M.blocks}_dec_b", [P, 4], F32))
        t1 = ctx.enter_context(M.nc.sbuf_tensor(f"{M.blocks}_ax1", [P, T], F32))
        t2 = ctx.enter_context(M.nc.sbuf_tensor(f"{M.blocks}_ax2", [P, T], F32))
        la = ctx.enter_context(M.nc.sbuf_tensor(f"{M.blocks}_log_a", [P, 4, TA], F32))
        z = ctx.enter_context(M.nc.sbuf_tensor(f"{M.blocks}_dec_z", [P, 4, TA], F32))
        pre = ctx.enter_context(M.nc.sbuf_tensor(f"{M.blocks}_dec_pre", [P, 4, TA], F32))
        block = ctx.enter_context(nc.Block())

        @block.sync
        def _(sp):
            sp.dma_start(dw[0:16], A["dec_w"][0]).then_inc(s["par"], 16)
            sp.dma_start(dw[32:48], A["dec_w"][1]).then_inc(s["par"], 16)
            sp.dma_start(db[:], A["dec_b"]).then_inc(s["par"], 16)

        @block.tensor
        def _(pe):
            pe.wait_ge(s["par"], 48)
            for j in range(4):
                d, c = j // 2, j % 2
                if j >= 1:
                    pe.wait_ge(s["lin"], j)
                nc.tensor.matmul(M.PS[:, 0, :], dw[32 * d:32 * d + 16, c * P:(c + 1) * P],
                                 B.KA[32 * d:32 * d + 16, 2, 0:T], start=True, stop=True)
                nc.tensor.matmul(M.PS[:, 1, 0:TC], dw[32 * d:32 * d + 16, c * P:(c + 1) * P],
                                 B.KA[32 * d:32 * d + 16, 2, T:TA], start=True, stop=True).then_inc(s["z"], 1)
            for j in range(4):
                x = B.PT[:, 4 + j, 0:T] if j < 2 else B.KA[:, j - 2, 0:T]
                nc.tensor.matmul(M.PS[:, 2 + j, :], B.K2[:, J_ROT:J_ROT + P], x, start=True,
                                 stop=True).then_inc(s["rot"], 1)

        @block.vector
        def _(dve):
            step = Steps(dve, s["step"])
            tt, ts, stt = nc.vector.tensor_tensor, nc.vector.tensor_scalar, nc.vector.scalar_tensor_tensor
            dve.wait_ge(s["par"], 48)
            for j in range(4):
                dve.wait_ge(s["z"], j + 1)
                step(ts(z[:, j, 0:T], M.PS[:, 0, :], db[:, j:j + 1], None, ALU.add))
                ts(z[:, j, T:TA], M.PS[:, 1, 0:TC], db[:, j:j + 1], None, ALU.add).then_inc(s["lin"], 1)
                dve.wait_ge(s["lin"], j + 1)
                stt(out=la[:, j, :], in0=z[:, j, :], scalar=-1.0, in1=z[:, j, :], op0=ALU.mult,
                    op1=ALU.max).then_inc(s["e1"], 1)
            for j in range(4):
                x = B.PT[:, 4 + j, 0:T] if j < 2 else B.KA[:, j - 2, 0:T]
                dve.wait_ge(s["rot"], j + 1)
                step(tt(t1[:], x, B.K2[:, J_COS:J_COS + T], ALU.mult))
                step(tt(t2[:], M.PS[:, 2 + j, :], B.K2[:, J_SIN:J_SIN + T], ALU.mult))
                step(tt(x, t1[:], t2[:], ALU.add))
            for j in range(4):
                d = j // 2
                dve.wait_ge(s["la"], j + 1)
                step(stt(out=la[:, j, :], in0=z[:, j, :], scalar=0.0, in1=la[:, j, :], op0=ALU.min, op1=ALU.subtract))
                step(ts(la[:, j, :], la[:, j, :], 1.0 / 16, None, ALU.mult))
                step(nc.vector.tensor_tensor_scan(out=pre[:, j, :], data0=B.K2[:, J_RST:J_RST + TA], data1=la[:, j, :],
                                                  initial=0.0, op0=ALU.mult, op1=ALU.add))
                p3 = pre[:, j, :].rearrange("p (n l) -> p n l", l=64)
                z3 = z[:, j, :].rearrange("p (n l) -> p n l", l=64)
                total = p3[:, :, 63:64].to_broadcast([P, NC, 64])
                step(nc.vector.tensor_copy(B.dec[:, j, :], p3[:, :, 63]))
                if d == 0:
                    tt(z3, total, p3, ALU.subtract).then_inc(s["ex"], 1)
                else:
                    step(tt(z3, total, p3, ALU.subtract))
                    step(tt(t1[:], z[:, j, 0:T], la[:, j, 0:T], ALU.add))
                    step(tt(z[:, j, :], pre[:, j, :], la[:, j, :], ALU.subtract))
                    nc.vector.tensor_copy(pre[:, j, 0:T], t1[:]).then_inc(s["ex"], 1)
            for j in range(4):
                c = j % 2
                dve.wait_ge(s["exd"], j + 1)
                step(stt(out=B.qe[:, j, :], in0=B.PT[:, 4 + c, 0:T], scalar=64 ** -0.5, in1=B.qe[:, j, :],
                         op0=ALU.mult, op1=ALU.mult))
                step(tt(B.ke[:, j, :], B.KA[:, c, 0:T], B.ke[:, j, :], ALU.mult))
                step(tt(B.kd[:, j, :], B.KA[:, c, :], B.kd[:, j, :], ALU.mult))

        @block.scalar
        def _(act):
            step = Steps(act, s["step2"])
            for j in range(4):
                act.wait_ge(s["e1"], j + 1)
                step(nc.scalar.activation(la[:, j, :], la[:, j, :], ACT.Exp, scale=-1.0))
            for j in range(4):
                nc.scalar.activation(la[:, j, :], la[:, j, :], ACT.Ln, bias=1.0).then_inc(s["la"], 1)
            for j in range(4):
                act.wait_ge(s["ex"], j + 1)
                step(nc.scalar.activation(B.dec[:, j, :], B.dec[:, j, :], ACT.Exp))
                step(nc.scalar.activation(B.qe[:, j, :], pre[:, j, 0:T], ACT.Exp))
                step(nc.scalar.activation(B.ke[:, j, :], pre[:, j, 0:T], ACT.Exp, scale=-1.0))
                nc.scalar.activation(B.kd[:, j, :], z[:, j, :], ACT.Exp).then_inc(s["exd"], 1)
            for c in range(4):
                nc.scalar.activation(B.PT[:, 6 + c, 0:T], B.PT[:, 6 + c, 0:T], ACT.Silu)
    give(nc, s)


def gla_states(nc, M, B):
    s = take(M, "tr tr_out kv kv_free state")
    NT = TA // P
    with ExitStack() as ctx:
        kt = ctx.enter_context(M.nc.sbuf_tensor(f"{M.blocks}_kd_tok", [P, 2, NT, 256], F32))
        S = ctx.enter_context(M.nc.sbuf_tensor(f"{M.blocks}_state", [P, 2, 2, P], F32))
        block = ctx.enter_context(nc.Block())

        def bank(c, n):
            m = n // 2
            return M.PS[:, 4 * (n % 2) + 2 * c + m // 4, (m % 4) * P:(m % 4 + 1) * P]

        @block.tensor
        def _(pe):
            for d in range(2):
                if d:
                    pe.wait_ge(s["kv_free"], 1)
                for t in range(NT):
                    n = d * NT + t
                    if t >= 2:
                        pe.wait_ge(s["tr_out"], n - 1)
                    for c in range(2):
                        mm = nc.tensor.transpose(M.PS[:, t % 2, c * P:(c + 1) * P], B.kd[:, 2 * d + c, t * P:(t + 1) * P],
                                                 M.K[:, K_ID:K_ID + P])
                    mm.then_inc(s["tr"], 1)
                pe.wait_ge(s["tr_out"], (d + 1) * NT)
                for odd in range(2):
                    for n in range(odd, 2 * NT, 2):
                        for h in range(4):
                            b, r = 64 * (h % 2), 64 * odd
                            mm = nc.tensor.matmul(bank(h // 2, n)[b:b + 64], kt[r:r + 64, d, n // 2, h * 64:(h + 1) * 64],
                                                  B.V[r:r + 64, n // 2, h * P:(h + 1) * P], start=True, stop=True)
                mm.then_inc(s["kv"], 1)

        @block.scalar
        def _(act):
            for d in range(2):
                for t in range(NT):
                    act.wait_ge(s["tr"], d * NT + t + 1)
                    nc.scalar.activation(kt[:, d, t, :], M.PS[:, t % 2, 0:256], ACT.Copy).then_inc(s["tr_out"], 1)

        @block.vector
        def _(dve):
            done = 0
            for d in range(2):
                dve.wait_ge(s["kv"], d + 1)
                order = [8, 9, 10, 11] + list(range(8))
                if d:
                    order = [11, 10, 9, 8] + list(range(7, -1, -1))
                for i, n in enumerate(order[:-1]):
                    nxt = order[i + 1]
                    for c in range(2):
                        out = B.Sp[:, d, c, nxt, :] if nxt < 8 else S[:, c, i % 2, :]
                        if i == 0:
                            ins = nc.vector.tensor_copy(out, bank(c, n))
                        else:
                            cur = B.Sp[:, d, c, n, :] if n < 8 else S[:, c, (i - 1) % 2, :]
                            dve.wait_ge(s["state"], done - 1)
                            ins = nc.vector.scalar_tensor_tensor(out=out, in0=cur, scalar=B.dec[:, 2 * d + c, n:n + 1],
                                                                 in1=bank(c, n), op0=ALU.mult, op1=ALU.add)
                        ins.then_inc(s["state"], 1)
                        done += 1
                dve.wait_ge(s["state"], done)
                dve.sem_inc(s["kv_free"], 1)
    give(nc, s)


def gla_outputs(nc, M, A, B):
    s = take(M, "par att masked pv sq ssum sd rstd norm done")
    with ExitStack() as ctx:
        am = ctx.enter_context(M.nc.sbuf_tensor(f"{M.blocks}_gla_att", [P, 2, 2 * P], F32))
        hw = ctx.enter_context(M.nc.sbuf_tensor(f"{M.blocks}_gla_hw", [P, 2], F32))
        sq = ctx.enter_context(M.nc.sbuf_tensor(f"{M.blocks}_gla_sq", [P, 4, T], F32))
        nm = ctx.enter_context(M.nc.sbuf_tensor(f"{M.blocks}_gla_nm", [P, 4, T], F32))
        block = ctx.enter_context(nc.Block())
        N = 4 * TT

        @block.sync
        def _(sp):
            sp.dma_start(hw[:, 0:1], A["head_w"]).then_inc(s["par"], 16)

        @block.tensor
        def _(pe):
            def scores(n):
                h, t = n // TT, n % TT
                b, c = 64 * (h % 2), h // 2
                if n >= 2:
                    pe.wait_ge(s["masked"], n - 1)
                for d in range(2):
                    mm = nc.tensor.matmul(M.PS[:, n % 2, d * P:(d + 1) * P], B.ke[b:b + 64, 2 * d + c, t * P:(t + 1) * P],
                                          B.qe[b:b + 64, 2 * d + c, t * P:(t + 1) * P], start=True, stop=True)
                mm.then_inc(s["att"], 1)

            def values(n):
                h, t = n // TT, n % TT
                b, c = 64 * (h % 2), h // 2
                pe.wait_ge(s["masked"], n + 1)
                for d in range(2):
                    nc.tensor.matmul(M.PS[:, 2 + h, t * P:(t + 1) * P], B.V[:, t, h * P:(h + 1) * P],
                                     am[:, n % 2, d * P:(d + 1) * P], start=(d == 0), stop=False)
                for d in range(2):
                    for j in range(2):
                        at = t * P + j * 64
                        last = d == 1 and j == 1
                        mm = nc.tensor.matmul(M.PS[:, 2 + h, at:at + 64], B.Sp[b:b + 64, d, c, 2 * t + j, :],
                                              B.qe[b:b + 64, 2 * d + c, at:at + 64], start=False, stop=last)
                mm.then_inc(s["pv"], 1)

            for n in range(N + 1):
                if n < N:
                    scores(n)
                if n >= 1:
                    values(n - 1)
            for h in range(4):
                pe.wait_ge(s["sq"], h + 1)
                if h >= 2:
                    pe.wait_ge(s["sd"], h - 1)
                nc.tensor.matmul(M.PS[:, 6 + h % 2, :], M.K[:, K_ONE:K_ONE + P], sq[:, h, :], start=True,
                                 stop=True).then_inc(s["ssum"], 1)

        @block.vector
        def _(dve):
            for n in range(N):
                dve.wait_ge(s["att"], n + 1)
                if n >= 2:
                    dve.wait_ge(s["pv"], n - 1)
                nc.vector.tensor_tensor(am[:, n % 2, :], M.PS[:, n % 2, 0:2 * P], B.K2[:, J_MASK:J_MASK + 2 * P],
                                        ALU.mult).then_inc(s["masked"], 1)
            dve.wait_ge(s["par"], 16)
            for h in range(4):
                dve.wait_ge(s["sd"], h + 1)
                nc.vector.reciprocal(sq[:, h, :], sq[:, h, :]).then_inc(s["rstd"], 1)
                dve.wait_ge(s["rstd"], h + 1)
                nc.vector.tensor_tensor(nm[:, h, :], M.PS[:, 2 + h, :], sq[:, h, :], ALU.mult).then_inc(s["norm"], 1)
                dve.wait_ge(s["norm"], h + 1)
                nc.vector.scalar_tensor_tensor(out=B.mixT[:, 4 + h, :], in0=nm[:, h, :], scalar=hw[:, 0:1],
                                               in1=B.PT[:, 6 + h, 0:T], op0=ALU.mult, op1=ALU.mult).then_inc(s["done"], 1)

        @block.scalar
        def _(act):
            for h in range(4):
                act.wait_ge(s["pv"], TT * (h + 1))
                nc.scalar.activation(sq[:, h, :], M.PS[:, 2 + h, :], ACT.Square).then_inc(s["sq"], 1)
            for h in range(4):
                act.wait_ge(s["ssum"], h + 1)
                nc.scalar.activation(sq[:, h, :], M.PS[:, 6 + h % 2, :], ACT.Sqrt, bias=M.eps[:, 1:2],
                                     scale=1.0 / P).then_inc(s["sd"], 1)
    give(nc, s)


def feed_forward(nc, M, A, i, spans, rounds):
    with ExitStack() as ctx:
        def tensor(name, shape, dt, where=ctx):
            return where.enter_context(M.nc.sbuf_tensor(f"ffn{i}_{name}", shape, dt))

        TW = sum(n for _, n, _ in spans)
        M.hR = tensor("h_parts", [P, 2, KD, TW], F32R)
        with ExitStack() as inner:
            M.hT = tensor("hT", [P, KD, TW], F32, inner)
            rms_modulate(nc, M, A["norm_ffn"][i], spans, 3, 4)
        hid = tensor("hidden", [P, 2, max(rounds), TW], F32R)
        f0 = 0
        for r, NF in enumerate(rounds):
            gated_up(nc, M, lambda n: A["f_gu"][i, n + f0], hid, NF, [(t, n) for t, n, _ in spans])
            ride = None
            if i == 0:
                per = N_MOD // len(rounds) // KD
                ride = (modulation(A, 3, per), A["b_ada"][3], A["cond"][1], r * KD * per, per)
            gemm_residual(nc, M, lambda n: A["f_down"][i, n, :, f0:f0 + NF], hid, NF, spans, 5, 1.0, ride=ride)
            f0 += NF


def block_two(nc, M, A):
    both = [(0, T, 0), (T, TC, 1)]
    latent = both[:1]

    def tensor(ctx, name, shape, dt=F32):
        return ctx.enter_context(M.nc.sbuf_tensor("two_" + name, shape, dt))

    adopt(nc, M, (1, 4))
    with ExitStack() as ctx:
        B = Buffers()
        B.PT, B.V = tensor(ctx, "ab_projT", [P, 12, TA]), tensor(ctx, "ab_values", [P, TA // P, 1024])
        with ExitStack() as inner:
            M.hR = tensor(inner, "ab_h_parts", [P, 2, KD, TA], F32R)
            M.hT = tensor(inner, "ab_hT", [P, KD, TA])
            rms_modulate(nc, M, A["norm_mix"][0], both, 0, 1)
            project(nc, M, lambda n: A["ab_t"][n], 12, B.PT, [(0, T), (T, TC)], A["ab_v"], 2, B.V, TA // P)
        B.mixT = tensor(ctx, "ab_mixT", [P, KD, TA])
        with ExitStack() as inner:
            B.rel = tensor(inner, "rel", [P, 8, 16 * 64])
            spatial_gate(nc, M, A, B)
            attend2(nc, M, B)
        M.hR = tensor(ctx, "ab_mix_parts", [P, 2, KD, TA], F32R)
        gemm_residual(nc, M, lambda n: A["ab_out"][n], M.hR, KD, both, 2, 1.0, mix=B.mixT)
    feed_forward(nc, M, A, 0, both, (8, 8, 6))

    adopt(nc, M, (1, 4))
    with ExitStack() as ctx:
        B = Buffers()
        B.PT, B.KA = tensor(ctx, "cd_projT", [P, 10, T]), tensor(ctx, "cd_keysT", [P, 3, TA])
        B.V, B.K2 = tensor(ctx, "cd_values", [P, TA // P, 512]), tensor(ctx, "cd_consts", [P, J_N])
        with ExitStack() as inner:
            M.hR = tensor(inner, "cd_h_parts", [P, 2, KD, TA], F32R)
            M.hT = tensor(inner, "cd_hT", [P, KD, TA])
            rms_modulate(nc, M, A["norm_mix"][1], both, 0, 1)
            project(nc, M, lambda n: A["cd_t"][n], 10, B.PT, [(0, T)])
            project(nc, M, lambda n: A["cd_k"][n], 3, B.KA, [(0, T), (T, TC)], A["cd_v"], 1, B.V, TA // P,
                    [(B.K2[:], A["consts2"])])
        B.mixT = tensor(ctx, "cd_mixT", [P, KD, T])
        with ExitStack() as inner:
            fourier(nc, M, A, B)
            B.qe, B.ke = tensor(inner, "qe", [P, 4, T]), tensor(inner, "ke", [P, 4, T])
            B.kd, B.dec = tensor(inner, "kd", [P, 4, TA]), tensor(inner, "dec", [P, 4, TA // 64])
            gla_prepare(nc, M, A, B)
            B.Sp = tensor(inner, "Sp", [P, 2, 2, 8, P])
            gla_states(nc, M, B)
            gla_outputs(nc, M, A, B)
        M.hR = tensor(ctx, "cd_mix_parts", [P, 2, KD, T], F32R)
        gemm_residual(nc, M, lambda n: A["cd_out"][n], M.hR, KD, latent, 2, 1.0, mix=B.mixT)
    feed_forward(nc, M, A, 1, latent, (12, 10))
    M.hT = M.xT
    rms_modulate(nc, M, A["final_w"], latent)


def program(nc, A, out, parts=2):
    with ExitStack() as ctx:
        def sb(name, shape):
            return ctx.enter_context(nc.sbuf_tensor(name, shape, F32))

        M = Buffers()
        M.nc, M.blocks = nc, 0
        M.PS = ctx.enter_context(nc.psum_tensor("PS", [P, 8, 512], F32))
        M.xT = sb("xT", [P, KD, TA])
        M.K = sb("consts", [P, K_N])
        M.mod, M.mod_next = sb("mod", [P, 2 * N_MOD]), sb("mod_next", [P, 2 * N_MOD])
        M.eps = sb("eps", [P, 2])
        s = take(M, "eps_in stored")
        with nc.Block() as block:
            @block.vector
            def _(dve):
                nc.vector.memset(M.eps[:, 0:1], EPS).then_inc(s["eps_in"], 1)
                nc.vector.memset(M.eps[:, 1:2], RMS_EPS).then_inc(s["eps_in"], 1)
        give(nc, s)
        block_one(nc, M, A)
        if parts > 1:
            block_two(nc, M, A)
        s = take(M, "stored")
        with nc.Block() as block:
            @block.sync
            def _(sp):
                sp.dma_start(out, M.xT[:, :, 0:T]).then_inc(s["stored"], 16)
                sp.wait_ge(s["stored"], 16)
        give(nc, s)



def consts():
    K = np.zeros((P, K_N), np.float32)
    i = np.arange(P)
    K[:, K_ID:K_ID + P] = np.eye(P)
    rot = np.zeros((P, P))
    for m in range(P):
        rot[m + HALF if m % HD < HALF else m - HALF, m] = -1.0 if m % HD < HALF else 1.0
    K[:, K_ROT:K_ROT + P] = rot
    K[:, K_ONE:K_ONE + P] = 1.0
    K[:, K_MEAN:K_MEAN + P] = 1.0 / D
    K[:, K_RANK:K_RANK + NE] = NE - np.arange(NE)
    K[:, K_RANK + NE:K_RANK + NE + NG] = NG - np.arange(NG)
    K[:, K_FREQ] = np.float32(10000.0) ** (-(i % HALF).astype(np.float32) / np.float32(HALF))
    return K


def consts2():
    K = np.zeros((P, J_N), np.float32)
    i = np.arange(P)
    for m in range(P):
        K[m + 16 if m % 32 < 16 else m - 16, J_ROT + m] = -1.0 if m % 32 < 16 else 1.0
    same = i[:, None] // 64 == i[None] // 64
    K[:, J_MASK:J_MASK + P] = same & (i[:, None] <= i[None])
    K[:, J_MASK + P:J_MASK + 2 * P] = same & (i[:, None] >= i[None])
    t = np.arange(T, dtype=np.float32)
    pos = np.where((i % 64 < 32)[:, None], t[None] // 64, t[None] % 64).astype(np.float32)
    freq = (np.float32(10000.0) ** (-(i % 16).astype(np.float32) / np.float32(16))).astype(np.float32)
    ang = (pos * freq[:, None]).astype(np.float32).astype(np.float64)
    K[:, J_COS:J_COS + T], K[:, J_SIN:J_SIN + T] = np.cos(ang), np.sin(ang)
    K[:, J_RST:J_RST + TA] = np.arange(TA) % 64 != 0
    ang = 2 * np.pi * ((i[:, None] * i[None]) % P) / P
    K[:, J_DFT:J_DFT + P] = np.cos(ang) / 256
    K[:, J_DFT + P:J_DFT + 2 * P] = -np.sin(ang) / 256
    return K


def chunks(w, width=P):
    *lead, r, c = w.shape
    w = w.reshape(*lead, r // P, P, c // width, width)
    n = len(lead)
    return np.ascontiguousarray(w.transpose(*range(n), n + 2, n + 1, n, n + 3))


def mixer_consts():
    L = np.zeros((P, L_N), np.float32)
    i = np.arange(P)
    d = np.arange(T)[None] - i[:, None]
    for h in range(NH_R):
        L[:, h * T:(h + 1) * T] = np.where(d >= 0, np.exp(np.maximum(d, 0) * math.log1p(-2.0 ** (-5 - h))), 0)
    L[:, L_HEAD:L_HEAD + P] = (i[:, None] // HD == i[None] // HD) / HD
    L[:, L_UP:L_UP + P] = i[:, None] <= i[None]
    for h in range(NH_M):
        L[h, L_SELH + h * P:L_SELH + (h + 1) * P] = 1.0
        L[h, L_SELP + h * HD:L_SELP + (h + 1) * HD] = 1.0
    return L


def cols(v):
    return np.ascontiguousarray(np.swapaxes(v.reshape(*v.shape[:-1], -1, P), -1, -2))


def feats(x):
    return np.ascontiguousarray(x.T.reshape(-1, P, x.shape[0]).transpose(1, 0, 2))


def layout(i):
    a = {}
    w = i["w_in"]
    o = np.cumsum([0, 512, 512, 512, 256, 64, 4, 256, 256, 256, 256, 256, 256, 256, 256, 4, 4])
    aq, ak, av, iq, ik, iw, rq, rk, rv, rg, mq, mk, mv, mo, mi, mf = (w[:, :, o[j]:o[j + 1]] for j in range(16))
    gates = np.zeros((DEPTH, D, P), np.float32)
    gates[:, :, 0:4], gates[:, :, 32:36] = mi, mf
    a["w_in_t"] = chunks(np.concatenate([aq, ak, iq, ik, ik, rq, rk, rg, mq, mk, mo, gates], axis=2))
    a["w_in_v"] = chunks(np.concatenate([av, rv, mv], axis=2), 512)
    a["w_in_i"] = chunks(iw, NH_I)[:, 0]
    ada_w = np.stack([i["w_ada"][0], i["w_ada"][1], i["ada_w_2"][0], i["ada_w_2"][1]])
    a["w_ada"] = np.ascontiguousarray(ada_w.transpose(0, 2, 1)).reshape(2 * DEPTH * N_MOD, P, D)
    a["b_ada"] = np.repeat(cols(np.concatenate([i["b_ada"], i["ada_b_2"]])), 2, axis=2)
    cw = np.concatenate([i["conv_w"], i["conv_b"][:, None]], axis=1)
    a["conv"] = np.ascontiguousarray(cw.reshape(DEPTH, CONV + 1, 4, P).transpose(0, 3, 2, 1))
    a["gate_b"] = np.ascontiguousarray(np.stack([i["i_bias"], i["f_bias"]], axis=2))
    a["w_out"] = chunks(i["w_out"])
    for n in ("mix", "ffn"):
        a["ln_" + n] = np.ascontiguousarray(np.stack([cols(i[f"ln_{n}_g"]), cols(i[f"ln_{n}_b"])], axis=2))
    a["w_router"] = chunks(i["w_router"], NE)[0]
    a["b_router"] = i["b_router"]
    a["w_gu"] = np.concatenate([chunks(i["w_gate"]), chunks(i["w_up"])], axis=4).reshape(DEPTH, NE * 2, P, 2 * KD, P)
    a["w_down"] = chunks(i["w_down"].reshape(DEPTH, NE * FE, D))
    a["consts"] = consts()
    a["mixer_consts"] = mixer_consts()
    a["positions"] = i["positions"][0]
    a["cond"] = np.stack([np.stack([i["c"][0], i["c"][0]]), np.stack([i["c_2"][0], i["c_ctx_2"]])])
    a["x"] = feats(i["x"][0])
    a["ctx"] = feats(i["ctx_2"][0])
    a["norm_mix"], a["norm_ffn"] = cols(i["norm_mix_w_2"]), cols(i["norm_ffn_w_2"])
    a["final_w"] = cols(i["final_norm_w_2"])
    u, v, q, k, nv = np.split(i["ab_w_in_2"][0], 5, axis=1)
    a["ab_t"] = chunks(np.concatenate([u, q, k], axis=1))
    a["ab_v"] = chunks(np.concatenate([v, nv], axis=1), 512)
    a["ab_out"] = chunks(i["ab_w_out_2"][0])
    a["sgu_w"] = np.ascontiguousarray(i["ab_sgu_w_2"][0].transpose(2, 0, 1))
    a["sgu_b"] = np.ascontiguousarray(i["ab_sgu_b_2"][0].reshape(-1))
    a["sgu_nw"] = cols(i["ab_sgu_norm_w_2"][0])
    c = np.arange(64)
    start = np.clip(c - 8, 0, 48)
    seen = (c[None] >= start[:, None]) & (c[None] < start[:, None] + 16)
    rel = i["ab_rel_bias_2"][0][:, :, np.clip(c[None] - c[:, None] + 15, 0, 30)]
    rel = np.where(seen, rel, np.float32(NEG)).transpose(2, 0, 1, 3)
    a["rel"] = np.zeros((P, 8, 16, 64), np.float32)
    a["rel"][0:64, :, 0:15] = rel
    a["rel"][64:, :, 1:16] = rel
    a["rel"] = a["rel"].reshape(P, 8, 1024)
    w = i["cd_w_in_2"][0]
    f, q, k, v, g, al = np.split(w, np.cumsum([512, 256, 256, 512, 512]), axis=1)
    a["cd_t"] = chunks(np.concatenate([f, q, g], axis=1))
    low = np.zeros((D, P), np.float32)
    low[:, 0:16], low[:, 32:48] = al[:, 0:16], al[:, 16:32]
    a["cd_k"] = chunks(np.concatenate([k, low], axis=1))
    a["cd_v"] = chunks(v, 512)
    a["cd_out"] = chunks(i["cd_w_out_2"][0])
    a["dec_w"] = np.ascontiguousarray(np.stack([i["cd_decay_w_fwd_2"][0], i["cd_decay_w_bwd_2"][0]]))
    a["dec_b"] = cols(np.concatenate([i["cd_decay_b_fwd_2"][0], i["cd_decay_b_bwd_2"][0]]))
    a["head_w"] = np.ascontiguousarray(i["cd_head_norm_w_2"].reshape(P, 1))
    a["f_gu"] = np.concatenate([chunks(i["ffn_w_gate_2"]), chunks(i["ffn_w_up_2"])], axis=3)
    a["f_down"] = chunks(i["ffn_w_down_2"])
    a["consts2"] = consts2()
    ang = 2 * np.pi * ((np.arange(T)[:, None] * np.arange(T)[None]) % T) / T
    dft = np.stack([np.cos(ang), np.sin(ang)]).astype(np.float32)
    a["dft_t"] = np.ascontiguousarray(dft.reshape(2, TT, P, T).transpose(2, 0, 1, 3))
    return a


def kernel(**inputs):
    import concourse.bacc as bacc
    from concourse.bass_utils import run_bass_kernel_spmd as run

    arrays = layout({k: np.asarray(v) for k, v in inputs.items()})
    nc = bacc.Bacc("TRN2", target_bir_lowering=False, num_devices=1)
    A = {n: nc.dram_tensor("in_" + n, a.shape, mybir.dt.from_np(a.dtype), kind="ExternalInput").ap()
                           for n, a in arrays.items()}
    out = nc.dram_tensor("out_x", (P, KD, T), F32, kind="ExternalOutput").ap()
    program(nc, A, out)
    r = run(nc, [{"in_" + n: a for n, a in arrays.items()}], core_ids=[0])
    y = r.results[0]["out_x"]
    return np.ascontiguousarray(y.transpose(2, 1, 0)).reshape(1, T, D)
```

```python
import math
from contextlib import ExitStack

import numpy as np
import concourse.bass as bass
from concourse import mybir

F32 = mybir.dt.float32
I32 = mybir.dt.int32
F32R = mybir.dt.float32r
ALU = mybir.AluOpType
ACT = mybir.ActivationFunctionType
AX = mybir.AxisListType

P = 128
D = 1024
KD = D // P
T = 512
TT = T // P
TC = 256
TA = T + TC
DEPTH = 2
HD = 64
HALF = HD // 2
NH_A, NH_I, NH_R, NH_M = 8, 4, 4, 4
TOPK = 128
CONV = 4
NE, NG, EPG, FE = 16, 4, 4, 256
EPS = 1e-5
RMS_EPS = 1e-6
ALPHA = (2.0 * DEPTH) ** 0.25
NEG = -1.0e30
MAGIC = 12582912.0
TWO_PI = (6.28125, 0.0019350051879882812, 3.019915981956753e-07)
PI_IN = 3.1415925

C_AQ, C_AK, C_IQ, C_IK, C_RQ, C_RK, C_RG, C_MQ, C_MK, C_MO, C_G = 0, 4, 8, 10, 11, 13, 15, 17, 19, 21, 23
N_ROPE = 15
N_CH = 24
N_MOD = 6 * KD
N_V = 1024
V_A, V_R, V_M = 0, 512, 768
ROUNDS = 2
VC = 256

K_ID, K_ROT, K_ONE, K_MEAN = (P * i for i in range(4))
K_RANK = 4 * P
K_FREQ = K_RANK + NE + NG
K_N = K_FREQ + 1

L_HEAD = NH_R * T
L_UP = L_HEAD + P
L_SELH = L_UP + P
L_SELP = L_SELH + NH_M * P
L_N = L_SELP + NH_M // 2 * P

J_ROT, J_MASK, J_COS, J_SIN, J_RST = 0, P, 3 * P, 3 * P + T, 3 * P + 2 * T
J_DFT = J_RST + TA
J_N = J_DFT + 2 * P
FFN = 2816


class Buffers:
    pass


class Item:

    def __init__(self, q, segs, vs, o):
        self.q, self.segs, self.vs, self.o = q, segs, vs, o


class Steps:

    def __init__(self, eng, sem):
        self.eng, self.sem, self.n = eng, sem, 0

    def __call__(self, ins):
        ins.then_inc(self.sem, 1)
        self.n += 1
        self.eng.wait_ge(self.sem, self.n)


def take(M, names):
    M.blocks += 1
    return {n: M.nc.alloc_semaphore(f"b{M.blocks}_{n}") for n in names.split()}


def give(nc, s, weights_in=()):
    for w in weights_in:
        nc.gpsimd.sem_clear(w)
    nc.clear_and_free_semaphores(list(s.values()))
    nc.all_engine_barrier()


def setup(nc, M, A):
    s = take(M, "loaded stream step table sines kept r0 r1 bias_in cond_in sig summed added")
    NB = 4
    with ExitStack() as ctx:
        R = Modulation(nc, M, ctx, s, modulation(A, 0, NB), A["b_ada"][0], A["cond"][0], 0, NB, 1)
        pi = ctx.enter_context(M.nc.sbuf_tensor(f"{M.blocks}_pos_int", [P, T], I32))
        ang = ctx.enter_context(M.nc.sbuf_tensor(f"{M.blocks}_angle", [P, T], F32))
        turns = ctx.enter_context(M.nc.sbuf_tensor(f"{M.blocks}_turns", [P, T], F32))
        r = ctx.enter_context(M.nc.sbuf_tensor(f"{M.blocks}_reduced", [P, 2, T], F32))
        block = ctx.enter_context(nc.Block())

        @block.sync
        def _(sp):
            sp.dma_start(M.K[:], A["consts"]).then_inc(s["loaded"], 16)
            sp.dma_start(pi[:], A["positions"].partition_broadcast(P)).then_inc(s["loaded"], 16)
            R.load(sp)
            R.load_first(sp)
            with sp.Fori(1, N_MOD // NB // 2) as i:
                for u in range(2):
                    R.load_next(sp, i, u)
            sp.dma_start(M.xT[:, :, 0:T], A["x"]).then_inc(s["stream"], 16)
            load_first(sp, M, proj_weights(A, 0), M.weights_in[M.turn])
            sp.dma_start(M.xT[:, :, T:TA], A["ctx"]).then_inc(s["stream"], 16)
            sp.wait_ge(s["stream"], 32)

        @block.vector
        def _(dve):
            step = Steps(dve, s["step"])
            dve.wait_ge(s["loaded"], 32)
            step(nc.vector.tensor_copy(r[:, 0, :], pi[:]))
            step(nc.vector.tensor_scalar(ang[:], r[:, 0, :], M.K[:, K_FREQ:K_FREQ + 1], None, ALU.mult))
            for j, quarter in enumerate((0.25, 0.0)):
                step(nc.vector.tensor_scalar(turns[:], ang[:], float(1 / (2 * math.pi)), quarter, ALU.mult, ALU.add))
                step(nc.vector.tensor_scalar(turns[:], turns[:], MAGIC, None, ALU.add))
                step(nc.vector.tensor_scalar(turns[:], turns[:], -MAGIC, None, ALU.add))
                src = ang[:]
                for c in TWO_PI:
                    step(nc.vector.scalar_tensor_tensor(out=r[:, j, :], in0=turns[:], scalar=-c, in1=src,
                                                        op0=ALU.mult, op1=ALU.add))
                    src = r[:, j, :]
                if quarter:
                    step(nc.vector.tensor_scalar(r[:, j, :], r[:, j, :], math.pi / 2, None, ALU.add))
                step(nc.vector.tensor_scalar(r[:, j, :], r[:, j, :], -PI_IN, PI_IN, ALU.max, ALU.min))
            nc.vector.tensor_scalar(r[:, 0, :], r[:, 0, :], 1.0, None, ALU.mult).then_inc(s["table"], 1)
            R.conditions(dve)
            with dve.Fori(0, N_MOD // NB // 2) as i:
                for u in range(2):
                    R.chunks(dve, i, u)

        @block.scalar
        def _(act):
            R.sigmoid(act)
            act.wait_ge(s["table"], 1)
            nc.scalar.activation(r[:, 0, :], r[:, 0, :], ACT.Sin).then_inc(s["sines"], 1)
            nc.scalar.activation(r[:, 1, :], r[:, 1, :], ACT.Sin).then_inc(s["sines"], 1)
            act.wait_ge(s["sines"], 2)
            act.dma_start(M.rope, r[:]).then_inc(s["kept"], 16)
            act.wait_ge(s["kept"], 16)
    give(nc, s)


def modulation(A, layer, n):
    def w(c):
        return A["w_ada"][bass.ds(c + layer * N_MOD, n)].rearrange("c p k -> p c k")
    return w


def modcol(M, part, k, c=0):
    j = (part * KD + k) * 2 + c
    return M.mod[:, j:j + 1]


def halves(t):
    return t[:, 0], t[:, 1]


def products(nc, terms, low_ready):
    for out, pairs in terms:
        for j, (w, x) in enumerate(pairs):
            nc.tensor.matmul(out, w[0], x[1], start=(j == 0), stop=False)
            nc.tensor.matmul(out, w[0], x[0], start=False, stop=False)
    low_ready()
    for out, pairs in terms:
        for j, (w, x) in enumerate(pairs):
            mm = nc.tensor.matmul(out, w[1], x[0], start=False, stop=(j == len(pairs) - 1))
    return mm


def products_moving(nc, terms, low_ready):
    for out, pairs in terms:
        for j, (w, x) in enumerate(pairs):
            nc.tensor.matmul(out, x[0], w[0], start=(j == 0), stop=False)
            nc.tensor.matmul(out, x[1], w[0], start=False, stop=False)
    low_ready()
    for out, pairs in terms:
        for j, (w, x) in enumerate(pairs):
            mm = nc.tensor.matmul(out, x[0], w[1], start=False, stop=(j == len(pairs) - 1))
    return mm


def blocks(t, k):
    return t[0][:, k], t[1][:, k]


def tokens(t, k, t0, nt):
    return t[:, 0, k, t0:t0 + nt], t[:, 1, k, t0:t0 + nt]


STREAM = "used high_done split_done "


def raw_slots(M, KP):
    return M.raw[:, :, 0:KP * P].rearrange("p u (k q) -> p u k q", q=P)


def load_first(sp, M, weights, ready):
    w, KP = weights
    for u in range(2):
        sp.dma_start(raw_slots(M, KP)[:, u], w(u)).then_inc(ready[u], 16)


def proj_weights(A, l):
    return lambda n: A["w_proj"][n + l * N_CH], KD


def value_weights(A, l):
    return lambda n: A["w_in_v"][l, n], 2 * KD


def down_weights(A, l, r, NF):
    return lambda n: A["w_down"][l, n, :, r * NF:(r + 1) * NF], NF


def gate_up_weights(A, l, r, NF):
    return lambda n: A["w_gu"][l, n + r * NF], 2 * KD


def out_weights(A, l):
    return lambda n: A["w_out"][l, n], KD


class Stream:

    def __init__(self, nc, M, ctx, s, weights, N, following):
        self.nc, self.s, self.N, self.following = nc, s, N, following
        self.w, KP = weights
        self.M, self.raw = M, raw_slots(M, KP)
        self.ready = M.weights_in[M.turn]
        M.turn = (M.turn + 1) % len(M.weights_in)
        self.next_ready = M.weights_in[M.turn]
        self.part = ctx.enter_context(nc.sbuf_tensor(f"{M.blocks}_w_part", [P, 2, 2, KP, P], F32R))
        self.pairs = N // 2

    def load(self, sp):
        if self.pairs > 1:
            with sp.Fori(1, self.pairs) as i:
                for u in range(2):
                    sp.wait_ge(self.s["split_done"], 2 * i + u - 1)
                    sp.dma_start(self.raw[:, u], self.w(2 * i + u)).then_inc(self.ready[u], 16)
        if self.N % 2:
            sp.wait_ge(self.s["split_done"], self.N - 2)
            sp.dma_start(self.raw[:, 0], self.w(self.N - 1)).then_inc(self.ready[0], 16)
        if self.following:
            sp.wait_ge(self.s["split_done"], self.N)
            load_first(sp, self.M, self.following, self.next_ready)

    def high(self, act, n, u, loads):
        act.wait_ge(self.ready[u], 16 * loads)
        act.wait_ge(self.s["used"], n + 1)
        self.nc.scalar.activation(self.part[:, u, 0], self.raw[:, u], ACT.Copy).then_inc(self.s["high_done"], 1)

    def highs(self, act, out, early=None, later=None):
        self.high(act, 0, 0, 1)
        if early:
            early()
        whole = self.pairs if self.N % 2 else self.pairs - 1
        if later:
            self.high(act, 1, 1, 1)
            out(0, 0)
            self.high(act, 2, 0, 2)
            later()
            out(1, 1)
        start = 1 if later else 0
        if whole > start:
            with act.Fori(start, whole) as i:
                self.high(act, 2 * i + 1, 1, i + 1)
                out(2 * i, 0)
                self.high(act, 2 * i + 2, 0, i + 2)
                out(2 * i + 1, 1)
        if self.N % 2:
            out(self.N - 1, 0)
        else:
            self.high(act, self.N - 1, 1, self.pairs)
            out(self.N - 2, 0)
            out(self.N - 1, 1)

    def lows(self, pool, also=None):
        def low(n, u):
            pool.wait_ge(self.s["high_done"], n + 1)
            self.nc.gpsimd.tensor_tensor(self.part[:, u, 1], self.raw[:, u], self.part[:, u, 0].bitcast(F32),
                                         ALU.subtract).then_inc(self.s["split_done"], 1)

        low(0, 0)
        low(1, 1)
        if self.pairs > 1:
            with pool.Fori(1, self.pairs) as i:
                for u in range(2):
                    low(2 * i + u, u)
                    if also:
                        also(pool, i, u)
        if self.N % 2:
            low(self.N - 1, 0)

    def open(self, pe):
        pe.sem_inc(self.s["used"], 2)

    def one(self, pe, chunk, n, u):
        pe.wait_ge(self.s["high_done"], n + 1)
        low_ready = lambda: pe.wait_ge(self.s["split_done"], n + 1)
        chunk(n, u, halves(self.part[:, u]), low_ready).then_inc(self.s["used"], 1)

    def multiply(self, pe, chunk, after=None, first_after=0, n_after=0, start=0):
        def loop(a, z, tail):
            with pe.Fori(a, z) as i:
                for u in range(2):
                    self.one(pe, chunk, 2 * i + u, u)
                if tail:
                    tail(i)

        end = max(first_after + n_after, start)
        if first_after > start:
            loop(start, first_after, None)
        if n_after:
            loop(first_after, end, after)
        if end < self.pairs:
            loop(end, self.pairs, None)
        if self.N % 2:
            self.one(pe, chunk, self.N - 1, 0)


def at(t, n, *rest):
    return t[(slice(None), bass.ds(n, 1)) + rest]


def split_rows(nc, s, dst, k, src, eng):
    eng.wait_ge(s["h_high"], k + 1)
    nc.vector.tensor_tensor(dst[:, 1, k], src, dst[:, 0, k].bitcast(F32), ALU.subtract).then_inc(s["h_done"], 1)


def proj1(nc, M, A, l, B, following):
    s = take(M, STREAM + "h_f32 h_high h_done psum_free raw_done rot_done t1 t2 turned wi index_done rope_in")
    with ExitStack() as ctx:
        h, hp = M.hT, M.hR
        S = Stream(nc, M, ctx, s, proj_weights(A, l), N_CH, following)
        rope = ctx.enter_context(nc.sbuf_tensor(f"{M.blocks}_rope", [P, 2, T], F32))
        WI = ctx.enter_context(nc.sbuf_tensor(f"{M.blocks}_proj_wi", [P, KD, NH_I], F32))
        t1 = ctx.enter_context(nc.sbuf_tensor(f"{M.blocks}_rope_cos", [P, 2, T], F32))
        t2 = ctx.enter_context(nc.sbuf_tensor(f"{M.blocks}_rope_sin", [P, 2, T], F32))
        block = ctx.enter_context(nc.Block())
        PAIRS = (N_ROPE + 1) // 2

        @block.sync
        def _(sp):
            sp.dma_start(WI[:], A["w_in_i"][l]).then_inc(s["wi"], 16)
            sp.dma_start(rope[:], M.rope).then_inc(s["rope_in"], 16)
            S.load(sp)

        @block.tensor
        def _(pe):
            def chunk(n, u, w, low_ready):
                pe.wait_ge(s["psum_free"], n + 1)
                terms = [(M.PS[:, u, :], [(blocks(w, k), tokens(hp, k, 0, T)) for k in range(KD)])]
                return products(nc, terms, low_ready)

            def rotate(i):
                for u in range(2):
                    pe.wait_ge(s["raw_done"], 2 * i + u - 1)
                    pe.wait_ge(s["turned"], 2 * i + u - 1)
                    nc.tensor.matmul(M.PS[:, 2 + u, :], M.K[:, K_ROT:K_ROT + P], at(B.PT, 2 * i + (u - 2), slice(None)),
                                     start=True, stop=True).then_inc(s["rot_done"], 1)

            S.open(pe)
            pe.wait_ge(s["h_done"], KD)
            S.multiply(pe, chunk, rotate, 1, PAIRS)
            pe.wait_ge(s["wi"], 16)
            for t in range(TT):
                for k in range(KD):
                    mm = nc.tensor.matmul(M.PS[:, 6, t * NH_I:(t + 1) * NH_I], h[:, k, t * P:(t + 1) * P],
                                          WI[:, k, :], start=(k == 0), stop=(k == KD - 1))
            mm.then_inc(s["index_done"], 1)

        @block.gpsimd
        def _(pool):
            S.lows(pool)

        @block.scalar
        def _(act):
            act.sem_inc(s["psum_free"], 2)
            for k in range(KD):
                nc.scalar.activation(h[:, k, :], M.xT[:, k, 0:T], ACT.Identity,
                                     bias=modcol(M, 0, k), scale=modcol(M, 1, k)).then_inc(s["h_f32"], 1)
            for k in range(KD):
                act.wait_ge(s["h_f32"], k + 1)
                nc.scalar.activation(hp[:, 0, k], h[:, k, :], ACT.Copy).then_inc(s["h_high"], 1)

            def copy(n, u):
                act.wait_ge(s["used"], n + 3)
                nc.scalar.activation(at(B.PT, n, slice(None)), M.PS[:, u, :], ACT.Copy).then_inc(s["raw_done"], 1)
                act.wait_ge(s["raw_done"], n + 1)
                act.sem_inc(s["psum_free"], 1)

            S.highs(act, copy)
            act.wait_ge(s["index_done"], 1)
            nc.scalar.activation(B.iw[:], M.PS[:, 6, 0:TT * NH_I], ACT.Copy, scale=NH_I ** -0.5 * HD ** -0.5)

        @block.vector
        def _(dve):
            dve.sem_inc(s["turned"], 2)
            for k in range(KD):
                split_rows(nc, s, hp, k, h[:, k, :], dve)

            dve.wait_ge(s["rope_in"], 16)

            def turn(n, u):
                x = at(B.PT, n, slice(None))
                dve.wait_ge(s["rot_done"], n + 1)
                nc.vector.tensor_tensor(t1[:, u:u + 1], x, rope[:, 0:1],
                                        ALU.mult).then_inc(s["t1"], 1)
                nc.vector.tensor_tensor(t2[:, u], M.PS[:, 2 + u, :], rope[:, 1], ALU.mult).then_inc(s["t2"], 1)
                dve.wait_ge(s["t1"], n + 1)
                dve.wait_ge(s["t2"], n + 1)
                nc.vector.tensor_tensor(x, t1[:, u:u + 1], t2[:, u:u + 1], ALU.add).then_inc(s["turned"], 1)

            with dve.Fori(0, N_ROPE // 2) as i:
                for u in range(2):
                    turn(2 * i + u, u)
            turn(N_ROPE - 1, 0)
            dve.wait_ge(s["rot_done"], N_ROPE + 1)
    give(nc, s, S.ready)


def convolve(nc, M, A, l, B):
    s = take(M, "par step conv gates sig act_step ab_done tr cp dec_in")
    rows = NH_M
    with ExitStack() as ctx:
        cw = ctx.enter_context(M.nc.sbuf_tensor(f"{M.blocks}_conv_w", [P, 4, CONV + 1], F32))
        gb = ctx.enter_context(M.nc.sbuf_tensor(f"{M.blocks}_gate_b", [rows, 2], F32))
        acc = ctx.enter_context(M.nc.sbuf_tensor(f"{M.blocks}_conv_acc", [P, 4, T], F32))
        z = ctx.enter_context(M.nc.sbuf_tensor(f"{M.blocks}_f_pre", [rows, T], F32))
        e = ctx.enter_context(M.nc.sbuf_tensor(f"{M.blocks}_f_exp", [rows, T], F32))
        lf = ctx.enter_context(M.nc.sbuf_tensor(f"{M.blocks}_log_f", [rows, T], F32))
        one = ctx.enter_context(M.nc.sbuf_tensor(f"{M.blocks}_one_row", [rows, T], F32))
        bs = ctx.enter_context(M.nc.sbuf_tensor(f"{M.blocks}_f_sum", [rows, T], F32))
        a = ctx.enter_context(M.nc.sbuf_tensor(f"{M.blocks}_i_rel", [rows, T], F32))
        am = ctx.enter_context(M.nc.sbuf_tensor(f"{M.blocks}_i_max", [rows, T], F32))
        th = ctx.enter_context(M.nc.sbuf_tensor(f"{M.blocks}_floor", [rows, T], F32))
        block = ctx.enter_context(nc.Block())

        @block.sync
        def _(sp):
            sp.dma_start(cw[:], A["conv"][l]).then_inc(s["par"], 16)
            sp.dma_start(gb[:], A["gate_b"][l]).then_inc(s["par"], 16)
            sp.dma_start(B.L[:], A["mixer_consts"]).then_inc(s["dec_in"], 16)
            sp.wait_ge(s["dec_in"], 16)

        @block.vector
        def _(dve):
            step = Steps(dve, s["step"])
            dve.wait_ge(s["par"], 32)
            step(nc.vector.tensor_scalar(z[:], B.PT[32:32 + rows, C_G, :], gb[:, 1:2], None, ALU.add))
            nc.vector.scalar_tensor_tensor(out=lf[:], in0=z[:], scalar=-1.0, in1=z[:], op0=ALU.mult,
                                           op1=ALU.max).then_inc(s["gates"], 1)
            step(nc.vector.memset(one[:], 1.0))

            def conv(c):
                x = B.PT[:, C_MQ + c, :]
                step(nc.vector.tensor_scalar(acc[:, c, :], x, cw[:, c, CONV - 1:CONV], cw[:, c, CONV:CONV + 1],
                                             ALU.mult, ALU.add))
                for back in range(1, CONV):
                    ins = nc.vector.scalar_tensor_tensor(
                        out=acc[:, c, back:T], in0=x[:, 0:T - back], scalar=cw[:, c, CONV - 1 - back:CONV - back],
                        in1=acc[:, c, back:T], op0=ALU.mult, op1=ALU.add)
                    if back < CONV - 1:
                        step(ins)
                    else:
                        ins.then_inc(s["conv"], 1)

            conv(0)
            dve.wait_ge(s["sig"], 1)
            step(nc.vector.scalar_tensor_tensor(out=lf[:], in0=z[:], scalar=0.0, in1=e[:], op0=ALU.min,
                                                op1=ALU.subtract))
            step(nc.vector.tensor_tensor_scan(out=bs[:], data0=one[:], data1=lf[:], initial=0.0,
                                              op0=ALU.mult, op1=ALU.add))
            step(nc.vector.scalar_tensor_tensor(out=a[:], in0=B.PT[0:rows, C_G, :], scalar=gb[:, 0:1], in1=bs[:],
                                                op0=ALU.add, op1=ALU.subtract))
            step(nc.vector.tensor_tensor_scan(out=am[:], data0=a[:], data1=a[:], initial=0.0,
                                              op0=ALU.max, op1=ALU.max))
            step(nc.vector.tensor_tensor(th[:], bs[:], am[:], ALU.add))
            nc.vector.tensor_scalar(th[:], th[:], -1.0, 80.0, ALU.mult, ALU.min).then_inc(s["ab_done"], 1)
            for c in range(1, 4):
                conv(c)

        @block.scalar
        def _(act):
            act.wait_ge(s["gates"], 1)
            nc.scalar.activation(e[:], lf[:], ACT.Exp, scale=-1.0).then_inc(s["act_step"], 1)
            act.wait_ge(s["act_step"], 1)
            nc.scalar.activation(e[:], e[:], ACT.Ln, bias=1.0).then_inc(s["sig"], 1)
            for c in range(2):
                nc.scalar.activation(B.PT[:, C_MO + c, :], B.PT[:, C_MO + c, :], ACT.Sigmoid)
            for c in range(2):
                nc.scalar.activation(B.PT[:, C_RG + c, :], B.PT[:, C_RG + c, :], ACT.Silu)
            act.wait_ge(s["ab_done"], 1)
            nc.scalar.activation(th[:], th[:], ACT.Exp).then_inc(s["act_step"], 1)
            for h in range(NH_M):
                act.wait_ge(s["tr"], h + 1)
                nc.scalar.activation(B.Amax[:, h, :], M.PS[:, h, :], ACT.Copy).then_inc(s["cp"], 1)
            for p in range(NH_M // 2):
                act.wait_ge(s["tr"], NH_M + p + 1)
                nc.scalar.activation(B.floor[:, p, :], M.PS[:, NH_M + p, :], ACT.Copy).then_inc(s["cp"], 1)
            act.wait_ge(s["tr"], NH_M + NH_M // 2 + 1)
            nc.scalar.activation(B.acol[:], M.PS[:, 6, 0:TT * NH_M], ACT.Copy).then_inc(s["cp"], 1)
            for c in range(4):
                act.wait_ge(s["conv"], c + 1)
                nc.scalar.activation(B.PT[:, C_MQ + c, :], acc[:, c, :], ACT.Silu)

        @block.tensor
        def _(pe):
            pe.wait_ge(s["dec_in"], 16)
            pe.wait_ge(s["ab_done"], 1)
            for h in range(NH_M):
                nc.tensor.matmul(M.PS[:, h, :], B.L[0:rows, L_SELH + h * P:L_SELH + (h + 1) * P], am[:],
                                 start=True, stop=True).then_inc(s["tr"], 1)
            pe.wait_ge(s["act_step"], 2)
            for p in range(NH_M // 2):
                nc.tensor.matmul(M.PS[:, NH_M + p, :], B.L[0:rows, L_SELP + p * P:L_SELP + (p + 1) * P], th[:],
                                 start=True, stop=True).then_inc(s["tr"], 1)
            for t in range(TT):
                mm = nc.tensor.transpose(M.PS[:, 6, t * NH_M:(t + 1) * NH_M], a[:, t * P:(t + 1) * P],
                                         M.K[0:rows, K_ID:K_ID + rows])
            mm.then_inc(s["tr"], 1)
    give(nc, s)


class SelectKeys:

    BANKS = (2, 3, 6, 7)

    def __init__(self, nc, M, ctx, s, B):
        self.nc, self.M, self.s, self.B = nc, M, s, B
        self.sc, self.tmp, self.work = (ctx.enter_context(nc.sbuf_tensor(f"{M.blocks}_{name}", [P, T], F32))
                                        for name in ("score", "score_h", "score_left"))
        self.best = ctx.enter_context(nc.sbuf_tensor(f"{M.blocks}_best8", [P, 8], F32))

    def bank(self, n, w):
        return self.M.PS[:, self.BANKS[n % 4], 0:w]

    def scores(self, pe, j):
        t = TT - 1 - j
        for h in range(NH_I):
            n, w, b = j * NH_I + h, P * (t + 1), HD * (h % 2)
            if n >= 4:
                pe.wait_ge(self.s["taken"], n - 3)
            self.nc.tensor.matmul(self.bank(n, w), self.B.PT[b:b + HD, C_IQ + h // 2, t * P:(t + 1) * P],
                                  self.B.PT[b:b + HD, C_IK, 0:w], start=True, stop=True).then_inc(self.s["scored"], 1)

    def choose(self, dve):
        nc, B, s = self.nc, self.B, self.s
        sc, tmp, work, best = self.sc, self.tmp, self.work, self.best
        step = Steps(dve, s["step"])
        for j in range(TT):
            t = TT - 1 - j
            w = P * (t + 1)
            for h in range(NH_I):
                n, i = j * NH_I + h, t * NH_I + h
                dve.wait_ge(s["scored"], n + 1)
                out = tmp if h else sc
                nc.vector.tensor_scalar(out[:, 0:w], self.bank(n, w), 0.0, B.iw[:, i:i + 1],
                                        ALU.max, ALU.mult).then_inc(s["taken"], 1)
                if h:
                    dve.wait_ge(s["taken"], n + 1)
                    step(nc.vector.tensor_tensor(sc[:, 0:w], sc[:, 0:w], tmp[:, 0:w], ALU.add))
            if t == 0:
                step(nc.vector.memset(B.bias[:, 0, 0:w], 0.0))
                step(nc.vector.memset(B.bias[0:64, 0, 64:w], NEG))
                continue
            step(nc.vector.memset(sc[0:64, w - 64:w], -3.0e38))
            src = sc
            for r in range(TOPK // 8):
                step(nc.vector.max(best[:], src[:, 0:w]))
                step(nc.vector.match_replace(work[:, 0:w], best[:], src[:, 0:w], -1.0e38))
                src = work
            step(nc.vector.tensor_tensor(tmp[:, 0:w], work[:, 0:w], sc[:, 0:w], ALU.is_equal))
            step(nc.vector.tensor_scalar(B.bias[:, t, 0:w], tmp[:, 0:w], NEG, None, ALU.mult))


def attend(nc, M, items, scale):
    s = take(M, "s_done sm_done nm_done exp_done p_done t_done pt_done pv_done o_done step")
    N = len(items)
    WM = max(sum(w for _, w, _ in it.segs) for it in items)
    with ExitStack() as ctx:
        sm = ctx.enter_context(M.nc.sbuf_tensor(f"{M.blocks}_att_s", [P, 2, WM], F32))
        pr = ctx.enter_context(M.nc.sbuf_tensor(f"{M.blocks}_att_p", [P, 2, WM], F32))
        pt = ctx.enter_context(M.nc.sbuf_tensor(f"{M.blocks}_att_pT", [P, 2, WM], F32))
        mx = ctx.enter_context(M.nc.sbuf_tensor(f"{M.blocks}_att_max", [P, N], F32))
        nm = ctx.enter_context(M.nc.sbuf_tensor(f"{M.blocks}_att_nmax", [P, N], F32))
        su = ctx.enter_context(M.nc.sbuf_tensor(f"{M.blocks}_att_sum", [P, N], F32))
        ri = ctx.enter_context(M.nc.sbuf_tensor(f"{M.blocks}_att_rsum", [P, N], F32))
        block = ctx.enter_context(nc.Block())

        def width(n):
            return sum(w for _, w, _ in items[n].segs)

        @block.tensor
        def _(pe):
            def scores(n):
                if n >= 2:
                    pe.wait_ge(s["sm_done"], n - 1)
                for j, (k, w, _) in enumerate(items[n].segs):
                    mm = nc.tensor.matmul(M.PS[:, 2 * (n % 2) + j, 0:w], items[n].q, k, start=True, stop=True)
                mm.then_inc(s["s_done"], 1)

            def turn(n):
                pe.wait_ge(s["p_done"], n + 1)
                if n >= 1:
                    pe.wait_ge(s["pt_done"], n)
                for b in range(width(n) // P):
                    mm = nc.tensor.transpose(M.PS[:, 4 + b // 4, (b % 4) * P:(b % 4 + 1) * P],
                                             pr[:, n % 2, b * P:(b + 1) * P], M.K[:, K_ID:K_ID + P])
                mm.then_inc(s["t_done"], 1)

            def values(n):
                pe.wait_ge(s["pt_done"], n + 1)
                m, c = n // 2, HD * (n % 2)
                if m >= 2:
                    pe.wait_ge(s["o_done"], m - 1)
                B_ = width(n) // P
                for b in range(B_):
                    mm = nc.tensor.matmul(M.PS[c:c + HD, 6 + m % 2, 0:P], items[n].vs[b],
                                          pt[:, n % 2, b * P:(b + 1) * P], start=(b == 0), stop=(b == B_ - 1))
                mm.then_inc(s["pv_done"], 1)

            scores(0)
            for n in range(N + 2):
                if n + 1 < N:
                    scores(n + 1)
                if 1 <= n <= N:
                    turn(n - 1)
                if n >= 2:
                    values(n - 2)

        @block.vector
        def _(dve):
            step = Steps(dve, s["step"])

            def front(n):
                dve.wait_ge(s["s_done"], n + 1)
                if n >= 2:
                    dve.wait_ge(s["exp_done"], n - 1)
                at = 0
                for j, (_, w, bias) in enumerate(items[n].segs):
                    src, out = M.PS[:, 2 * (n % 2) + j, 0:w], sm[:, n % 2, at:at + w]
                    if bias is None:
                        ins = nc.vector.tensor_scalar(out, src, scale, None, ALU.mult)
                    else:
                        ins = nc.vector.scalar_tensor_tensor(out=out, in0=src, scalar=scale, in1=bias,
                                                             op0=ALU.mult, op1=ALU.add)
                    at += w
                    if j < len(items[n].segs) - 1:
                        step(ins)
                ins.then_inc(s["sm_done"], 1)
                dve.wait_ge(s["sm_done"], n + 1)
                step(nc.vector.tensor_reduce(mx[:, n:n + 1], sm[:, n % 2, 0:at], AX.X, ALU.max))
                nc.vector.tensor_scalar(nm[:, n:n + 1], mx[:, n:n + 1], -1.0, None, ALU.mult).then_inc(s["nm_done"], 1)

            def back(n):
                dve.wait_ge(s["exp_done"], n + 1)
                step(nc.vector.reciprocal(ri[:, n:n + 1], su[:, n:n + 1]))
                w = width(n)
                nc.vector.tensor_scalar(pr[:, n % 2, 0:w], pr[:, n % 2, 0:w], ri[:, n:n + 1], None,
                                        ALU.mult).then_inc(s["p_done"], 1)

            for n in range(N + 1):
                if n < N:
                    front(n)
                if n >= 1:
                    back(n - 1)

        @block.scalar
        def _(act):
            def exps(n):
                act.wait_ge(s["nm_done"], n + 1)
                if n >= 2:
                    act.wait_ge(s["t_done"], n - 1)
                w = width(n)
                nc.scalar.activation(pr[:, n % 2, 0:w], sm[:, n % 2, 0:w], ACT.Exp, bias=nm[:, n:n + 1],
                                     accum_out=su[:, n:n + 1]).then_inc(s["exp_done"], 1)

            def copy_turned(n):
                act.wait_ge(s["t_done"], n + 1)
                if n >= 2:
                    act.wait_ge(s["pv_done"], n - 1)
                w = width(n)
                ins = nc.scalar.activation(pt[:, n % 2, 0:min(w, 512)], M.PS[:, 4, 0:min(w, 512)], ACT.Copy)
                if w > 512:
                    ins = nc.scalar.activation(pt[:, n % 2, 512:w], M.PS[:, 5, 0:w - 512], ACT.Copy)
                ins.then_inc(s["pt_done"], 1)

            def copy_out(m):
                act.wait_ge(s["pv_done"], 2 * m + 2)
                nc.scalar.activation(items[2 * m].o, M.PS[:, 6 + m % 2, 0:P], ACT.Copy).then_inc(s["o_done"], 1)

            for n in range(N + 2):
                if n < N:
                    exps(n)
                if 1 <= n <= N:
                    copy_turned(n - 1)
                if n >= 2 and n % 2 == 1:
                    copy_out((n - 3) // 2)
    give(nc, s)


def attend1(nc, M, B):
    items = []
    for t in range(TT):
        w = P * (t + 1)
        for h in range(NH_A):
            b, c = HD * (h % 2), h // 2
            items.append(Item(
                q=B.PT[b:b + HD, C_AQ + c, t * P:(t + 1) * P],
                segs=[(B.PT[b:b + HD, C_AK + c, 0:w], w, B.bias[:, t, 0:w])],
                vs=[B.V[:, j, V_A + h * HD:V_A + (h + 1) * HD] for j in range(t + 1)],
                o=B.mixT[:, c, t * P:(t + 1) * P]))
    attend(nc, M, items, HD ** -0.5)


def linear_mixers(nc, M, B):
    s = take(M, "s_done p_done pv_done e_in e_done y_done step")
    N = 2 * NH_R * TT
    G = N // 8
    with ExitStack() as ctx:
        pb = ctx.enter_context(M.nc.sbuf_tensor(f"{M.blocks}_lin_p", [P, 2, T], F32))
        eb = ctx.enter_context(M.nc.sbuf_tensor(f"{M.blocks}_lin_e", [P, 2, T], F32))
        den = ctx.enter_context(M.nc.sbuf_tensor(f"{M.blocks}_lin_den", [P, T], F32))
        block = ctx.enter_context(nc.Block())

        def item(n):
            kind, h, t = n // (NH_R * TT), n // TT % NH_R, n % TT
            return kind, h, t, T - P * t

        @block.tensor
        def _(pe):
            def scores(n):
                kind, h, t, w = item(n)
                b = HD * (h % 2)
                q, k = (C_MQ, C_MK) if kind else (C_RQ, C_RK)
                if n >= 2:
                    pe.wait_ge(s["p_done"], n - 1)
                nc.tensor.matmul(M.PS[:, n % 2, 0:w], B.PT[b:b + HD, k + h // 2, t * P:(t + 1) * P],
                                 B.PT[b:b + HD, q + h // 2, t * P:T], start=True, stop=True).then_inc(s["s_done"], 1)

            def values(n):
                kind, h, t, w = item(n)
                b, g = HD * (h % 2), n // 8
                pe.wait_ge(s["p_done"], n + 1)
                if n % 8 == 0 and g >= 2:
                    pe.wait_ge(s["y_done"], g - 1)
                v0 = (V_M if kind else V_R) + h * HD
                mm = nc.tensor.matmul(M.PS[b:b + HD, 2 + g % 2, T - w:T], B.V[:, t, v0:v0 + HD], pb[:, n % 2, 0:w],
                                      start=(t == 0), stop=(t == TT - 1))
                if kind:
                    mm = nc.tensor.matmul(M.PS[b:b + HD, 4 + g % 2, T - w:T], M.K[:, K_ONE:K_ONE + HD],
                                          pb[:, n % 2, 0:w], start=(t == 0), stop=(t == TT - 1))
                mm.then_inc(s["pv_done"], 1)

            for n in range(N + 1):
                if n < N:
                    scores(n)
                if n >= 1:
                    values(n - 1)

        @block.vector
        def _(dve):
            step = Steps(dve, s["step"])

            def weigh(n):
                kind, h, t, w = item(n)
                if n >= 2:
                    dve.wait_ge(s["pv_done"], n - 1)
                if kind:
                    m = n - NH_R * TT
                    dve.wait_ge(s["e_done"], m + 1)
                    dve.wait_ge(s["s_done"], n + 1)
                    step(nc.vector.scalar_tensor_tensor(out=pb[:, n % 2, 0:w], in0=M.PS[:, n % 2, 0:w],
                                                        scalar=HD ** -0.5, in1=eb[:, m % 2, 0:w],
                                                        op0=ALU.mult, op1=ALU.mult))
                    nc.vector.tensor_tensor(pb[:, n % 2, 0:P], pb[:, n % 2, 0:P], B.L[:, L_UP:L_UP + P],
                                            ALU.mult).then_inc(s["p_done"], 1)
                else:
                    dve.wait_ge(s["s_done"], n + 1)
                    nc.vector.scalar_tensor_tensor(out=pb[:, n % 2, 0:w], in0=M.PS[:, n % 2, 0:w],
                                                   scalar=HD ** -0.5, in1=B.L[:, h * T:h * T + w],
                                                   op0=ALU.mult, op1=ALU.mult).then_inc(s["p_done"], 1)

            def exponent(m):
                h, t = m // TT, m % TT
                w = T - P * t
                if m >= 2:
                    dve.wait_ge(s["p_done"], NH_R * TT + m - 1)
                nc.vector.tensor_scalar(eb[:, m % 2, 0:w], B.Amax[:, h, T - w:T],
                                        B.acol[:, t * NH_M + h:t * NH_M + h + 1], 0.0,
                                        ALU.subtract, ALU.max).then_inc(s["e_in"], 1)

            def take_pair(g):
                dve.wait_ge(s["pv_done"], 8 * g + 8)
                if g < 2:
                    nc.vector.tensor_copy(B.Y[:, g, :], M.PS[:, 2 + g % 2, :]).then_inc(s["y_done"], 1)
                    return
                step(nc.vector.tensor_scalar(den[:], M.PS[:, 4 + g % 2, :], -1.0, None, ALU.mult))
                step(nc.vector.tensor_tensor(den[:], M.PS[:, 4 + g % 2, :], den[:], ALU.max))
                step(nc.vector.tensor_tensor(den[:], den[:], B.floor[:, g - 2, :], ALU.max))
                step(nc.vector.reciprocal(den[:], den[:]))
                step(nc.vector.tensor_tensor(den[:], den[:], B.PT[:, C_MO + g - 2, :], ALU.mult))
                nc.vector.tensor_tensor(B.Y[:, g, :], M.PS[:, 2 + g % 2, :], den[:], ALU.mult).then_inc(s["y_done"], 1)

            half = NH_R * TT
            for n in range(N + 1):
                if half - 1 <= n < N - 1:
                    exponent(n + 1 - half)
                if n < N:
                    weigh(n)
                if n >= 1 and n % 8 == 0:
                    take_pair(n // 8 - 1)

        @block.scalar
        def _(act):
            for m in range(NH_M * TT):
                w = T - P * (m % TT)
                act.wait_ge(s["e_in"], m + 1)
                nc.scalar.activation(eb[:, m % 2, 0:w], eb[:, m % 2, 0:w], ACT.Exp, scale=-1.0).then_inc(s["e_done"], 1)
    give(nc, s)


def head_norm(nc, M, B):
    s = take(M, "mean cen sq var sd norm rstd done")
    with ExitStack() as ctx:
        cen = ctx.enter_context(M.nc.sbuf_tensor(f"{M.blocks}_hn_cen", [P, 4, T], F32))
        sq = ctx.enter_context(M.nc.sbuf_tensor(f"{M.blocks}_hn_sq", [P, 4, T], F32))
        block = ctx.enter_context(nc.Block())
        heads = B.L[:, L_HEAD:L_HEAD + P]

        @block.tensor
        def _(pe):
            for c in range(4):
                nc.tensor.matmul(M.PS[:, c, :], heads, B.Y[:, c, :], start=True, stop=True).then_inc(s["mean"], 1)
            for c in range(4):
                pe.wait_ge(s["sq"], c + 1)
                nc.tensor.matmul(M.PS[:, 4 + c, :], heads, sq[:, c, :], start=True, stop=True).then_inc(s["var"], 1)

        @block.vector
        def _(dve):
            for c in range(4):
                dve.wait_ge(s["mean"], c + 1)
                nc.vector.tensor_tensor(cen[:, c, :], B.Y[:, c, :], M.PS[:, c, :], ALU.subtract).then_inc(s["cen"], 1)
            for c in range(4):
                dve.wait_ge(s["sd"], c + 1)
                nc.vector.reciprocal(sq[:, c, :], sq[:, c, :]).then_inc(s["rstd"], 1)
                dve.wait_ge(s["rstd"], c + 1)
                out = B.mixT[:, 4 + c, :] if c >= 2 else cen[:, c, :]
                nc.vector.tensor_tensor(out, cen[:, c, :], sq[:, c, :], ALU.mult).then_inc(s["norm"], 1)
                if c < 2:
                    dve.wait_ge(s["norm"], c + 1)
                    nc.vector.tensor_tensor(B.mixT[:, 4 + c, :], cen[:, c, :], B.PT[:, C_RG + c, :],
                                            ALU.mult).then_inc(s["done"], 1)

        @block.scalar
        def _(act):
            for c in range(4):
                act.wait_ge(s["cen"], c + 1)
                nc.scalar.activation(sq[:, c, :], cen[:, c, :], ACT.Square).then_inc(s["sq"], 1)
            for c in range(4):
                act.wait_ge(s["var"], c + 1)
                nc.scalar.activation(sq[:, c, :], M.PS[:, 4 + c, :], ACT.Sqrt, bias=M.eps[:, 0:1]).then_inc(s["sd"], 1)
    give(nc, s)


class Modulation:

    def __init__(self, nc, M, ctx, s, w, b, cond, first, n, conds=2):
        self.nc, self.M, self.s, self.w, self.first, self.n = nc, M, s, w, first, n
        self.b, self.cond, self.conds = b, cond, conds
        self.W = ctx.enter_context(nc.sbuf_tensor(f"{M.blocks}_mod_w", [P, 2, n, D], F32))
        self.B = ctx.enter_context(nc.sbuf_tensor(f"{M.blocks}_mod_b", [P, 2 * N_MOD], F32))
        self.J = ctx.enter_context(nc.sbuf_tensor(f"{M.blocks}_mod_c", [P, D], F32))
        self.acc = ctx.enter_context(nc.sbuf_tensor(f"{M.blocks}_mod_acc", [P, 2, 2 * n], F32))
        self.ready = (s["r0"], s["r1"])

    def silu_cond(self, c):
        return self.M.PS[:, 2 + 4 * c:4 + 4 * c, :].rearrange("p a b -> p (a b)")

    def load(self, sp):
        s = self.s
        sp.dma_start(self.B[:], self.b).then_inc(s["bias_in"], 16)
        for c in range(self.conds):
            if c:
                sp.wait_ge(s["summed"], c)
            sp.dma_start(self.J[:], self.cond[c].partition_broadcast(P)).then_inc(s["cond_in"], 16)

    def load_first(self, eng):
        for u in range(2):
            eng.dma_start(self.W[:, u], self.w(self.first + u * self.n)).then_inc(self.ready[u], 16)

    def load_next(self, sp, i, u):
        sp.wait_ge(self.s["added"], 2 * i + u - 1)
        sp.dma_start(self.W[:, u], self.w(2 * i * self.n + (self.first + u * self.n))).then_inc(self.ready[u], 16)

    def sigmoid(self, act):
        for c in range(self.conds):
            act.wait_ge(self.s["cond_in"], 16 * (c + 1))
            for j in range(2):
                self.nc.scalar.activation(self.M.PS[:, 2 + 4 * c + j, :], self.J[:, j * 512:(j + 1) * 512],
                                          ACT.Sigmoid).then_inc(self.s["sig"], 1)

    def conditions(self, dve):
        self.nc.vector.memset(self.acc[:], 0.0).then_inc(self.s["bias_in"], 16)
        for c in range(self.conds):
            dve.wait_ge(self.s["sig"], 2 * c + 2)
            self.nc.vector.tensor_tensor(self.silu_cond(c), self.J[:], self.silu_cond(c),
                                         ALU.mult).then_inc(self.s["summed"], 1)
        dve.wait_ge(self.s["summed"], self.conds)
        dve.wait_ge(self.s["bias_in"], 32)

    def chunks(self, dve, i, u):
        nc, s, C = self.nc, self.s, self.conds
        K = C * self.n
        dve.wait_ge(self.ready[u], 16 * i + 16)
        for j in range(K):
            a = j // C * 2 + j % C
            nc.vector.tensor_tensor_reduce(out=self.J[:], in0=self.W[:, u, j // C], in1=self.silu_cond(j % C),
                                           scale=1.0, scalar=0.0, op0=ALU.mult, op1=ALU.add,
                                           accum_out=self.acc[:, u, a:a + 1]).then_inc(s["summed"], 1)
            dve.wait_ge(s["summed"], 2 * K * i + (C + u * K + j + 1))
        col = 2 * self.n * (2 * i + u) + 2 * self.first
        nc.vector.tensor_tensor(self.M.mod_next[:, bass.ds(col, 2 * self.n)], self.acc[:, u, :],
                                self.B[:, bass.ds(col, 2 * self.n)], ALU.add).then_inc(s["added"], 1)


def gemm_residual(nc, M, weights, src, spans, gate, alpha, following, mix=None, ride=None):
    s = take(M, STREAM + "h_high h_done psum_free scaled r0 r1 bias_in cond_in sig summed added")
    NS = len(spans)
    TW = sum(n for _, n, _ in spans)
    with ExitStack() as ctx:
        S = Stream(nc, M, ctx, s, weights, KD, following)
        KP = weights[1]
        tmp = ctx.enter_context(nc.sbuf_tensor(f"{M.blocks}_out_t", [P, 1, TW], F32))
        if ride:
            rw, rb, cond, r_first, r_n = ride
            R = Modulation(nc, M, ctx, s, rw, rb, cond, r_first, r_n)
        block = ctx.enter_context(nc.Block())

        @block.sync
        def _(sp):
            if ride:
                R.load(sp)
            S.load(sp)

        @block.tensor
        def _(pe):
            def chunk(n, u, w, low_ready):
                pe.wait_ge(s["psum_free"], NS * n + NS)
                terms = [(M.PS[:, 4 * u + a, 0:nt], [(blocks(w, k), tokens(src, k, t0, nt)) for k in range(KP)])
                         for a, (t0, nt, _) in enumerate(spans)]
                return products(nc, terms, low_ready)

            S.open(pe)
            if mix is not None:
                pe.wait_ge(s["h_done"], KD)
            S.multiply(pe, chunk)

        @block.gpsimd
        def _(pool):
            if ride:
                R.load_first(pool)
            S.lows(pool, R.load_next if ride else None)

        @block.scalar
        def _(act):
            if mix is not None:
                for k in range(KD):
                    nc.scalar.activation(src[:, 0, k], mix[:, k, :], ACT.Copy).then_inc(s["h_high"], 1)
            S.highs(act, lambda n, u: None, (lambda: R.sigmoid(act)) if ride else None)

        @block.vector
        def _(dve):
            dve.sem_inc(s["psum_free"], 2 * NS)
            dve.sem_inc(s["scaled"], NS)
            if mix is not None:
                for k in range(KD):
                    split_rows(nc, s, src, k, mix[:, k, :], dve)
            if ride:
                R.conditions(dve)
            with dve.Fori(0, KD // 2) as i:
                for u in range(2):
                    if ride:
                        R.chunks(dve, i, u)
                    dve.wait_ge(s["used"], 2 * i + u + 3)
                    dve.wait_ge(s["scaled"], 2 * NS * i + NS * (u + 1))
                    off = 0
                    for a, (t0, nt, c) in enumerate(spans):
                        g = M.mod[:, bass.ds((gate * KD + 2 * i + u) * 2 + c, 1)]
                        nc.vector.tensor_scalar(tmp[:, 0, off:off + nt], M.PS[:, 4 * u + a, 0:nt], g, None,
                                                ALU.mult).then_inc(s["psum_free"], 1)
                        off += nt
                    off = 0
                    for a, (t0, nt, c) in enumerate(spans):
                        dve.wait_ge(s["psum_free"], 2 * NS + 2 * NS * i + NS * u + a + 1)
                        x = M.xT[:, bass.ds(2 * i + u, 1), t0:t0 + nt]
                        nc.vector.scalar_tensor_tensor(out=x, in0=x, scalar=float(alpha),
                                                       in1=tmp[:, 0:1, off:off + nt],
                                                       op0=ALU.mult, op1=ALU.add).then_inc(s["scaled"], 1)
                        off += nt
    give(nc, s, S.ready)


def adopt(nc, M, plus_one):
    s = take(M, "copied done")
    with nc.Block() as block:
        @block.vector
        def _(dve):
            nc.vector.tensor_copy(M.mod[:], M.mod_next[:]).then_inc(s["copied"], 1)
            dve.wait_ge(s["copied"], 1)
            for part in plus_one:
                m = M.mod[:, part * KD * 2:(part + 1) * KD * 2]
                nc.vector.tensor_scalar(m, m, 1.0, None, ALU.add).then_inc(s["done"], 1)
    give(nc, s)


def layer_norm(nc, M, gb):
    s = take(M, "par mean cen sq var sd rstd norm done")
    with ExitStack() as ctx:
        GB = ctx.enter_context(M.nc.sbuf_tensor(f"{M.blocks}_ln_gb", [P, 2, KD], F32))
        sq = ctx.enter_context(M.nc.sbuf_tensor(f"{M.blocks}_ln_sq", [P, 4, T], F32))
        rs = ctx.enter_context(M.nc.sbuf_tensor(f"{M.blocks}_ln_rs", [P, T], F32))
        block = ctx.enter_context(nc.Block())
        mean = M.K[:, K_MEAN:K_MEAN + P]

        @block.sync
        def _(sp):
            sp.dma_start(GB[:], gb).then_inc(s["par"], 16)

        @block.tensor
        def _(pe):
            for k in range(KD):
                mm = nc.tensor.matmul(M.PS[:, 0, :], mean, M.xT[:, k, 0:T], start=(k == 0), stop=(k == KD - 1))
            mm.then_inc(s["mean"], 1)
            for k in range(KD):
                pe.wait_ge(s["sq"], k + 1)
                nc.tensor.matmul(M.PS[:, 1, :], mean, sq[:, k % 4, :], start=(k == 0),
                                 stop=(k == KD - 1)).then_inc(s["var"], 1)

        @block.vector
        def _(dve):
            dve.wait_ge(s["mean"], 1)
            for k in range(KD):
                nc.vector.tensor_tensor(M.xT[:, k, 0:T], M.xT[:, k, 0:T], M.PS[:, 0, :],
                                        ALU.subtract).then_inc(s["cen"], 1)
            dve.wait_ge(s["sd"], 1)
            nc.vector.reciprocal(rs[:], rs[:]).then_inc(s["rstd"], 1)
            dve.wait_ge(s["rstd"], 1)
            for k in range(KD):
                nc.vector.tensor_tensor(M.xT[:, k, 0:T], M.xT[:, k, 0:T], rs[:], ALU.mult).then_inc(s["norm"], 1)

        @block.scalar
        def _(act):
            for k in range(KD):
                act.wait_ge(s["cen"], k + 1)
                if k >= 4:
                    act.wait_ge(s["var"], k - 3)
                nc.scalar.activation(sq[:, k % 4, :], M.xT[:, k, 0:T], ACT.Square).then_inc(s["sq"], 1)
            act.wait_ge(s["var"], KD)
            nc.scalar.activation(rs[:], M.PS[:, 1, :], ACT.Sqrt, bias=M.eps[:, 0:1]).then_inc(s["sd"], 1)
            act.wait_ge(s["par"], 16)
            for k in range(KD):
                act.wait_ge(s["norm"], k + 1)
                nc.scalar.activation(M.xT[:, k, 0:T], M.xT[:, k, 0:T], ACT.Identity, bias=GB[:, 1, k:k + 1],
                                     scale=GB[:, 0, k:k + 1]).then_inc(s["done"], 1)
    give(nc, s)


def route(nc, M, A, sc, bi):
    s = take(M, "par h_f32 h_high h_done logits sig biased")
    with ExitStack() as ctx:
        wr = ctx.enter_context(M.nc.sbuf_tensor(f"{M.blocks}_router_w", [P, KD, NE], F32))
        br = ctx.enter_context(M.nc.sbuf_tensor(f"{M.blocks}_router_b", [P, NE], F32))
        block = ctx.enter_context(nc.Block())

        @block.sync
        def _(sp):
            sp.dma_start(wr[:], A["w_router"]).then_inc(s["par"], 16)
            sp.dma_start(br[:], A["b_router"].partition_broadcast(P)).then_inc(s["par"], 16)

        @block.tensor
        def _(pe):
            pe.wait_ge(s["par"], 32)
            pe.wait_ge(s["h_f32"], KD)
            for t in range(TT):
                for k in range(KD):
                    mm = nc.tensor.matmul(M.PS[:, 0, t * NE:(t + 1) * NE], M.hT[:, k, t * P:(t + 1) * P], wr[:, k, :],
                                          start=(k == 0), stop=(k == KD - 1))
            mm.then_inc(s["logits"], 1)

        @block.scalar
        def _(act):
            for k in range(KD):
                nc.scalar.activation(M.hT[:, k, 0:T], M.xT[:, k, 0:T], ACT.Identity,
                                     bias=modcol(M, 3, k), scale=modcol(M, 4, k)).then_inc(s["h_f32"], 1)
            for k in range(KD):
                act.wait_ge(s["h_f32"], k + 1)
                nc.scalar.activation(M.hR[:, 0, k], M.hT[:, k, :], ACT.Copy).then_inc(s["h_high"], 1)
            act.wait_ge(s["logits"], 1)
            nc.scalar.activation(sc[:], M.PS[:, 0, 0:TT * NE].rearrange("p (t e) -> p t e", t=TT),
                                 ACT.Sigmoid).then_inc(s["sig"], 1)

        @block.vector
        def _(dve):
            for k in range(KD):
                split_rows(nc, s, M.hR, k, M.hT[:, k, :], dve)
            dve.wait_ge(s["par"], 32)
            dve.wait_ge(s["sig"], 1)
            nc.vector.tensor_tensor(bi[:], sc[:], br[:].unsqueeze(1).to_broadcast([P, TT, NE]),
                                    ALU.add).then_inc(s["biased"], 1)
    give(nc, s)


class Router:

    def __init__(self, nc, M, ctx, s, sc, bi):
        self.nc, self.M, self.s, self.sc, self.bi = nc, M, s, sc, bi

        def tensor(name, n, m=TT):
            return ctx.enter_context(nc.sbuf_tensor(f"{M.blocks}_r_{name}", [P, m, n], F32))

        self.v, self.eq, self.chosen = tensor("cand", NE), tensor("eq", NE), tensor("chosen", NE)
        self.pair, self.gs, self.ge = tensor("pair", 6, TT * NG), tensor("group", NG), tensor("geq", NG)
        self.m1 = ctx.enter_context(nc.sbuf_tensor(f"{M.blocks}_r_m1", [P, TT], F32))

    def turn(self, pe):
        pe.wait_ge(self.s["routed"], 1)
        for t in range(TT):
            mm = self.nc.tensor.transpose(self.M.PS[0:NE, 1, t * P:(t + 1) * P], self.v[:, t, :],
                                          self.M.K[:, K_ID:K_ID + P])
        mm.then_inc(self.s["rows_in_psum"], 1)
        pe.wait_ge(self.s["rows_done"], 1)

    def copy(self, act, gT):
        act.wait_ge(self.s["rows_in_psum"], 1)
        self.nc.scalar.activation(gT[:], self.M.PS[0:NE, 1, :], ACT.Copy).then_inc(self.s["rows_done"], 1)

    def choose(self, dve):
        nc, M, s = self.nc, self.M, self.s
        v, eq, chosen, pair, gs, ge, m1 = self.v, self.eq, self.chosen, self.pair, self.gs, self.ge, self.m1
        step = Steps(dve, s["step"])
        rank_e = M.K[:, K_RANK:K_RANK + NE].unsqueeze(1).to_broadcast([P, TT, NE])
        rank_g = M.K[:, K_RANK + NE:K_RANK + NE + NG].unsqueeze(1).to_broadcast([P, TT, NG])
        over_e = lambda a, n: a[:].unsqueeze(2).to_broadcast([P, TT, n])
        tt = nc.vector.tensor_tensor
        quad = self.bi[:].rearrange("p t (g e) -> p (t g) e", e=EPG)
        at = 0
        for a in range(EPG - 1):
            for b in range(a + 1, EPG):
                step(tt(pair[:, :, at:at + 1], quad[:, :, a:a + 1], quad[:, :, b:b + 1], ALU.add))
                at += 1
        step(nc.vector.tensor_reduce(gs[:].rearrange("p t g -> p (t g)"), pair[:], AX.X, ALU.max))

        def first_best(out, val, n, rank):
            step(nc.vector.tensor_reduce(m1[:], val[:], AX.X, ALU.max))
            step(tt(out[:], val[:], over_e(m1, n), ALU.is_equal))
            step(tt(out[:], out[:], rank, ALU.mult))
            step(nc.vector.tensor_reduce(m1[:], out[:], AX.X, ALU.max))
            step(tt(out[:], out[:], over_e(m1, n), ALU.is_equal))

        first_best(ge, gs, NG, rank_g)
        geb = ge[:].rearrange("p t g -> p (t g)").unsqueeze(2).to_broadcast([P, TT * NG, EPG])
        step(tt(v[:].rearrange("p t (g e) -> p (t g) e", e=EPG), quad, geb, ALU.mult))
        step(nc.vector.tensor_scalar(ge[:], ge[:], -1.0, -NEG, ALU.add, ALU.mult))
        vq = v[:].rearrange("p t (g e) -> p (t g) e", e=EPG)
        step(tt(vq, vq, geb, ALU.add))
        first_best(chosen, v, NE, rank_e)
        step(nc.vector.scalar_tensor_tensor(out=v[:].rearrange("p t e -> p (t e)"),
                                            in0=chosen[:].rearrange("p t e -> p (t e)"), scalar=NEG,
                                            in1=v[:].rearrange("p t e -> p (t e)"), op0=ALU.mult, op1=ALU.add))
        first_best(eq, v, NE, rank_e)
        step(tt(chosen[:], chosen[:], eq[:], ALU.add))
        step(tt(v[:], chosen[:], self.sc[:], ALU.mult))
        step(nc.vector.tensor_reduce(m1[:], v[:], AX.X, ALU.add))
        step(nc.vector.reciprocal(m1[:], m1[:]))
        tt(v[:], v[:], over_e(m1, NE), ALU.mult).then_inc(s["routed"], 1)


def gated_up(nc, M, weights, hid, NF, spans, following, gates=None, gT=None, e0=0,
             scores=None):
    s = take(M, STREAM + "step routed rows_in_psum rows_done spread spread_out silu_done psum_free gated high_out low_out")
    TW = sum(n for _, n in spans)
    with ExitStack() as ctx:
        S = Stream(nc, M, ctx, s, weights, NF, following)
        sl = ctx.enter_context(nc.sbuf_tensor(f"{M.blocks}_silu", [P, 2, TW], F32))
        pr = ctx.enter_context(nc.sbuf_tensor(f"{M.blocks}_silu_up", [P, 2, TW], F32))
        block = ctx.enter_context(nc.Block())
        NG_ = NF // 2
        if scores:
            R = Router(nc, M, ctx, s, *scores)

        @block.sync
        def _(sp):
            S.load(sp)

        @block.gpsimd
        def _(pool):
            S.lows(pool)

        @block.tensor
        def _(pe):
            S.open(pe)
            def chunk(n, u, w, low_ready):
                pe.wait_ge(s["psum_free"], n + 1)
                terms = [(M.PS[:, 4 * u + 2 * part + a, 0:nt],
                          [(blocks(w, part * KD + k), tokens(M.hR, k, t0, nt)) for k in range(KD)])
                         for part in range(2) for a, (t0, nt) in enumerate(spans)]
                return products(nc, terms, low_ready)

            if scores:
                for u in range(2):
                    S.one(pe, chunk, u, u)
                R.turn(pe)
            if gates is not None:
                for e in range(NG_):
                    if e >= 4:
                        pe.wait_ge(s["spread_out"], e - 3)
                    one = M.K[0:NE, K_ID + e0 + e:K_ID + e0 + e + 1].to_broadcast([NE, P])
                    nc.tensor.matmul(M.PS[:, 2 * (e % 4) + 1, :], one, gT[:], start=True,
                                     stop=True).then_inc(s["spread"], 1)
            S.multiply(pe, chunk, start=1 if scores else 0)

        @block.scalar
        def _(act):
            def spread():
                if scores:
                    R.copy(act, gT)
                for e in range(NG_ if gates is not None else 0):
                    act.wait_ge(s["spread"], e + 1)
                    nc.scalar.activation(gates[:, e, :], M.PS[:, 2 * (e % 4) + 1, :],
                                         ACT.Copy).then_inc(s["spread_out"], 1)

            def out(n, u):
                act.wait_ge(s["used"], n + 3)
                off = 0
                for a, (_, nt) in enumerate(spans):
                    ins = nc.scalar.activation(sl[:, u, off:off + nt], M.PS[:, 4 * u + a, 0:nt], ACT.Silu)
                    off += nt
                ins.then_inc(s["silu_done"], 1)

            S.highs(act, out, None if scores else spread, spread if scores else None)

        @block.vector
        def _(dve):
            dve.sem_inc(s["psum_free"], 2)
            if scores:
                R.choose(dve)
            with dve.Fori(0, NF // 2) as i:
                for u in range(2):
                    n = 2 * i + u
                    dve.wait_ge(s["silu_done"], n + 1)
                    off = 0
                    for a, (_, nt) in enumerate(spans):
                        ins = nc.vector.tensor_tensor(pr[:, u, off:off + nt], sl[:, u, off:off + nt],
                                                      M.PS[:, 4 * u + 2 + a, 0:nt], ALU.mult)
                        off += nt
                    ins.then_inc(s["psum_free"], 1)
                    dve.wait_ge(s["psum_free"], n + 3)
                    if gates is not None:
                        dve.wait_ge(s["spread_out"], NG_)
                        nc.vector.tensor_tensor(pr[:, u:u + 1], pr[:, u:u + 1], at(gates, i, slice(None)),
                                                ALU.mult).then_inc(s["gated"], 1)
                        dve.wait_ge(s["gated"], n + 1)
                    high = at(hid[:, 0], n, slice(None))
                    nc.vector.tensor_copy(high, pr[:, u:u + 1]).then_inc(s["high_out"], 1)
                    dve.wait_ge(s["high_out"], n + 1)
                    nc.vector.tensor_tensor(at(hid[:, 1], n, slice(None)), pr[:, u:u + 1], high.bitcast(F32),
                                            ALU.subtract).then_inc(s["low_out"], 1)
    give(nc, s, S.ready)


def block_one(nc, M, A):
    def tensor(ctx, name, shape, dt=F32):
        return ctx.enter_context(M.nc.sbuf_tensor("one_" + name, shape, dt))

    M.rope = nc.dram_tensor("rope_tables", (P, 2, T), F32).ap()
    setup(nc, M, A)
    NF = NE * FE // P // ROUNDS
    with nc.Fori(0, DEPTH) as l:
        adopt(nc, M, (1, 2, 4, 5))
        with ExitStack() as ctx:
            B = Buffers()
            B.PT = tensor(ctx, "projT", [P, N_CH, T])
            B.V = tensor(ctx, "values", [P, TT, N_V])
            B.iw = tensor(ctx, "index_w", [P, TT * NH_I])
            B.bias = tensor(ctx, "key_bias", [P, TT, T])
            with ExitStack() as inner:
                M.hR = tensor(inner, "mix_h_parts", [P, 2, KD, T], F32R)
                with M.nc.sbuf_tensor("hT_mix", [P, KD, T], F32) as M.hT:
                    proj1(nc, M, A, l, B, value_weights(A, l))
                project_values(nc, M, value_weights(A, l), N_V // VC, B.V, TT, out_weights(A, l), B)
            B.mixT = tensor(ctx, "mixT", [P, KD, T])
            with ExitStack() as inner:
                B.L = tensor(inner, "mixer_consts", [P, L_N])
                B.Amax = tensor(inner, "i_max_all", [P, NH_M, T])
                B.floor = tensor(inner, "floor_all", [P, NH_M // 2, T])
                B.acol = tensor(inner, "i_rel_col", [P, TT * NH_M])
                B.Y = tensor(inner, "lin_y", [P, 4, T])
                convolve(nc, M, A, l, B)
                attend1(nc, M, B)
                linear_mixers(nc, M, B)
                head_norm(nc, M, B)
            M.hR = tensor(ctx, "mix_parts", [P, 2, KD, T], F32R)
            gemm_residual(nc, M, out_weights(A, l), M.hR, [(0, T, 0)], 2, ALPHA, gate_up_weights(A, l, 0, NF),
                          mix=B.mixT)
        layer_norm(nc, M, A["ln_mix"][l])
        with ExitStack() as ctx:
            M.hR = tensor(ctx, "ffn_h_parts", [P, 2, KD, T], F32R)
            gT = tensor(ctx, "gate_rows", [NE, T])
            scores = tensor(ctx, "router_scores", [P, TT, NE]), tensor(ctx, "router_biased", [P, TT, NE])
            with ExitStack() as inner:
                M.hT = tensor(inner, "hT_ffn", [P, KD, T])
                route(nc, M, A, *scores)
            hid = tensor(ctx, "hidden", [P, 2, NF, T], F32R)
            for r in range(ROUNDS):
                with M.nc.sbuf_tensor(f"expert_gates{r}", [P, NE // ROUNDS, T], F32) as gates:
                    gated_up(nc, M, gate_up_weights(A, l, r, NF), hid, NF, [(0, T)], down_weights(A, l, r, NF),
                             gates, gT, r * NE // ROUNDS, None if r else scores)
                per = N_MOD // ROUNDS // KD
                ride = (modulation(A, l + 1, per), A["b_ada"][l + 1], A["cond"][l], r * KD * per, per)
                following = (gate_up_weights(A, l, r + 1, NF) if r + 1 < ROUNDS else proj_weights(A, l + 1))
                gemm_residual(nc, M, down_weights(A, l, r, NF), hid, [(0, T, 0)], 5, 1.0 if r else ALPHA,
                              following, ride=ride)
        layer_norm(nc, M, A["ln_ffn"][l])


def rms_modulate(nc, M, w, spans, shift=None, scale=None):
    s = take(M, "par ws sq sum sd rstd norm h_f32 h_high h_done")
    NS = len(spans)
    with ExitStack() as ctx:
        nw = ctx.enter_context(M.nc.sbuf_tensor(f"{M.blocks}_norm_w", [P, KD], F32))
        ws = ctx.enter_context(M.nc.sbuf_tensor(f"{M.blocks}_norm_ws", [P, 2, KD], F32))
        sq = ctx.enter_context(M.nc.sbuf_tensor(f"{M.blocks}_rms_sq", [P, 4, T], F32))
        rs = ctx.enter_context(M.nc.sbuf_tensor(f"{M.blocks}_rms_rs", [P, 2, T], F32))
        block = ctx.enter_context(nc.Block())

        @block.sync
        def _(sp):
            sp.dma_start(nw[:], w).then_inc(s["par"], 16)

        @block.tensor
        def _(pe):
            for a, (t0, nt, c) in enumerate(spans):
                for k in range(KD):
                    n = a * KD + k
                    pe.wait_ge(s["sq"], n + 1)
                    nc.tensor.matmul(M.PS[:, a, 0:nt], M.K[:, K_MEAN:K_MEAN + P], sq[:, n % 4, 0:nt],
                                     start=(k == 0), stop=(k == KD - 1)).then_inc(s["sum"], 1)

        @block.vector
        def _(dve):
            dve.wait_ge(s["par"], 16)
            for a, (t0, nt, c) in enumerate(spans):
                if scale is None:
                    nc.vector.tensor_copy(ws[:, a, :], nw[:]).then_inc(s["ws"], 1)
                else:
                    part = M.mod[:, scale * KD * 2:(scale + 1) * KD * 2].rearrange("p (k c) -> p k c", c=2)
                    nc.vector.tensor_tensor(ws[:, a, :], nw[:], part[:, :, c], ALU.mult).then_inc(s["ws"], 1)
            for a, (t0, nt, c) in enumerate(spans):
                dve.wait_ge(s["sd"], a + 1)
                nc.vector.reciprocal(rs[:, a, 0:nt], rs[:, a, 0:nt]).then_inc(s["rstd"], 1)
                dve.wait_ge(s["rstd"], a + 1)
                for k in range(KD):
                    nc.vector.tensor_tensor(M.hT[:, k, t0:t0 + nt], M.xT[:, k, t0:t0 + nt], rs[:, a, 0:nt],
                                            ALU.mult).then_inc(s["norm"], 1)
            if scale is not None:
                for a, (t0, nt, c) in enumerate(spans):
                    for k in range(KD):
                        dve.wait_ge(s["h_high"], a * KD + k + 1)
                        nc.vector.tensor_tensor(M.hR[:, 1, k, t0:t0 + nt], M.hT[:, k, t0:t0 + nt],
                                                M.hR[:, 0, k, t0:t0 + nt].bitcast(F32),
                                                ALU.subtract).then_inc(s["h_done"], 1)

        @block.scalar
        def _(act):
            for a, (t0, nt, c) in enumerate(spans):
                for k in range(KD):
                    n = a * KD + k
                    if n >= 4:
                        act.wait_ge(s["sum"], n - 3)
                    nc.scalar.activation(sq[:, n % 4, 0:nt], M.xT[:, k, t0:t0 + nt], ACT.Square).then_inc(s["sq"], 1)
                act.wait_ge(s["sum"], (a + 1) * KD)
                nc.scalar.activation(rs[:, a, 0:nt], M.PS[:, a, 0:nt], ACT.Sqrt, bias=M.eps[:, 1:2]).then_inc(s["sd"], 1)
            act.wait_ge(s["ws"], NS)
            for a, (t0, nt, c) in enumerate(spans):
                for k in range(KD):
                    act.wait_ge(s["norm"], a * KD + k + 1)
                    h = M.hT[:, k, t0:t0 + nt]
                    bias = 0.0 if shift is None else modcol(M, shift, k, c)
                    nc.scalar.activation(h, h, ACT.Identity, bias=bias, scale=ws[:, a, k:k + 1]).then_inc(s["h_f32"], 1)
            if scale is not None:
                for a, (t0, nt, c) in enumerate(spans):
                    for k in range(KD):
                        act.wait_ge(s["h_f32"], a * KD + k + 1)
                        nc.scalar.activation(M.hR[:, 0, k, t0:t0 + nt], M.hT[:, k, t0:t0 + nt],
                                             ACT.Copy).then_inc(s["h_high"], 1)
    give(nc, s)


def project(nc, M, weights, N, out, spans, following, loads=()):
    s = take(M, STREAM + "psum_free copied more")
    with ExitStack() as ctx:
        S = Stream(nc, M, ctx, s, weights, N, following)
        block = ctx.enter_context(nc.Block())

        @block.sync
        def _(sp):
            S.load(sp)
            for dst, src in loads:
                sp.dma_start(dst, src).then_inc(s["more"], 16)
            if loads:
                sp.wait_ge(s["more"], 16 * len(loads))

        @block.gpsimd
        def _(pool):
            S.lows(pool)

        @block.tensor
        def _(pe):
            def chunk(n, u, w, low_ready):
                pe.wait_ge(s["psum_free"], n + 1)
                terms = [(M.PS[:, 4 * u + a, 0:nt], [(blocks(w, k), tokens(M.hR, k, t0, nt)) for k in range(KD)])
                         for a, (t0, nt) in enumerate(spans)]
                return products(nc, terms, low_ready)

            S.open(pe)
            S.multiply(pe, chunk)

        @block.scalar
        def _(act):
            act.sem_inc(s["psum_free"], 2)

            def copy(n, u):
                act.wait_ge(s["used"], n + 3)
                off = 0
                for a, (_, nt) in enumerate(spans):
                    ins = nc.scalar.activation(at(out, n, slice(off, off + nt)), M.PS[:, 4 * u + a, 0:nt], ACT.Copy)
                    off += nt
                ins.then_inc(s["copied"], 1)
                act.wait_ge(s["copied"], n + 1)
                act.sem_inc(s["psum_free"], 1)

            S.highs(act, copy)
    give(nc, s, S.ready)


def project_values(nc, M, weights, N, out, tiles, following, B=None):
    s = take(M, STREAM + "psum_free copied scored taken step")
    with ExitStack() as ctx:
        S = Stream(nc, M, ctx, s, weights, N, following)
        K = SelectKeys(nc, M, ctx, s, B) if B else None
        block = ctx.enter_context(nc.Block())

        @block.sync
        def _(sp):
            S.load(sp)

        @block.gpsimd
        def _(pool):
            S.lows(pool)

        @block.tensor
        def _(pe):
            def chunk(n, u, w, low_ready):
                pe.wait_ge(s["psum_free"], n + 1)
                for odd in range(2):
                    terms = [(M.PS[:, 4 * u + t // 2, odd * VC:(odd + 1) * VC],
                              [(blocks(w, slice(2 * k, 2 * k + 2)), tokens(M.hR, k, t * P, P)) for k in range(KD)])
                             for t in range(odd, tiles, 2)]
                    mm = products_moving(nc, terms, low_ready)
                return mm

            S.open(pe)
            if K:
                for n in range(N):
                    K.scores(pe, n)
                    S.one(pe, chunk, n, n % 2)
            else:
                S.multiply(pe, chunk)

        @block.vector
        def _(dve):
            if K:
                K.choose(dve)

        @block.scalar
        def _(act):
            act.sem_inc(s["psum_free"], 2)

            def copy(n, u):
                act.wait_ge(s["used"], n + 3)
                src = M.PS[:, 4 * u:4 * u + tiles // 2, :].rearrange("p b (t v) -> p (b t) v", v=VC)
                nc.scalar.activation(out[:, :, bass.ds(n * VC, VC)], src, ACT.Copy).then_inc(s["copied"], 1)
                act.wait_ge(s["copied"], n + 1)
                act.sem_inc(s["psum_free"], 1)

            S.highs(act, copy)
    give(nc, s, S.ready)


def spatial_gate(nc, M, A, B):
    s = take(M, "rel_in par gelu_v ssq sd rstd normed gelu_u gate biased done")
    NT = TA // P
    with ExitStack() as ctx:
        sw = ctx.enter_context(M.nc.sbuf_tensor(f"{M.blocks}_sgu_w", [P, 4, P], F32))
        sb_ = ctx.enter_context(M.nc.sbuf_tensor(f"{M.blocks}_sgu_b", [P, 4 * P], F32))
        nw = ctx.enter_context(M.nc.sbuf_tensor(f"{M.blocks}_sgu_nw", [P, 4], F32))
        ssq = ctx.enter_context(M.nc.sbuf_tensor(f"{M.blocks}_sgu_ssq", [P, NT], F32))
        junk = ctx.enter_context(M.nc.sbuf_tensor(f"{M.blocks}_sgu_sq", [P, NT, 512], F32))
        g_ = ctx.enter_context(M.nc.sbuf_tensor(f"{M.blocks}_sgu_gate", [P, 2, 512], F32))
        block = ctx.enter_context(nc.Block())

        @block.sync
        def _(sp):
            sp.dma_start(sw[:], A["sgu_w"]).then_inc(s["par"], 16)
            sp.dma_start(sb_[:], A["sgu_b"].partition_broadcast(P)).then_inc(s["par"], 16)
            sp.dma_start(nw[:], A["sgu_nw"]).then_inc(s["par"], 16)
            sp.dma_start(B.rel[:], A["rel"]).then_inc(s["rel_in"], 16)
            sp.wait_ge(s["rel_in"], 16)

        @block.scalar
        def _(act):
            for t in range(NT):
                v = B.V[:, t, 0:512]
                nc.scalar.activation(v, v, ACT.Gelu_apprx_tanh).then_inc(s["gelu_v"], 1)
            for c in range(4):
                u = B.PT[:, c, :]
                nc.scalar.activation(u, u, ACT.Gelu_apprx_tanh).then_inc(s["gelu_u"], 1)
            for t in range(NT):
                act.wait_ge(s["gelu_v"], t + 1)
                nc.scalar.activation(junk[:, t, :], B.V[:, t, 0:512], ACT.Square,
                                     accum_out=ssq[:, t:t + 1]).then_inc(s["ssq"], 1)
            act.wait_ge(s["ssq"], NT)
            nc.scalar.activation(ssq[:], ssq[:], ACT.Sqrt, bias=M.eps[:, 1:2], scale=1.0 / 512).then_inc(s["sd"], 1)

        @block.vector
        def _(dve):
            dve.wait_ge(s["sd"], 1)
            nc.vector.reciprocal(ssq[:], ssq[:]).then_inc(s["rstd"], 1)
            dve.wait_ge(s["rstd"], 1)
            for t in range(NT):
                v = B.V[:, t, 0:512]
                nc.vector.tensor_scalar(v, v, ssq[:, t:t + 1], None, ALU.mult).then_inc(s["normed"], 1)
            dve.wait_ge(s["par"], 48)
            n = 0
            for g in range(4):
                dve.wait_ge(s["gate"], g + 1)
                dve.wait_ge(s["gelu_u"], g + 1)
                for a, (t0, nt) in enumerate(((0, T), (T, TC))):
                    out = g_[:, a, 0:nt].rearrange("p (t q) -> p t q", q=P)
                    bias = sb_[:, g * P:(g + 1) * P].unsqueeze(1).to_broadcast([P, nt // P, P])
                    nc.vector.scalar_tensor_tensor(out=out, in0=M.PS[:, 2 * g + a, 0:nt].rearrange("p (t q) -> p t q", q=P),
                                                   scalar=nw[:, g:g + 1], in1=bias, op0=ALU.mult,
                                                   op1=ALU.add).then_inc(s["biased"], 1)
                    n += 1
                    dve.wait_ge(s["biased"], n)
                    nc.vector.tensor_tensor(B.mixT[:, g, t0:t0 + nt], g_[:, a, 0:nt], B.PT[:, g, t0:t0 + nt],
                                            ALU.mult).then_inc(s["done"], 1)

        @block.tensor
        def _(pe):
            pe.wait_ge(s["par"], 48)
            pe.wait_ge(s["normed"], NT)
            for g in range(4):
                for t in range(NT):
                    mm = nc.tensor.matmul(M.PS[:, 2 * g + t // 4, (t % 4) * P:(t % 4 + 1) * P],
                                          B.V[:, t, g * P:(g + 1) * P], sw[:, g, :], start=True, stop=True)
                mm.then_inc(s["gate"], 1)
    give(nc, s)


def attend2(nc, M, B):
    items = []
    for t in range(TA // P):
        for h in range(8):
            b, c = HD * (h % 2), h // 2
            ctx_keys = (B.PT[b:b + HD, 8 + c, T:TA], TC, None)
            grid_keys = (B.PT[b:b + HD, 8 + c, 0:T], T, B.rel[:, h, (7 - 2 * t) * 64:(15 - 2 * t) * 64])
            latent = t < TT
            items.append(Item(
                q=B.PT[b:b + HD, 4 + c, t * P:(t + 1) * P],
                segs=[grid_keys, ctx_keys] if latent else [ctx_keys],
                vs=[B.V[:, j, 512 + h * HD:512 + (h + 1) * HD] for j in range(0 if latent else TT, TA // P)],
                o=B.mixT[:, 4 + c, t * P:(t + 1) * P]))
    attend(nc, M, items, HD ** -0.5)


class Fourier:

    BANKS = (0, 1, 6, 7)

    def __init__(self, nc, M, ctx, s, A, B):
        self.nc, self.M, self.s, self.A, self.B = nc, M, s, A, B
        self.FT = ctx.enter_context(nc.sbuf_tensor(f"{M.blocks}_dft_t", [P, 2, TT, T], F32))
        self.G = ctx.enter_context(nc.sbuf_tensor(f"{M.blocks}_dft_g", [P, 8, 2 * P], F32))

    def mixed(self, n, a, z):
        if n < 8:
            return self.B.mixT[:, 4 + n // 2, n % 2 * 2 * P + a:n % 2 * 2 * P + z]
        return self.G[:, n - 8, a:z]

    def load(self, sp):
        sp.dma_start(self.FT[:], self.A["dft_t"]).then_inc(self.s["tab"], 16)

    def channels(self, pe):
        B = self.B
        for n in range(16):
            g, t = n // TT, n % TT
            if n >= 2:
                pe.wait_ge(self.s["ch_out"], n - 1)
            self.nc.tensor.matmul(self.M.PS[:, 6 + n % 2, 0:2 * P], B.PT[:, g, t * P:(t + 1) * P],
                                  B.K2[:, J_DFT:J_DFT + 2 * P], start=True, stop=True).then_inc(self.s["ch"], 1)

    def tokens(self, pe):
        pe.wait_ge(self.s["tab"], 16)
        pe.wait_ge(self.s["ch_out"], 16)
        for g in range(4):
            for t in range(TT):
                for j in range(2):
                    mm = self.nc.tensor.matmul(self.M.PS[:, self.BANKS[g], :], self.mixed(g * TT + t, j * P, (j + 1) * P),
                                               self.FT[:, j, t, :], start=(t + j == 0),
                                               stop=(t == TT - 1 and j == 1))
            mm.then_inc(self.s["tok"], 1)

    def copy_channels(self, act):
        for n in range(16):
            act.wait_ge(self.s["ch"], n + 1)
            self.nc.scalar.activation(self.mixed(n, 0, 2 * P), self.M.PS[:, 6 + n % 2, 0:2 * P],
                                      ACT.Copy).then_inc(self.s["ch_out"], 1)

    def copy_results(self, act):
        for g in range(4):
            act.wait_ge(self.s["tok"], g + 1)
            self.nc.scalar.activation(self.B.mixT[:, g, :], self.M.PS[:, self.BANKS[g], :], ACT.Copy)


def gla_prepare(nc, M, A, B):
    s = take(M, "par rot step z lin e1 la ex exd step2 tab ch ch_out tok")
    NC = TA // 64
    with ExitStack() as ctx:
        dw = ctx.enter_context(M.nc.sbuf_tensor(f"{M.blocks}_dec_w", [48, 256], F32))
        db = ctx.enter_context(M.nc.sbuf_tensor(f"{M.blocks}_dec_b", [P, 4], F32))
        t1 = ctx.enter_context(M.nc.sbuf_tensor(f"{M.blocks}_ax1", [P, T], F32))
        t2 = ctx.enter_context(M.nc.sbuf_tensor(f"{M.blocks}_ax2", [P, T], F32))
        la = ctx.enter_context(M.nc.sbuf_tensor(f"{M.blocks}_log_a", [P, 4, TA], F32))
        z = ctx.enter_context(M.nc.sbuf_tensor(f"{M.blocks}_dec_z", [P, 4, TA], F32))
        pre = ctx.enter_context(M.nc.sbuf_tensor(f"{M.blocks}_dec_pre", [P, 4, TA], F32))
        F = Fourier(nc, M, ctx, s, A, B)
        block = ctx.enter_context(nc.Block())

        @block.sync
        def _(sp):
            sp.dma_start(dw[0:16], A["dec_w"][0]).then_inc(s["par"], 16)
            sp.dma_start(dw[32:48], A["dec_w"][1]).then_inc(s["par"], 16)
            sp.dma_start(db[:], A["dec_b"]).then_inc(s["par"], 16)
            F.load(sp)

        @block.tensor
        def _(pe):
            pe.wait_ge(s["par"], 48)
            for j in range(4):
                d, c = j // 2, j % 2
                if j >= 1:
                    pe.wait_ge(s["lin"], j)
                nc.tensor.matmul(M.PS[:, 0, :], dw[32 * d:32 * d + 16, c * P:(c + 1) * P],
                                 B.KA[32 * d:32 * d + 16, 2, 0:T], start=True, stop=True)
                nc.tensor.matmul(M.PS[:, 1, 0:TC], dw[32 * d:32 * d + 16, c * P:(c + 1) * P],
                                 B.KA[32 * d:32 * d + 16, 2, T:TA], start=True, stop=True).then_inc(s["z"], 1)
            for j in range(4):
                x = B.PT[:, 4 + j, 0:T] if j < 2 else B.KA[:, j - 2, 0:T]
                nc.tensor.matmul(M.PS[:, 2 + j, :], B.K2[:, J_ROT:J_ROT + P], x, start=True,
                                 stop=True).then_inc(s["rot"], 1)
            F.channels(pe)
            pe.wait_ge(s["lin"], 4)
            F.tokens(pe)

        @block.vector
        def _(dve):
            step = Steps(dve, s["step"])
            tt, ts, stt = nc.vector.tensor_tensor, nc.vector.tensor_scalar, nc.vector.scalar_tensor_tensor
            dve.wait_ge(s["par"], 48)
            for j in range(4):
                dve.wait_ge(s["z"], j + 1)
                step(ts(z[:, j, 0:T], M.PS[:, 0, :], db[:, j:j + 1], None, ALU.add))
                ts(z[:, j, T:TA], M.PS[:, 1, 0:TC], db[:, j:j + 1], None, ALU.add).then_inc(s["lin"], 1)
                dve.wait_ge(s["lin"], j + 1)
                stt(out=la[:, j, :], in0=z[:, j, :], scalar=-1.0, in1=z[:, j, :], op0=ALU.mult,
                    op1=ALU.max).then_inc(s["e1"], 1)
            for j in range(4):
                x = B.PT[:, 4 + j, 0:T] if j < 2 else B.KA[:, j - 2, 0:T]
                dve.wait_ge(s["rot"], j + 1)
                step(tt(t1[:], x, B.K2[:, J_COS:J_COS + T], ALU.mult))
                step(tt(t2[:], M.PS[:, 2 + j, :], B.K2[:, J_SIN:J_SIN + T], ALU.mult))
                step(tt(x, t1[:], t2[:], ALU.add))
            for j in range(4):
                d = j // 2
                dve.wait_ge(s["la"], j + 1)
                step(stt(out=la[:, j, :], in0=z[:, j, :], scalar=0.0, in1=la[:, j, :], op0=ALU.min, op1=ALU.subtract))
                step(ts(la[:, j, :], la[:, j, :], 1.0 / 16, None, ALU.mult))
                step(nc.vector.tensor_tensor_scan(out=pre[:, j, :], data0=B.K2[:, J_RST:J_RST + TA], data1=la[:, j, :],
                                                  initial=0.0, op0=ALU.mult, op1=ALU.add))
                p3 = pre[:, j, :].rearrange("p (n l) -> p n l", l=64)
                z3 = z[:, j, :].rearrange("p (n l) -> p n l", l=64)
                total = p3[:, :, 63:64].to_broadcast([P, NC, 64])
                step(nc.vector.tensor_copy(B.dec[:, j, :], p3[:, :, 63]))
                if d == 0:
                    tt(z3, total, p3, ALU.subtract).then_inc(s["ex"], 1)
                else:
                    step(tt(z3, total, p3, ALU.subtract))
                    step(tt(t1[:], z[:, j, 0:T], la[:, j, 0:T], ALU.add))
                    step(tt(z[:, j, :], pre[:, j, :], la[:, j, :], ALU.subtract))
                    nc.vector.tensor_copy(pre[:, j, 0:T], t1[:]).then_inc(s["ex"], 1)
            for j in range(4):
                c = j % 2
                dve.wait_ge(s["exd"], j + 1)
                step(stt(out=B.qe[:, j, :], in0=B.PT[:, 4 + c, 0:T], scalar=64 ** -0.5, in1=B.qe[:, j, :],
                         op0=ALU.mult, op1=ALU.mult))
                step(tt(B.ke[:, j, :], B.KA[:, c, 0:T], B.ke[:, j, :], ALU.mult))
                step(tt(B.kd[:, j, :], B.KA[:, c, :], B.kd[:, j, :], ALU.mult))

        @block.scalar
        def _(act):
            step = Steps(act, s["step2"])
            for j in range(4):
                act.wait_ge(s["e1"], j + 1)
                step(nc.scalar.activation(la[:, j, :], la[:, j, :], ACT.Exp, scale=-1.0))
            for j in range(4):
                nc.scalar.activation(la[:, j, :], la[:, j, :], ACT.Ln, bias=1.0).then_inc(s["la"], 1)
            F.copy_channels(act)
            for j in range(4):
                act.wait_ge(s["ex"], j + 1)
                step(nc.scalar.activation(B.dec[:, j, :], B.dec[:, j, :], ACT.Exp))
                step(nc.scalar.activation(B.qe[:, j, :], pre[:, j, 0:T], ACT.Exp))
                step(nc.scalar.activation(B.ke[:, j, :], pre[:, j, 0:T], ACT.Exp, scale=-1.0))
                nc.scalar.activation(B.kd[:, j, :], z[:, j, :], ACT.Exp).then_inc(s["exd"], 1)
            for c in range(4):
                nc.scalar.activation(B.PT[:, 6 + c, 0:T], B.PT[:, 6 + c, 0:T], ACT.Silu)
            F.copy_results(act)
    give(nc, s)


def gla_states(nc, M, B):
    s = take(M, "tr tr_out kv kv_free state")
    NT = TA // P
    with ExitStack() as ctx:
        kt = ctx.enter_context(M.nc.sbuf_tensor(f"{M.blocks}_kd_tok", [P, 2, NT, 256], F32))
        S = ctx.enter_context(M.nc.sbuf_tensor(f"{M.blocks}_state", [P, 2, 2, P], F32))
        block = ctx.enter_context(nc.Block())

        def bank(c, n):
            m = n // 2
            return M.PS[:, 4 * (n % 2) + 2 * c + m // 4, (m % 4) * P:(m % 4 + 1) * P]

        @block.tensor
        def _(pe):
            for d in range(2):
                if d:
                    pe.wait_ge(s["kv_free"], 1)
                for t in range(NT):
                    n = d * NT + t
                    if t >= 2:
                        pe.wait_ge(s["tr_out"], n - 1)
                    for c in range(2):
                        mm = nc.tensor.transpose(M.PS[:, t % 2, c * P:(c + 1) * P], B.kd[:, 2 * d + c, t * P:(t + 1) * P],
                                                 M.K[:, K_ID:K_ID + P])
                    mm.then_inc(s["tr"], 1)
                pe.wait_ge(s["tr_out"], (d + 1) * NT)
                for odd in range(2):
                    for n in range(odd, 2 * NT, 2):
                        for h in range(4):
                            b, r = 64 * (h % 2), 64 * odd
                            mm = nc.tensor.matmul(bank(h // 2, n)[b:b + 64], kt[r:r + 64, d, n // 2, h * 64:(h + 1) * 64],
                                                  B.V[r:r + 64, n // 2, h * P:(h + 1) * P], start=True, stop=True)
                mm.then_inc(s["kv"], 1)

        @block.scalar
        def _(act):
            for d in range(2):
                for t in range(NT):
                    act.wait_ge(s["tr"], d * NT + t + 1)
                    nc.scalar.activation(kt[:, d, t, :], M.PS[:, t % 2, 0:256], ACT.Copy).then_inc(s["tr_out"], 1)

        @block.vector
        def _(dve):
            done = 0
            for d in range(2):
                dve.wait_ge(s["kv"], d + 1)
                order = [8, 9, 10, 11] + list(range(8))
                if d:
                    order = [11, 10, 9, 8] + list(range(7, -1, -1))
                for i, n in enumerate(order[:-1]):
                    nxt = order[i + 1]
                    for c in range(2):
                        out = B.Sp[:, d, c, nxt, :] if nxt < 8 else S[:, c, i % 2, :]
                        if i == 0:
                            ins = nc.vector.tensor_copy(out, bank(c, n))
                        else:
                            cur = B.Sp[:, d, c, n, :] if n < 8 else S[:, c, (i - 1) % 2, :]
                            dve.wait_ge(s["state"], done - 1)
                            ins = nc.vector.scalar_tensor_tensor(out=out, in0=cur, scalar=B.dec[:, 2 * d + c, n:n + 1],
                                                                 in1=bank(c, n), op0=ALU.mult, op1=ALU.add)
                        ins.then_inc(s["state"], 1)
                        done += 1
                dve.wait_ge(s["state"], done)
                dve.sem_inc(s["kv_free"], 1)
    give(nc, s)


def gla_outputs(nc, M, A, B):
    s = take(M, "par att masked pv sq ssum sd rstd norm done")
    with ExitStack() as ctx:
        am = ctx.enter_context(M.nc.sbuf_tensor(f"{M.blocks}_gla_att", [P, 2, 2 * P], F32))
        hw = ctx.enter_context(M.nc.sbuf_tensor(f"{M.blocks}_gla_hw", [P, 2], F32))
        sq = ctx.enter_context(M.nc.sbuf_tensor(f"{M.blocks}_gla_sq", [P, 4, T], F32))
        nm = ctx.enter_context(M.nc.sbuf_tensor(f"{M.blocks}_gla_nm", [P, 4, T], F32))
        block = ctx.enter_context(nc.Block())
        N = 4 * TT

        @block.sync
        def _(sp):
            sp.dma_start(hw[:, 0:1], A["head_w"]).then_inc(s["par"], 16)

        @block.tensor
        def _(pe):
            def scores(n):
                h, t = n // TT, n % TT
                b, c = 64 * (h % 2), h // 2
                if n >= 2:
                    pe.wait_ge(s["masked"], n - 1)
                for d in range(2):
                    mm = nc.tensor.matmul(M.PS[:, n % 2, d * P:(d + 1) * P], B.ke[b:b + 64, 2 * d + c, t * P:(t + 1) * P],
                                          B.qe[b:b + 64, 2 * d + c, t * P:(t + 1) * P], start=True, stop=True)
                mm.then_inc(s["att"], 1)

            def values(n):
                h, t = n // TT, n % TT
                b, c = 64 * (h % 2), h // 2
                pe.wait_ge(s["masked"], n + 1)
                for d in range(2):
                    nc.tensor.matmul(M.PS[:, 2 + h, t * P:(t + 1) * P], B.V[:, t, h * P:(h + 1) * P],
                                     am[:, n % 2, d * P:(d + 1) * P], start=(d == 0), stop=False)
                for d in range(2):
                    for j in range(2):
                        at = t * P + j * 64
                        last = d == 1 and j == 1
                        mm = nc.tensor.matmul(M.PS[:, 2 + h, at:at + 64], B.Sp[b:b + 64, d, c, 2 * t + j, :],
                                              B.qe[b:b + 64, 2 * d + c, at:at + 64], start=False, stop=last)
                mm.then_inc(s["pv"], 1)

            for n in range(N + 1):
                if n < N:
                    scores(n)
                if n >= 1:
                    values(n - 1)
            for h in range(4):
                pe.wait_ge(s["sq"], h + 1)
                if h >= 2:
                    pe.wait_ge(s["sd"], h - 1)
                nc.tensor.matmul(M.PS[:, 6 + h % 2, :], M.K[:, K_ONE:K_ONE + P], sq[:, h, :], start=True,
                                 stop=True).then_inc(s["ssum"], 1)

        @block.vector
        def _(dve):
            for n in range(N):
                dve.wait_ge(s["att"], n + 1)
                if n >= 2:
                    dve.wait_ge(s["pv"], n - 1)
                nc.vector.tensor_tensor(am[:, n % 2, :], M.PS[:, n % 2, 0:2 * P], B.K2[:, J_MASK:J_MASK + 2 * P],
                                        ALU.mult).then_inc(s["masked"], 1)
            dve.wait_ge(s["par"], 16)
            for h in range(4):
                dve.wait_ge(s["sd"], h + 1)
                nc.vector.reciprocal(sq[:, h, :], sq[:, h, :]).then_inc(s["rstd"], 1)
                dve.wait_ge(s["rstd"], h + 1)
                nc.vector.tensor_tensor(nm[:, h, :], M.PS[:, 2 + h, :], sq[:, h, :], ALU.mult).then_inc(s["norm"], 1)
                dve.wait_ge(s["norm"], h + 1)
                nc.vector.scalar_tensor_tensor(out=B.mixT[:, 4 + h, :], in0=nm[:, h, :], scalar=hw[:, 0:1],
                                               in1=B.PT[:, 6 + h, 0:T], op0=ALU.mult, op1=ALU.mult).then_inc(s["done"], 1)

        @block.scalar
        def _(act):
            for h in range(4):
                act.wait_ge(s["pv"], TT * (h + 1))
                nc.scalar.activation(sq[:, h, :], M.PS[:, 2 + h, :], ACT.Square).then_inc(s["sq"], 1)
            for h in range(4):
                act.wait_ge(s["ssum"], h + 1)
                nc.scalar.activation(sq[:, h, :], M.PS[:, 6 + h % 2, :], ACT.Sqrt, bias=M.eps[:, 1:2],
                                     scale=1.0 / P).then_inc(s["sd"], 1)
    give(nc, s)


def ffn_up(A, i, f0):
    return lambda n: A["f_gu"][i, n + f0], 2 * KD


def ffn_down(A, i, f0, NF):
    return lambda n: A["f_down"][i, n, :, f0:f0 + NF], NF


def feed_forward(nc, M, A, i, spans, rounds, following):
    with ExitStack() as ctx:
        def tensor(name, shape, dt, where=ctx):
            return where.enter_context(M.nc.sbuf_tensor(f"ffn{i}_{name}", shape, dt))

        TW = sum(n for _, n, _ in spans)
        M.hR = tensor("h_parts", [P, 2, KD, TW], F32R)
        with ExitStack() as inner:
            M.hT = tensor("hT", [P, KD, TW], F32, inner)
            rms_modulate(nc, M, A["norm_ffn"][i], spans, 3, 4)
        hid = tensor("hidden", [P, 2, max(rounds), TW], F32R)
        f0 = 0
        for r, NF in enumerate(rounds):
            gated_up(nc, M, ffn_up(A, i, f0), hid, NF, [(t, n) for t, n, _ in spans], ffn_down(A, i, f0, NF))
            ride = None
            if i == 0:
                per = N_MOD // len(rounds) // KD
                ride = (modulation(A, 3, per), A["b_ada"][3], A["cond"][1], r * KD * per, per)
            after = ffn_up(A, i, f0 + NF) if r + 1 < len(rounds) else following
            gemm_residual(nc, M, ffn_down(A, i, f0, NF), hid, spans, 5, 1.0, after, ride=ride)
            f0 += NF


def block_two(nc, M, A):
    both = [(0, T, 0), (T, TC, 1)]
    latent = both[:1]
    ab_out, cd_t, cd_k, cd_out = ((lambda n, w=A[name]: w[n], KD) for name in ("ab_out", "cd_t", "cd_k", "cd_out"))
    ab_v, cd_v = ((lambda n, w=A[name]: w[n], 2 * KD) for name in ("ab_v", "cd_v"))

    def tensor(ctx, name, shape, dt=F32):
        return ctx.enter_context(M.nc.sbuf_tensor("two_" + name, shape, dt))

    adopt(nc, M, (1, 4))
    with ExitStack() as ctx:
        B = Buffers()
        B.PT, B.V = tensor(ctx, "ab_projT", [P, 12, TA]), tensor(ctx, "ab_values", [P, TA // P, 1024])
        with ExitStack() as inner:
            M.hR = tensor(inner, "ab_h_parts", [P, 2, KD, TA], F32R)
            M.hT = tensor(inner, "ab_hT", [P, KD, TA])
            rms_modulate(nc, M, A["norm_mix"][0], both, 0, 1)
            project(nc, M, proj_weights(A, DEPTH), 12, B.PT, [(0, T), (T, TC)], ab_v)
            project_values(nc, M, ab_v, 1024 // VC, B.V, TA // P, ab_out)
        B.mixT = tensor(ctx, "ab_mixT", [P, KD, TA])
        with ExitStack() as inner:
            B.rel = tensor(inner, "rel", [P, 8, 16 * 64])
            spatial_gate(nc, M, A, B)
            attend2(nc, M, B)
        M.hR = tensor(ctx, "ab_mix_parts", [P, 2, KD, TA], F32R)
        gemm_residual(nc, M, ab_out, M.hR, both, 2, 1.0, ffn_up(A, 0, 0), mix=B.mixT)
    feed_forward(nc, M, A, 0, both, (8, 8, 6), cd_t)

    adopt(nc, M, (1, 4))
    with ExitStack() as ctx:
        B = Buffers()
        B.PT, B.KA = tensor(ctx, "cd_projT", [P, 10, T]), tensor(ctx, "cd_keysT", [P, 3, TA])
        B.V, B.K2 = tensor(ctx, "cd_values", [P, TA // P, 512]), tensor(ctx, "cd_consts", [P, J_N])
        with ExitStack() as inner:
            M.hR = tensor(inner, "cd_h_parts", [P, 2, KD, TA], F32R)
            M.hT = tensor(inner, "cd_hT", [P, KD, TA])
            rms_modulate(nc, M, A["norm_mix"][1], both, 0, 1)
            project(nc, M, cd_t, 10, B.PT, [(0, T)], cd_k)
            project(nc, M, cd_k, 3, B.KA, [(0, T), (T, TC)], cd_v, [(B.K2[:], A["consts2"])])
            project_values(nc, M, cd_v, 512 // VC, B.V, TA // P, cd_out)
        B.mixT = tensor(ctx, "cd_mixT", [P, KD, T])
        with ExitStack() as inner:
            B.qe, B.ke = tensor(inner, "qe", [P, 4, T]), tensor(inner, "ke", [P, 4, T])
            B.kd, B.dec = tensor(inner, "kd", [P, 4, TA]), tensor(inner, "dec", [P, 4, TA // 64])
            gla_prepare(nc, M, A, B)
            B.Sp = tensor(inner, "Sp", [P, 2, 2, 8, P])
            gla_states(nc, M, B)
            gla_outputs(nc, M, A, B)
        M.hR = tensor(ctx, "cd_mix_parts", [P, 2, KD, T], F32R)
        gemm_residual(nc, M, cd_out, M.hR, latent, 2, 1.0, ffn_up(A, 1, 0), mix=B.mixT)
    feed_forward(nc, M, A, 1, latent, (12, 10), None)
    M.hT = M.xT
    rms_modulate(nc, M, A["final_w"], latent)


def program(nc, A, out, parts=2):
    with ExitStack() as ctx:
        def sb(name, shape):
            return ctx.enter_context(nc.sbuf_tensor(name, shape, F32))

        M = Buffers()
        M.nc, M.blocks = nc, 0
        M.PS = ctx.enter_context(nc.psum_tensor("PS", [P, 8, 512], F32))
        M.xT = sb("xT", [P, KD, TA])
        M.raw = sb("weights_raw", [P, 2, 2 * KD * P])
        M.weights_in = [[nc.alloc_semaphore(f"weights_in_{t}{u}") for u in range(2)] for t in range(3 + 2 * ROUNDS)]
        M.turn = 0
        M.K = sb("consts", [P, K_N])
        M.mod, M.mod_next = sb("mod", [P, 2 * N_MOD]), sb("mod_next", [P, 2 * N_MOD])
        M.eps = sb("eps", [P, 2])
        s = take(M, "eps_in")
        with nc.Block() as block:
            @block.vector
            def _(dve):
                nc.vector.memset(M.eps[:, 0:1], EPS).then_inc(s["eps_in"], 1)
                nc.vector.memset(M.eps[:, 1:2], RMS_EPS).then_inc(s["eps_in"], 1)
        give(nc, s)
        block_one(nc, M, A)
        if parts > 1:
            block_two(nc, M, A)
        s = take(M, "stored")
        with nc.Block() as block:
            @block.sync
            def _(sp):
                sp.dma_start(out, M.xT[:, :, 0:T]).then_inc(s["stored"], 16)
                sp.wait_ge(s["stored"], 16)
        give(nc, s)



def consts():
    K = np.zeros((P, K_N), np.float32)
    i = np.arange(P)
    K[:, K_ID:K_ID + P] = np.eye(P)
    rot = np.zeros((P, P))
    for m in range(P):
        rot[m + HALF if m % HD < HALF else m - HALF, m] = -1.0 if m % HD < HALF else 1.0
    K[:, K_ROT:K_ROT + P] = rot
    K[:, K_ONE:K_ONE + P] = 1.0
    K[:, K_MEAN:K_MEAN + P] = 1.0 / D
    K[:, K_RANK:K_RANK + NE] = NE - np.arange(NE)
    K[:, K_RANK + NE:K_RANK + NE + NG] = NG - np.arange(NG)
    K[:, K_FREQ] = np.float32(10000.0) ** (-(i % HALF).astype(np.float32) / np.float32(HALF))
    return K


def consts2():
    K = np.zeros((P, J_N), np.float32)
    i = np.arange(P)
    for m in range(P):
        K[m + 16 if m % 32 < 16 else m - 16, J_ROT + m] = -1.0 if m % 32 < 16 else 1.0
    same = i[:, None] // 64 == i[None] // 64
    K[:, J_MASK:J_MASK + P] = same & (i[:, None] <= i[None])
    K[:, J_MASK + P:J_MASK + 2 * P] = same & (i[:, None] >= i[None])
    t = np.arange(T, dtype=np.float32)
    pos = np.where((i % 64 < 32)[:, None], t[None] // 64, t[None] % 64).astype(np.float32)
    freq = (np.float32(10000.0) ** (-(i % 16).astype(np.float32) / np.float32(16))).astype(np.float32)
    ang = (pos * freq[:, None]).astype(np.float32).astype(np.float64)
    K[:, J_COS:J_COS + T], K[:, J_SIN:J_SIN + T] = np.cos(ang), np.sin(ang)
    K[:, J_RST:J_RST + TA] = np.arange(TA) % 64 != 0
    ang = 2 * np.pi * ((i[:, None] * i[None]) % P) / P
    K[:, J_DFT:J_DFT + P] = np.cos(ang) / 256
    K[:, J_DFT + P:J_DFT + 2 * P] = -np.sin(ang) / 256
    return K


def chunks(w, width=P):
    *lead, r, c = w.shape
    w = w.reshape(*lead, r // P, P, c // width, width)
    n = len(lead)
    return np.ascontiguousarray(w.transpose(*range(n), n + 2, n + 1, n, n + 3))


def value_chunks(w):
    c = chunks(w, VC)
    return c.reshape(*c.shape[:-2], -1, P)


def mixer_consts():
    L = np.zeros((P, L_N), np.float32)
    i = np.arange(P)
    d = np.arange(T)[None] - i[:, None]
    for h in range(NH_R):
        L[:, h * T:(h + 1) * T] = np.where(d >= 0, np.exp(np.maximum(d, 0) * math.log1p(-2.0 ** (-5 - h))), 0)
    L[:, L_HEAD:L_HEAD + P] = (i[:, None] // HD == i[None] // HD) / HD
    L[:, L_UP:L_UP + P] = i[:, None] <= i[None]
    for h in range(NH_M):
        L[h, L_SELH + h * P:L_SELH + (h + 1) * P] = 1.0
        L[h, L_SELP + h * HD:L_SELP + (h + 1) * HD] = 1.0
    return L


def cols(v):
    return np.ascontiguousarray(np.swapaxes(v.reshape(*v.shape[:-1], -1, P), -1, -2))


def feats(x):
    return np.ascontiguousarray(x.T.reshape(-1, P, x.shape[0]).transpose(1, 0, 2))


def layout(i):
    a = {}
    w = i["w_in"]
    o = np.cumsum([0, 512, 512, 512, 256, 64, 4, 256, 256, 256, 256, 256, 256, 256, 256, 4, 4])
    aq, ak, av, iq, ik, iw, rq, rk, rv, rg, mq, mk, mv, mo, mi, mf = (w[:, :, o[j]:o[j + 1]] for j in range(16))
    gates = np.zeros((DEPTH, D, P), np.float32)
    gates[:, :, 0:4], gates[:, :, 32:36] = mi, mf
    w_in = chunks(np.concatenate([aq, ak, iq, ik, ik, rq, rk, rg, mq, mk, mo, gates], axis=2))
    a["w_in_v"] = value_chunks(np.concatenate([av, rv, mv], axis=2))
    a["w_in_i"] = chunks(iw, NH_I)[:, 0]
    ada_w = np.stack([i["w_ada"][0], i["w_ada"][1], i["ada_w_2"][0], i["ada_w_2"][1]])
    a["w_ada"] = np.ascontiguousarray(ada_w.transpose(0, 2, 1)).reshape(2 * DEPTH * N_MOD, P, D)
    a["b_ada"] = np.repeat(cols(np.concatenate([i["b_ada"], i["ada_b_2"]])), 2, axis=2)
    cw = np.concatenate([i["conv_w"], i["conv_b"][:, None]], axis=1)
    a["conv"] = np.ascontiguousarray(cw.reshape(DEPTH, CONV + 1, 4, P).transpose(0, 3, 2, 1))
    a["gate_b"] = np.ascontiguousarray(np.stack([i["i_bias"], i["f_bias"]], axis=2))
    a["w_out"] = chunks(i["w_out"])
    for n in ("mix", "ffn"):
        a["ln_" + n] = np.ascontiguousarray(np.stack([cols(i[f"ln_{n}_g"]), cols(i[f"ln_{n}_b"])], axis=2))
    a["w_router"] = chunks(i["w_router"], NE)[0]
    a["b_router"] = i["b_router"]
    a["w_gu"] = np.concatenate([chunks(i["w_gate"]), chunks(i["w_up"])], axis=4).reshape(DEPTH, NE * 2, P, 2 * KD, P)
    a["w_down"] = chunks(i["w_down"].reshape(DEPTH, NE * FE, D))
    a["consts"] = consts()
    a["mixer_consts"] = mixer_consts()
    a["positions"] = i["positions"][0]
    a["cond"] = np.stack([np.stack([i["c"][0], i["c"][0]]), np.stack([i["c_2"][0], i["c_ctx_2"]])])
    a["x"] = feats(i["x"][0])
    a["ctx"] = feats(i["ctx_2"][0])
    a["norm_mix"], a["norm_ffn"] = cols(i["norm_mix_w_2"]), cols(i["norm_ffn_w_2"])
    a["final_w"] = cols(i["final_norm_w_2"])
    u, v, q, k, nv = np.split(i["ab_w_in_2"][0], 5, axis=1)
    a["w_proj"] = np.concatenate([w_in.reshape(-1, P, KD, P), chunks(np.concatenate([u, q, k], axis=1))])
    a["ab_v"] = value_chunks(np.concatenate([v, nv], axis=1))
    a["ab_out"] = chunks(i["ab_w_out_2"][0])
    a["sgu_w"] = np.ascontiguousarray(i["ab_sgu_w_2"][0].transpose(2, 0, 1))
    a["sgu_b"] = np.ascontiguousarray(i["ab_sgu_b_2"][0].reshape(-1))
    a["sgu_nw"] = cols(i["ab_sgu_norm_w_2"][0])
    c = np.arange(64)
    start = np.clip(c - 8, 0, 48)
    seen = (c[None] >= start[:, None]) & (c[None] < start[:, None] + 16)
    rel = i["ab_rel_bias_2"][0][:, :, np.clip(c[None] - c[:, None] + 15, 0, 30)]
    rel = np.where(seen, rel, np.float32(NEG)).transpose(2, 0, 1, 3)
    a["rel"] = np.zeros((P, 8, 16, 64), np.float32)
    a["rel"][0:64, :, 0:15] = rel
    a["rel"][64:, :, 1:16] = rel
    a["rel"] = a["rel"].reshape(P, 8, 1024)
    w = i["cd_w_in_2"][0]
    f, q, k, v, g, al = np.split(w, np.cumsum([512, 256, 256, 512, 512]), axis=1)
    a["cd_t"] = chunks(np.concatenate([f, q, g], axis=1))
    low = np.zeros((D, P), np.float32)
    low[:, 0:16], low[:, 32:48] = al[:, 0:16], al[:, 16:32]
    a["cd_k"] = chunks(np.concatenate([k, low], axis=1))
    a["cd_v"] = value_chunks(v)
    a["cd_out"] = chunks(i["cd_w_out_2"][0])
    a["dec_w"] = np.ascontiguousarray(np.stack([i["cd_decay_w_fwd_2"][0], i["cd_decay_w_bwd_2"][0]]))
    a["dec_b"] = cols(np.concatenate([i["cd_decay_b_fwd_2"][0], i["cd_decay_b_bwd_2"][0]]))
    a["head_w"] = np.ascontiguousarray(i["cd_head_norm_w_2"].reshape(P, 1))
    a["f_gu"] = np.concatenate([chunks(i["ffn_w_gate_2"]), chunks(i["ffn_w_up_2"])], axis=3)
    a["f_down"] = chunks(i["ffn_w_down_2"])
    a["consts2"] = consts2()
    ang = 2 * np.pi * ((np.arange(T)[:, None] * np.arange(T)[None]) % T) / T
    dft = np.stack([np.cos(ang), np.sin(ang)]).astype(np.float32)
    a["dft_t"] = np.ascontiguousarray(dft.reshape(2, TT, P, T).transpose(2, 0, 1, 3))
    return a


def kernel(**inputs):
    import concourse.bacc as bacc
    from concourse.bass_utils import run_bass_kernel_spmd as run

    arrays = layout({k: np.asarray(v) for k, v in inputs.items()})
    nc = bacc.Bacc("TRN2", target_bir_lowering=False, num_devices=1)
    A = {n: nc.dram_tensor("in_" + n, a.shape, mybir.dt.from_np(a.dtype), kind="ExternalInput").ap()
                           for n, a in arrays.items()}
    out = nc.dram_tensor("out_x", (P, KD, T), F32, kind="ExternalOutput").ap()
    program(nc, A, out)
    r = run(nc, [{"in_" + n: a for n, a in arrays.items()}], core_ids=[0])
    y = r.results[0]["out_x"]
    return np.ascontiguousarray(y.transpose(2, 1, 0)).reshape(1, T, D)
```
